# Optimizing a Trainium2 kernel written in Bass

```python
import jax
import jax.numpy as jnp
from jax import lax
import numpy as np

D_MODEL = 1024
BATCH = 1
SEQ = 256
DEPTH = 4

N_MIXERS = 3
N_A = (DEPTH + 2) // 3
N_B = (DEPTH + 1) // 3
N_C = DEPTH // 3
NORM_EPS = 1e-6

A_INNER = 2 * D_MODEL
A_HEADS = 4
A_DH = A_INNER // A_HEADS
A_CONV = 4
A_CHUNK = 64
A_IN_COLS = 2 * A_INNER + 2 * A_HEADS

B_HEADS = 16
B_DH = D_MODEL // B_HEADS
B_GROUPS = 4
B_QPG = B_HEADS // B_GROUPS
B_KV = B_GROUPS * B_DH
B_CMP_LEN = 32
B_CMP_STRIDE = 16
B_PHI_HIDDEN = 256
B_SEL_LEN = 64
B_TOPN = 16
B_N_LOCAL = 2
B_WINDOW = 512
B_SEL_QBLK = 32
B_IN_COLS = B_HEADS * B_DH + 6 * B_KV + 3 * B_HEADS
FORCE_SCORE = 1e9

C_PATTERNS = ((128, 1), (512, 4), (2048, 16))
C_HEADS = 16
C_DH = D_MODEL // C_HEADS
C_GROUP_W = C_HEADS * C_DH
C_IN_COLS = 3 * len(C_PATTERNS) * C_GROUP_W

BAND_QBLK = 128

F_HIDDEN = 2816
F_CONV = 3

kernel_name = 'hybrid_mlstm_nsa_dilated_convffn'

def rmsnorm(x, g):
    xf = x.astype(jnp.float32)
    y = xf * lax.rsqrt(jnp.mean(xf * xf, axis=-1, keepdims=True) + NORM_EPS)
    return (y * g.astype(jnp.float32)).astype(x.dtype)

def causal_dwconv(x, w, b):
    k_w, ch = w.shape
    y = lax.conv_general_dilated(x, w[:, None, :].astype(x.dtype), (1,), [(k_w - 1, 0)],
                                 dimension_numbers=('NWC', 'WIO', 'NWC'), feature_group_count=ch)
    return y + b.astype(x.dtype)

def mlstm_chunkwise(q, k, v, log_i, log_f):
    bsz, nh, t_len, dh = q.shape
    L = min(A_CHUNK, t_len)
    nc = t_len // L

    def to_chunks(a):
        return jnp.moveaxis(a.reshape(bsz, nh, nc, L, *a.shape[3:]), 2, 0)

    causal = jnp.tril(jnp.ones((L, L), dtype=bool))

    def step(carry, inp):
        c_st, n_st, m_st = carry
        qc, kc, vc, lic, lfc = inp
        b = jnp.cumsum(lfc, axis=-1)
        log_d = jnp.where(causal, b[..., :, None] - b[..., None, :] + lic[..., None, :], -jnp.inf)
        log_inter = b + m_st[..., None]
        m = jnp.maximum(log_inter, jnp.max(log_d, axis=-1))
        w_intra = jnp.exp(log_d - m[..., None])
        w_inter = jnp.exp(log_inter - m)
        s = jnp.einsum('bhid,bhjd->bhij', qc, kc) * w_intra
        num = w_inter[..., None] * jnp.einsum('bhid,bhde->bhie', qc, c_st) + jnp.einsum('bhij,bhje->bhie', s, vc)
        den = w_inter * jnp.einsum('bhid,bhd->bhi', qc, n_st) + jnp.sum(s, axis=-1)
        h = num / jnp.maximum(jnp.abs(den), jnp.exp(-m))[..., None]
        b_last = b[..., -1]
        log_w = b_last[..., None] - b + lic
        m_new = jnp.maximum(b_last + m_st, jnp.max(log_w, axis=-1))
        decay = jnp.exp(b_last + m_st - m_new)
        w_k = jnp.exp(log_w - m_new[..., None])[..., None] * kc
        c_new = decay[..., None, None] * c_st + jnp.einsum('bhjd,bhje->bhde', w_k, vc)
        n_new = decay[..., None] * n_st + jnp.sum(w_k, axis=2)
        return (c_new, n_new, m_new), h

    init = (jnp.zeros((bsz, nh, dh, dh), jnp.float32), jnp.zeros((bsz, nh, dh), jnp.float32),
            jnp.zeros((bsz, nh), jnp.float32))
    _, hs = lax.scan(step, init, (to_chunks(q), to_chunks(k), to_chunks(v), to_chunks(log_i), to_chunks(log_f)))
    return jnp.moveaxis(hs, 0, 2).reshape(bsz, nh, t_len, dh)

def mlstm_mixer(h, w_in, b_gate, conv_w, conv_b, wq, wk, wv, gn, skip, w_out):
    bsz, t_len, _ = h.shape
    f32 = jnp.float32
    proj = h @ w_in
    x_m = proj[..., :A_INNER]
    o_pre = proj[..., A_INNER:2 * A_INNER]
    gates = (proj[..., 2 * A_INNER:] + b_gate).astype(f32)
    log_i = jnp.moveaxis(gates[..., :A_HEADS], -1, 1)
    log_f = jax.nn.log_sigmoid(jnp.moveaxis(gates[..., A_HEADS:], -1, 1))
    x_c = jax.nn.silu(causal_dwconv(x_m, conv_w, conv_b))
    xc_h = x_c.reshape(bsz, t_len, A_HEADS, A_DH).astype(f32)
    xm_h = x_m.reshape(bsz, t_len, A_HEADS, A_DH).astype(f32)
    q = jnp.einsum('bthd,hde->bhte', xc_h, wq.astype(f32))
    k = jnp.einsum('bthd,hde->bhte', xc_h, wk.astype(f32)) * A_DH ** -0.5
    v = jnp.einsum('bthd,hde->bhte', xm_h, wv.astype(f32))
    h_t = jnp.moveaxis(mlstm_chunkwise(q, k, v, log_i, log_f), 1, 2)
    mu = jnp.mean(h_t, axis=-1, keepdims=True)
    var = jnp.mean(jnp.square(h_t - mu), axis=-1, keepdims=True)
    h_n = ((h_t - mu) * lax.rsqrt(var + NORM_EPS)).reshape(bsz, t_len, A_INNER) * gn.astype(f32)
    y = jax.nn.sigmoid(o_pre.astype(f32)) * h_n + skip.astype(f32) * x_c.astype(f32)
    return y.astype(h.dtype) @ w_out

def banded_attention(q, k, v, max_dist):
    bsz, t_len, g, r, dh = q.shape
    qblk = min(BAND_QBLK, t_len)
    nb = t_len // qblk
    n_prev = min(-(-max_dist // qblk), nb - 1)
    span = (n_prev + 1) * qblk
    pad = ((0, 0), (n_prev * qblk, 0), (0, 0), (0, 0))
    kp = jnp.pad(k, pad)
    vp = jnp.pad(v, pad)

    def one_block(bidx):
        start = bidx * qblk
        qb = lax.dynamic_slice_in_dim(q, start, qblk, axis=1)
        kb = lax.dynamic_slice_in_dim(kp, start, span, axis=1)
        vb = lax.dynamic_slice_in_dim(vp, start, span, axis=1)
        tq = start + jnp.arange(qblk)
        sk = start - n_prev * qblk + jnp.arange(span)
        diff = tq[:, None] - sk[None, :]
        mask = (diff >= 0) & (diff <= max_dist) & (sk >= 0)[None, :]
        s = jnp.einsum('bqgrd,bkgd->bgrqk', qb, kb).astype(jnp.float32)
        s = jnp.where(mask, s, -jnp.inf)
        m = jnp.max(s, axis=-1, keepdims=True)
        e = jnp.exp(s - m)
        den = jnp.sum(e, axis=-1, keepdims=True)
        o = jnp.einsum('bgrqk,bkgd->bqgrd', (e / den).astype(v.dtype), vb)
        return o, (m + jnp.log(den))[..., 0]

    o, lse = lax.map(one_block, jnp.arange(nb))
    o = jnp.moveaxis(o, 0, 1).reshape(bsz, t_len, g, r, dh)
    lse = jnp.transpose(lse, (1, 0, 4, 2, 3)).reshape(bsz, t_len, g, r)
    return o, lse

def nsa_compress(kv, pe, w1, b1, w2):
    bsz, t_len, g, dh = kv.shape
    ncmp = (t_len - B_CMP_LEN) // B_CMP_STRIDE + 1
    idx = jnp.arange(ncmp)[:, None] * B_CMP_STRIDE + jnp.arange(B_CMP_LEN)[None, :]
    blocks = kv[:, idx] + pe[None, None, :, None, :]
    flat = jnp.moveaxis(blocks, 3, 2).reshape(bsz, ncmp, g, B_CMP_LEN * dh)
    return jax.nn.silu(flat @ w1 + b1) @ w2

def nsa_selected(q, k, v, top_idx, top_ok):
    bsz, t_len, g, r, dh = q.shape
    n_top = top_idx.shape[-1]
    qblk = min(B_SEL_QBLK, t_len)
    nqb = t_len // qblk
    kb = jnp.moveaxis(k.reshape(bsz, t_len // B_SEL_LEN, B_SEL_LEN, g, dh), 3, 1)
    vb = jnp.moveaxis(v.reshape(bsz, t_len // B_SEL_LEN, B_SEL_LEN, g, dh), 3, 1)
    bi = jnp.arange(bsz)[:, None, None, None]
    gi = jnp.arange(g)[None, :, None, None]
    off = jnp.arange(B_SEL_LEN)

    def one_block(args):
        qb, ib, okb, tq = args
        kg = kb[bi, gi, ib]
        vg = vb[bi, gi, ib]
        kpos = ib[..., None] * B_SEL_LEN + off
        mask = (kpos <= tq[None, None, :, None, None]) & okb[..., None]
        s = jnp.einsum('bqgrd,bgqnkd->bgrqnk', qb, kg).astype(jnp.float32)
        s = jnp.where(mask[:, :, None], s, -jnp.inf).reshape(bsz, g, r, qblk, n_top * B_SEL_LEN)
        p = jax.nn.softmax(s, axis=-1).reshape(bsz, g, r, qblk, n_top, B_SEL_LEN)
        return jnp.einsum('bgrqnk,bgqnkd->bqgrd', p.astype(v.dtype), vg)

    qs = jnp.moveaxis(q.reshape(bsz, nqb, qblk, g, r, dh), 1, 0)
    iss = jnp.moveaxis(top_idx.reshape(bsz, g, nqb, qblk, n_top), 2, 0)
    oks = jnp.moveaxis(top_ok.reshape(bsz, g, nqb, qblk, n_top), 2, 0)
    tqs = jnp.arange(t_len).reshape(nqb, qblk)
    o = lax.map(one_block, (qs, iss, oks, tqs))
    return jnp.moveaxis(o, 0, 1).reshape(bsz, t_len, g, r, dh)

def nsa_mixer(h, w_in, b_gate, pe_k, pe_v, phik_w1, phik_b1, phik_w2, phiv_w1, phiv_b1, phiv_w2, w_out):
    bsz, t_len, _ = h.shape
    f32 = jnp.float32
    nq = B_HEADS * B_DH
    proj = h @ w_in
    q = proj[..., :nq].reshape(bsz, t_len, B_GROUPS, B_QPG, B_DH) * B_DH ** -0.5
    kv = proj[..., nq:nq + 6 * B_KV].reshape(bsz, t_len, 6, B_GROUPS, B_DH)
    k_cmp, v_cmp, k_sel, v_sel, k_win, v_win = [kv[:, :, i] for i in range(6)]
    gate = jax.nn.sigmoid(proj[..., nq + 6 * B_KV:] + b_gate).reshape(bsz, t_len, B_GROUPS, B_QPG, 3)

    kc = nsa_compress(k_cmp, pe_k, phik_w1, phik_b1, phik_w2)
    vc = nsa_compress(v_cmp, pe_v, phiv_w1, phiv_b1, phiv_w2)
    ncmp = kc.shape[1]
    tpos = jnp.arange(t_len)
    cmp_end = jnp.arange(ncmp) * B_CMP_STRIDE + B_CMP_LEN - 1
    cmask = cmp_end[None, :] <= tpos[:, None]
    s = jnp.einsum('btgrd,bngd->bgrtn', q, kc).astype(f32)
    s = jnp.where(cmask, s, -jnp.inf)
    m = jnp.max(s, axis=-1, keepdims=True)
    m = jnp.where(jnp.isfinite(m), m, 0.0)
    e = jnp.exp(s - m)
    den = jnp.sum(e, axis=-1, keepdims=True)
    p_cmp = e / jnp.where(den > 0, den, 1.0)
    o_cmp = jnp.einsum('bgrtn,bngd->btgrd', p_cmp.astype(h.dtype), vc)

    nsel = t_len // B_SEL_LEN
    n_top = min(B_TOPN, nsel)
    c_start = jnp.arange(ncmp)[:, None] * B_CMP_STRIDE
    s_start = jnp.arange(nsel)[None, :] * B_SEL_LEN
    overlap = ((c_start < s_start + B_SEL_LEN) & (c_start + B_CMP_LEN > s_start)).astype(f32)
    imp = jnp.einsum('bgrtn,ns->bgts', p_cmp, overlap)
    blk = jnp.arange(nsel)[None, :]
    cur = (tpos // B_SEL_LEN)[:, None]
    valid = blk <= cur
    forced = ((blk == 0) | (cur - blk < B_N_LOCAL)) & valid
    score = jnp.where(forced, FORCE_SCORE, jnp.where(valid, imp, -FORCE_SCORE))
    top_val, top_idx = lax.top_k(score, n_top)
    top_ok = top_val > -0.5 * FORCE_SCORE
    o_sel = nsa_selected(q, k_sel, v_sel, top_idx, top_ok)

    o_win, _ = banded_attention(q, k_win, v_win, B_WINDOW - 1)

    o = gate[..., 0:1] * o_cmp + gate[..., 1:2] * o_sel + gate[..., 2:3] * o_win
    return o.reshape(bsz, t_len, nq) @ w_out

def dilated_mixer(h, w_in, w_out):
    bsz, t_len, _ = h.shape
    proj = (h @ w_in).reshape(bsz, t_len, len(C_PATTERNS), 3, C_HEADS, C_DH)
    outs = []
    lses = []
    for gidx, (window, dil) in enumerate(C_PATTERNS):
        sub = t_len // dil

        def by_residue(a):
            return a.reshape(bsz, sub, dil, C_HEADS, C_DH).transpose(0, 2, 1, 3, 4).reshape(bsz * dil, sub, C_HEADS, C_DH)

        q = by_residue(proj[:, :, gidx, 0]) * C_DH ** -0.5
        k = by_residue(proj[:, :, gidx, 1])
        v = by_residue(proj[:, :, gidx, 2])
        o, lse = banded_attention(q[:, :, :, None], k, v, window // dil)
        outs.append(o.reshape(bsz, dil, sub, C_HEADS, C_DH).transpose(0, 2, 1, 3, 4).reshape(bsz, t_len, C_HEADS, C_DH))
        lses.append(lse.reshape(bsz, dil, sub, C_HEADS).transpose(0, 2, 1, 3).reshape(bsz, t_len, C_HEADS))
    alpha = jax.nn.softmax(jnp.stack(lses), axis=0)
    o = jnp.sum(alpha[..., None].astype(h.dtype) * jnp.stack(outs), axis=0)
    return o.reshape(bsz, t_len, C_GROUP_W) @ w_out

def conv_ffn(h, w_up, conv_w, conv_b, w_down):
    u = causal_dwconv(h @ w_up, conv_w, conv_b)
    gate, val = u[..., :F_HIDDEN], u[..., F_HIDDEN:]
    return (jax.nn.silu(gate) * val) @ w_down

def setup_inputs(seed: int = 0):
    key = jax.random.key(seed)
    keys = iter(jax.random.split(key, 48))

    def nrm(shape, scale):
        return jax.random.normal(next(keys), shape, jnp.float32) * scale

    def gain(shape):
        return 1.0 + nrm(shape, 0.02)

    res = (2.0 * DEPTH) ** -0.5
    d = D_MODEL
    inp = {}
    inp['x'] = nrm((BATCH, SEQ, d), 1.0)
    inp['norm_mix'] = gain((DEPTH, d))
    inp['norm_ffn'] = gain((DEPTH, d))
    inp['norm_final'] = gain((d,))
    inp['a_w_in'] = nrm((N_A, d, A_IN_COLS), d ** -0.5)
    f_bias = jnp.linspace(3.0, 6.0, A_HEADS, dtype=jnp.float32)
    inp['a_b_gate'] = jnp.concatenate([nrm((N_A, A_HEADS), 0.1), f_bias[None, :] + nrm((N_A, A_HEADS), 0.01)], axis=-1)
    inp['a_conv_w'] = nrm((N_A, A_CONV, A_INNER), A_CONV ** -0.5)
    inp['a_conv_b'] = nrm((N_A, A_INNER), 0.01)
    inp['a_wq'] = nrm((N_A, A_HEADS, A_DH, A_DH), A_DH ** -0.5)
    inp['a_wk'] = nrm((N_A, A_HEADS, A_DH, A_DH), A_DH ** -0.5)
    inp['a_wv'] = nrm((N_A, A_HEADS, A_DH, A_DH), A_DH ** -0.5)
    inp['a_gn'] = gain((N_A, A_INNER))
    inp['a_skip'] = gain((N_A, A_INNER))
    inp['a_w_out'] = nrm((N_A, A_INNER, d), A_INNER ** -0.5 * res)
    inp['b_w_in'] = nrm((N_B, d, B_IN_COLS), d ** -0.5)
    inp['b_b_gate'] = nrm((N_B, 3 * B_HEADS), 0.01)
    inp['b_pe_k'] = nrm((N_B, B_CMP_LEN, B_DH), 0.1)
    inp['b_pe_v'] = nrm((N_B, B_CMP_LEN, B_DH), 0.1)
    inp['b_phik_w1'] = nrm((N_B, B_CMP_LEN * B_DH, B_PHI_HIDDEN), (B_CMP_LEN * B_DH) ** -0.5)
    inp['b_phik_b1'] = nrm((N_B, B_PHI_HIDDEN), 0.01)
    inp['b_phik_w2'] = nrm((N_B, B_PHI_HIDDEN, B_DH), B_PHI_HIDDEN ** -0.5)
    inp['b_phiv_w1'] = nrm((N_B, B_CMP_LEN * B_DH, B_PHI_HIDDEN), (B_CMP_LEN * B_DH) ** -0.5)
    inp['b_phiv_b1'] = nrm((N_B, B_PHI_HIDDEN), 0.01)
    inp['b_phiv_w2'] = nrm((N_B, B_PHI_HIDDEN, B_DH), B_PHI_HIDDEN ** -0.5)
    inp['b_w_out'] = nrm((N_B, B_HEADS * B_DH, d), (B_HEADS * B_DH) ** -0.5 * res)
    inp['c_w_in'] = nrm((N_C, d, C_IN_COLS), d ** -0.5)
    inp['c_w_out'] = nrm((N_C, C_GROUP_W, d), C_GROUP_W ** -0.5 * res)
    inp['f_w_up'] = nrm((DEPTH, d, 2 * F_HIDDEN), d ** -0.5)
    inp['f_conv_w'] = nrm((DEPTH, F_CONV, 2 * F_HIDDEN), F_CONV ** -0.5)
    inp['f_conv_b'] = nrm((DEPTH, 2 * F_HIDDEN), 0.01)
    inp['f_w_down'] = nrm((DEPTH, F_HIDDEN, d), F_HIDDEN ** -0.5 * res)
    return inp

def reference(x, norm_mix, norm_ffn, norm_final,
              a_w_in, a_b_gate, a_conv_w, a_conv_b, a_wq, a_wk, a_wv, a_gn, a_skip, a_w_out,
              b_w_in, b_b_gate, b_pe_k, b_pe_v, b_phik_w1, b_phik_b1, b_phik_w2,
              b_phiv_w1, b_phiv_b1, b_phiv_w2, b_w_out,
              c_w_in, c_w_out,
              f_w_up, f_conv_w, f_conv_b, f_w_down):
    h = x
    for i in range(DEPTH):
        kind = i % N_MIXERS
        j = i // N_MIXERS
        hn = rmsnorm(h, norm_mix[i])
        if kind == 0:
            y = mlstm_mixer(hn, a_w_in[j], a_b_gate[j], a_conv_w[j], a_conv_b[j], a_wq[j], a_wk[j], a_wv[j],
                            a_gn[j], a_skip[j], a_w_out[j])
        elif kind == 1:
            y = nsa_mixer(hn, b_w_in[j], b_b_gate[j], b_pe_k[j], b_pe_v[j], b_phik_w1[j], b_phik_b1[j], b_phik_w2[j],
                          b_phiv_w1[j], b_phiv_b1[j], b_phiv_w2[j], b_w_out[j])
        else:
            y = dilated_mixer(hn, c_w_in[j], c_w_out[j])
        h = h + y
        h = h + conv_ffn(rmsnorm(h, norm_ffn[i]), f_w_up[i], f_conv_w[i], f_conv_b[i], f_w_down[i])
    return rmsnorm(h, norm_final)


_drawn_inputs = setup_inputs


def setup_inputs(seed=0):
    import zlib

    import numpy as np

    out = dict(_drawn_inputs(seed))
    spreads = {}
    factors = {'norm_mix': 4.051,
     'norm_ffn': 4.658,
     'norm_final': 27.301,
     'a_conv_b': 8.0,
     'a_gn': 40.461,
     'a_skip': 8.0,
     'b_b_gate': 64.0,
     'b_pe_k': 8.0,
     'b_pe_v': 24.029,
     'b_phik_w1': 2.919,
     'b_phik_b1': 200.0,
     'b_phik_w2': 2.722,
     'b_phiv_b1': 200.0,
     'f_conv_b': 8.0}
    for name, (base, spread) in spreads.items():
        noise = np.random.default_rng([zlib.crc32(name.encode()), seed]).standard_normal(out[name].shape)
        drawn = base * np.exp(spread * noise) if base else spread * noise
        out[name] = jnp.asarray(drawn.astype(out[name].dtype))
    for name, factor in factors.items():
        out[name] = (out[name] * factor).astype(out[name].dtype)
    return out
```

```python
import concourse.bass as bass
from concourse import mybir
from contextlib import ExitStack

P = 128
T = 256
TT = T // P
D = 1024
KT = D // P
DEPTH = 4
EPS = 1e-6
NEG = -1e30

F_HIDDEN = 2816
FC = F_HIDDEN // 256
F_TILES = F_HIDDEN // P

A_INNER = 2 * D
A_HEADS = 4
A_DH = A_INNER // A_HEADS
A_TAPS = 4
A_TILES = A_INNER // P
A_HT = A_DH // P

B_HEADS = 16
B_GROUPS = 4
B_PER = B_HEADS // B_GROUPS
DH = D // B_HEADS
B_KV = B_GROUPS * DH
B_CMP = (T - 32) // 16 + 1
B_CPAD = B_CMP + 1
B_SCORES = 3 * 272
B_PT = 1024

C_GROUPS = 3
C_QUADS = 4
C_T0 = C_GROUPS * P
C_SCORES = C_T0 + C_GROUPS * T
C_PT = 9 * P

UNIT = 2048
RING = 3
AHEAD = 2

fp32 = mybir.dt.float32
f32r = mybir.dt.float32r
ALU = mybir.AluOpType
ACT = mybir.ActivationFunctionType
AX = mybir.AxisListType

GAINS = {
    "norm": dict(h_added=TT, ssq_ready=TT, rstd_ready=2 * TT, hs_ready=TT, turned=4, hn_hi_ready=KT, hn_lo_ready=KT),
    "a": dict(gates_split=2, gates_made=1, gate_rows=9, gate_acts=2, gates_spread=1, gate_cols=3,
              xm_acc=2 * A_HEADS, xm_lo_ready=2 * A_HEADS, xm_taps=12 * A_HEADS,
              xc_ready=2 * A_HEADS, xc_hi_ready=2 * A_HEADS, xc_lo_ready=2 * A_HEADS, skip_ready=A_HEADS,
              v_ready=A_HEADS, q_ready=A_HEADS, k_ready=A_HEADS,
              decay_diff=A_HEADS, decay_exp=A_HEADS, decay_masked=A_HEADS, scores_made=A_HEADS,
              weights_ready=A_HEADS, o_ready=2 * A_HEADS, num_made=A_HEADS, head_stats=11 * A_HEADS,
              var_pow=A_HEADS, head_normed=A_HEADS, head_turned=A_HEADS, y_steps=5 * A_HEADS,
              y_hi_ready=A_HEADS, y_lo_ready=A_HEADS),
    "b": dict(b_gates_made=1, b_gates_split=2, b_cmp_copied=2, b_flat_ready=2, b_flat_hi=2, b_flat_lo=2,
              b_hidden_ready=2, b_cmp_made=2, b_cmp_ready=2, b_keys_ready=2, b_values_ready=2,
              b_q_ready=B_GROUPS, b_gate_steps=3, b_staged=B_GROUPS,
              b_scores=B_HEADS, b_added=B_HEADS, b_max=B_HEADS, b_neg=B_HEADS, b_exp=B_HEADS, b_rec=2 * B_HEADS,
              b_normed=B_HEADS, b_turned=B_HEADS, b_pt_act=B_HEADS, b_pt_dve=B_HEADS, b_out=B_HEADS,
              b_o_hi=B_HEADS // 2, b_o_lo=B_HEADS // 2),
    "c": dict(c_v_ready=3 * C_QUADS, c_q_ready=3 * C_QUADS, c_k_ready=3 * C_QUADS,
              c_scores=4 * C_QUADS, c_max=4 * C_QUADS, c_neg=4 * C_QUADS, c_exp=4 * C_QUADS, c_rec=4 * C_QUADS,
              c_normed=4 * C_QUADS, c_turned=4 * C_QUADS, c_pt_act=4 * C_QUADS, c_pt_dve=4 * C_QUADS,
              c_out=4 * C_QUADS, c_o_hi=2 * C_QUADS, c_o_lo=2 * C_QUADS),
    "last": dict(h_added=TT, ssq_ready=TT, rstd_ready=2 * TT),
    "ffn": dict(gate_acc=FC, val_acc=FC, gate_taps=4 * FC, val_taps=4 * FC,
                silu_ready=FC, prod_ready=FC, g_hi_ready=FC, g_lo_ready=FC),
}
UNITS = {"norm": 0, "last": 0, "a": 9 * A_HEADS, "b": 18, "c": 9 * C_QUADS + 4, "ffn": 3 * FC}


class Stage:

    def __init__(self, kind, layer, unit, base):
        self.kind, self.layer, self.unit, self.base = kind, layer, unit, base

    @property
    def first(self):
        return self.unit == 0

    @property
    def gain(self):
        return (self.layer % DEPTH) * KT + (self.layer // DEPTH) * DEPTH * KT

    def __getitem__(self, name):
        return self.base.get(name, 0)


def stages_of(plan):
    unit, base, out = 0, {}, []
    for kind, layer in plan:
        out.append(Stage(kind, layer, unit, dict(base)))
        for name, n in GAINS[kind].items():
            base[name] = base.get(name, 0) + (0 if name == "h_added" and unit == 0 else n)
        unit += UNITS[kind]
    return out, unit, base


def build(nc, a, out, plan):
    STAGES, N_UNITS, TOTAL = stages_of(plan)
    ctx = ExitStack()
    with ctx:
        def sb(name, shape, dt=fp32):
            return ctx.enter_context(nc.sbuf_tensor(name, shape, dt))

        def sem(name):
            return ctx.enter_context(nc.semaphore(name))

        raw = [sb(f"raw{i}", [P, UNIT]) for i in range(RING)]
        w_hi = [sb(f"w_hi{i}", [P, UNIT], f32r) for i in range(RING)]
        w_lo = [sb(f"w_lo{i}", [P, UNIT], f32r) for i in range(RING)]
        h = sb("h", [P, TT, D])
        hs = sb("hs", [P, TT, D])
        hn_hi = sb("hn_hi", [P, KT, T], f32r)
        hn_lo = sb("hn_lo", [P, KT, T], f32r)
        ssq = sb("ssq", [P, TT])
        mean_sq = sb("mean_sq", [P, TT])
        rstd = sb("rstd", [P, TT])
        half = sb("half", [P, TT])
        ident = sb("ident", [P, P])
        key_first = sb("key_first", [P, P])
        zeros = sb("zeros", [P, 512])
        residue4 = sb("residue4", [4, P])
        residue16 = sb("residue16", [16, P])
        mask_c = sb("mask_c", [P, C_SCORES])
        mask_b = sb("mask_b", [P, 800])
        has_cmp = sb("has_cmp", [P, 1])
        zero_r = sb("zero_r", [P, 512], f32r)
        N_GROUPS = 4 + 2 * DEPTH
        cols = sb("cols", [P, N_GROUPS * P])
        final_gain = sb("final_gain", [P, D])
        gate_raw = sb("gate_raw", [P, 2, KT, 2 * A_HEADS])
        gate_bias = sb("gate_bias", [A_HEADS, 2, 2])
        acc_gate = sb("acc_gate", [P, 2, T])
        acc_val = sb("acc_val", [P, 2, T])
        prod = sb("prod", [P, 2, T])
        g_hi = sb("g_hi", [P, 2, T], f32r)
        g_lo = sb("g_lo", [P, 2, T], f32r)

        GATE, VAL = 4, 5

        a_ctx = ExitStack()

        def sa(name, shape, dt=fp32):
            return a_ctx.enter_context(nc.sbuf_tensor(name, shape, dt))

        top_all = sa("top_all", [P, A_HEADS, T])
        source_col = sa("source_col", [P, TT, A_HEADS])
        floor_col = sa("floor_col", [P, TT, A_HEADS])
        xc = sa("xc", [P, A_HT, T])
        skipped = sa("skipped", [P, A_HT, T])
        o_gate = sa("o_gate", [P, A_HT, T])
        q_t = sa("q_t", [P, A_HT, T])
        k_t = sa("k_t", [P, A_HT, T])
        v_s = sa("v_s", [P, TT, A_DH])
        weights = sa("weights", [P, TT, T])
        head_n = sa("head_n", [P, TT, A_DH])
        y_all = sa("y_all", [P, A_HT, T])
        ones = sa("ones", [P, 2])
        den = sa("den", [P, TT])
        den_abs = sa("den_abs", [P, TT])
        den_max = sa("den_max", [P, TT])
        den_rec = sa("den_rec", [P, TT])
        rec_sq = sa("rec_sq", [P, TT])
        var_in = sa("var_in", [P, TT])
        var_eps = sa("var_eps", [P, TT])
        var_rs = sa("var_rs", [P, TT])
        h_scale = sa("h_scale", [P, TT])
        stats = sa("stats", [P, TT, 6])
        mv = sa("mv", [P, TT, 2])
        xm_hi = sa("xm_hi", [P, A_HT, T], f32r)
        xm_lo = sa("xm_lo", [P, A_HT, T], f32r)
        xc_hi = sa("xc_hi", [P, A_HT, T], f32r)
        xc_lo = sa("xc_lo", [P, A_HT, T], f32r)
        y_hi = sa("y_hi", [P, A_HT, T], f32r)
        y_lo = sa("y_lo", [P, A_HT, T], f32r)
        gate_pad = y_all[:, :, :].rearrange("p n (b c) -> p (n b) c", c=P)
        gate_hi = y_hi[:, :, :].rearrange("p n (b c) -> p (n b) c", c=P)
        gate_lo = y_lo[:, :, :].rearrange("p n (b c) -> p (n b) c", c=P)
        log_i, forget, absf, expf = [skipped[0:A_HEADS, n, :] for n in range(4)]
        logf, cum_f, source, top = [o_gate[0:A_HEADS, n, :] for n in range(4)]
        stab = weights[0:A_HEADS, 0, :]
        a_ctx.close()

        b_ctx = ExitStack()

        def sbb(name, shape, dt=fp32):
            return b_ctx.enter_context(nc.sbuf_tensor(name, shape, dt))

        b_q = sbb("b_q", [P, KT, T])
        b_keys = sbb("b_keys", [P, B_GROUPS, 544])
        b_values = sbb("b_values", [P, TT, B_GROUPS, P])
        b_vcmp = sbb("b_vcmp", [16, B_GROUPS, DH])
        b_hidden = sbb("b_hidden", [P, 2, TT, B_GROUPS * B_CMP])
        b_gate_raw = sbb("b_gate_raw", [P, KT, 3 * B_HEADS])
        b_gate_hi = sbb("b_gate_hi", [P, KT, 3 * B_HEADS], f32r)
        b_gate_lo = sbb("b_gate_lo", [P, KT, 3 * B_HEADS], f32r)
        b_gate_bias = sbb("b_gate_bias", [P, 3 * B_HEADS])
        b_gate_in = sbb("b_gate_in", [P, TT, 3 * B_HEADS])
        b_gates = sbb("b_gates", [P, B_HEADS, 6])
        b_w2 = sbb("b_w2", [P, 2, 2, DH])
        b_sm = sbb("b_sm", [P, 2, B_SCORES])
        b_pt = sbb("b_pt", [P, 2, B_PT])
        b_stage = sbb("b_stage", [P, 2 * T + 528 + 2 * P])
        b_svc = sbb("b_svc", [16, DH])
        b_sgate = sbb("b_sgate", [P, 6 * B_PER])
        b_mx = sbb("b_mx", [P, 2, 6])
        b_nm = sbb("b_nm", [P, 2, 6])
        b_den = sbb("b_den", [P, 2, 6])
        b_rden = sbb("b_rden", [P, 2, 6])
        b_fac = sbb("b_fac", [P, 2, 6])
        b_o_hi = sbb("b_o_hi", [P, KT, T], f32r)
        b_o_lo = sbb("b_o_lo", [P, KT, T], f32r)
        b_ctx.close()
        b_sq = b_stage[:, 0:2 * T].rearrange("p (n t) -> p n t", n=2)
        b_sk = b_stage[:, 2 * T:2 * T + 528]
        b_sv = b_stage[:, 2 * T + 528:2 * T + 528 + 2 * P].rearrange("p (t n) -> p t n", t=TT)
        FLAT = 16 * B_GROUPS * B_CMP
        x2 = [b_sm[:, :, :].rearrange("p a b -> p (a b)")[:, 0:4 * T].rearrange("p (g t) -> p g t", g=B_GROUPS),
              b_pt[:, 0, :].rearrange("p (g t) -> p g t", g=B_GROUPS)]
        flat = [x[:, 0:FLAT].rearrange("p (m g n) -> p m g n", m=16, g=B_GROUPS) for x in (b_pt[:, 1, :], b_stage[:, :])]

        def flat_part(x, n):
            return x[:, :, :].rearrange("p k t -> p (k t)")[:, n * FLAT:(n + 1) * FLAT]

        flat_hi = [flat_part(b_o_hi, n) for n in range(2)]
        flat_lo = [flat_part(b_o_lo, n) for n in range(2)]

        c_ctx = ExitStack()

        def sbc(name, shape, dt=fp32):
            return c_ctx.enter_context(nc.sbuf_tensor(name, shape, dt))

        c_q = sbc("c_q", [P, C_GROUPS, 2, T])
        c_k = sbc("c_k", [P, C_GROUPS, 2, T])
        c_v = sbc("c_v", [P, C_GROUPS, TT, 256])
        c_sm = sbc("c_sm", [P, 2, C_SCORES])
        c_pt = sbc("c_pt", [P, 2, C_PT])
        c_mx = sbc("c_mx", [P, 2, TT])
        c_nm = sbc("c_nm", [P, 2, TT])
        c_den = sbc("c_den", [P, 2, TT])
        c_rden = sbc("c_rden", [P, 2, TT])
        c_o_hi = sbc("c_o_hi", [P, KT, T], f32r)
        c_o_lo = sbc("c_o_lo", [P, KT, T], f32r)
        c_ctx.close()

        rows_ctx = ExitStack()
        rows = rows_ctx.enter_context(nc.sbuf_tensor("rows", [P, N_GROUPS, P], fp32))
        rows_ctx.close()
        ps = ctx.enter_context(nc.psum_tensor("ps", [P, 8, 512], fp32))

        unit_loaded = [sem(f"unit_loaded{i}") for i in range(RING)]
        hi_ready = sem("hi_ready")
        lo_ready = sem("lo_ready")
        unit_used = sem("unit_used")
        x_loaded = sem("x_loaded")
        masks_zeroed = sem("masks_zeroed")
        residues_turned = sem("residues_turned")
        residues_ready = sem("residues_ready")
        masks_filled = sem("masks_filled")
        masks_ready = sem("masks_ready")
        b_params_loaded = sem("b_params_loaded")
        b_pad_ready = sem("b_pad_ready")
        gate_loaded = sem("gate_loaded")
        gates_zeroed = sem("gates_zeroed")
        gates_padded = sem("gates_padded")
        scale_ready = sem("scale_ready")
        gain_loaded = sem("gain_loaded")
        rows_cleared = sem("rows_cleared")
        rows_loaded = sem("rows_loaded")
        rows_turned = sem("rows_turned")
        cols_ready = sem("cols_ready")
        zeros_ready = sem("zeros_ready")
        N_GATE_LOADS = 6

        ROW_LOADS = [(0, 0, a["norm_mix"].rearrange("l (k p) -> (l k) p", p=P)),
                     (0, 32, a["norm_ffn"].rearrange("l (k p) -> (l k) p", p=P))]
        conv_rows = a["a_conv_w"].rearrange("j i (k p) -> (j i k) p", p=P)
        ROW_LOADS += [(1, 0, conv_rows)]
        for n, name in enumerate(("a_conv_b", "a_gn", "a_skip")):
            ROW_LOADS += [(2, 2 * A_TILES * n, a[name].rearrange("j (k p) -> (j k) p", p=P))]
        for n, name in enumerate(("b_pe_k", "b_pe_v")):
            ROW_LOADS += [(3, 16 * n, a[name][0].rearrange("(m w) d -> m (w d)", w=2))]
        for n, name in enumerate(("b_phik_b1", "b_phiv_b1")):
            ROW_LOADS += [(3, 32 + 2 * n, a[name][0].rearrange("(k p) -> k p", p=P))]
        for L in range(DEPTH):
            w = a["f_conv_w"][L].rearrange("i (k p) -> (i k) p", p=P)
            ROW_LOADS += [(4 + 2 * L, 0, w[0:88, :]), (5 + 2 * L, 0, w[88:132, :]),
                          (5 + 2 * L, 44, a["f_conv_b"][L].rearrange("(k p) -> k p", p=P))]

        ident_ready = sem("ident_ready")
        out_ready = sem("out_ready")
        out_stored = sem("out_stored")
        names = sorted({n for g in GAINS.values() for n in g})
        S = {n: sem(n) for n in names}

        def col(group, index):
            return cols[:, bass.ds(index + group * P, 1)]

        up_w = a["f_w_up"].rearrange("l (kt p) n -> l p kt n", p=P)
        down_w = a["f_w_down"].rearrange("l (c b p) n -> l c p b n", b=2, p=P)

        def slot(u):
            return u % RING

        block = ctx.enter_context(nc.Block())

        @block.sync
        def _(sp):
            def load(u, src, passed=0):
                k = slot(u)
                if u >= RING or not isinstance(passed, int):
                    sp.wait_ge(lo_ready, passed + (u - RING + 1))
                dst = raw[k][:, :].rearrange("p (b n) -> p b n", n=src.shape[-1])
                sp.dma_start(dst, src).then_inc(unit_loaded[k], 16)

            def ffn(st):
                L, u = st.layer, st.unit

                def gate(i):
                    return up_w[L][:, :, bass.ds(i * 256, 256)]

                def val(i):
                    return up_w[L][:, :, bass.ds(i * 256 + F_HIDDEN, 256)]

                def down(i):
                    return down_w[L][bass.ds(i, 1)].rearrange("o p b n -> (o p) b n")

                def body(i, passed):
                    load(u + 1, val(i), passed)
                    load(u + 2, gate(i + 1), passed)
                    load(u + 3, down(i), passed)

                load(u, gate(0))
                body(0, 0)
                with sp.Fori(1, FC - 1) as i:
                    body(i, i * 3)
                load(u + 3 * FC - 2, val(FC - 1))
                load(u + 3 * FC - 1, down(FC - 1))

            def mlstm(st):
                j, u = st.layer // 3, st.unit
                w_in = a["a_w_in"][j].rearrange("(kt p) n -> p kt n", p=P)
                w_out = a["a_w_out"][j].rearrange("(h c b p) n -> h c p b n", c=2, b=2, p=P)

                def inner(h, c, at):
                    return w_in[:, :, bass.ds(h * A_DH + (at + c * 256), 256)]

                def head_w(name, h):
                    return a[name][j][bass.ds(h, 1)].rearrange("o (kt p) n -> (o p) kt n", p=P)

                def head(h, b, passed, more):
                    load(b, head_w("a_wv", h), passed)
                    load(b + 1, head_w("a_wq", h), passed)
                    load(b + 2, head_w("a_wk", h), passed)
                    load(b + 3, inner(h, 0, A_INNER), passed)
                    load(b + 4, inner(h, 1, A_INNER), passed)
                    if more:
                        load(b + 5, inner(h + 1, 0, 0), passed)
                        load(b + 6, inner(h + 1, 1, 0), passed)
                        b += 2
                    for c in range(2):
                        load(b + 5 + c, w_out[bass.ds(h, 1)].rearrange("o c p b n -> (o c) p b n")[c], passed)

                load(u, inner(0, 0, 0))
                load(u + 1, inner(0, 1, 0))
                head(0, u + 2, 0, True)
                with sp.Fori(1, A_HEADS - 1) as h:
                    head(h, u + 2, h * 9, True)
                head(A_HEADS - 1, u + 2 + 9 * (A_HEADS - 1), 0, False)

            def nsa(st):
                u = st.unit
                w_in = a["b_w_in"][0].rearrange("(kt p) n -> p kt n", p=P)
                w_out = a["b_w_out"][0].rearrange("(c b p) n -> c p b n", b=2, p=P)

                def kv(n):
                    return w_in[:, :, D + n * B_KV:D + (n + 1) * B_KV]

                def phi(name, n):
                    return a[name][0][n * 1024:(n + 1) * 1024, :].rearrange("(kt p) n -> p kt n", p=P)

                if st["h_added"]:
                    sp.wait_ge(S["h_added"], st["h_added"] - TT)
                sp.dma_start(b_gate_raw[:, :, :], w_in[:, :, D + 6 * B_KV:]).then_inc(b_params_loaded, 16)
                sp.dma_start(b_gate_bias[:, :], a["b_b_gate"][0].rearrange("(o n) -> o n", o=1).to_broadcast([P, 3 * B_HEADS])).then_inc(b_params_loaded, 16)
                for n, name in enumerate(("b_phik_w2", "b_phiv_w2")):
                    sp.dma_start(b_w2[:, n, :, :], a[name][0].rearrange("(c p) n -> p c n", p=P)).then_inc(b_params_loaded, 16)

                order = [kv(0), kv(1), kv(2), phi("b_phik_w1", 0), phi("b_phik_w1", 1), kv(3),
                         phi("b_phiv_w1", 0), phi("b_phiv_w1", 1), kv(4), kv(5)]
                order += [w_in[:, :, 256 * g:256 * (g + 1)] for g in range(B_GROUPS)]
                order += [w_out[c] for c in range(4)]
                for n, src in enumerate(order):
                    load(u + n, src)

            def dilated(st):
                u = st.unit
                w_in = a["c_w_in"][0].rearrange("(kt p) n -> p kt n", p=P)
                w_out = a["c_w_out"][0].rearrange("(c b p) n -> c p b n", b=2, p=P)

                def quad(i, passed):
                    for g in range(C_GROUPS):
                        for n, part in enumerate((2, 0, 1)):
                            load(u + 3 * g + n, w_in[:, :, bass.ds((i + (3 * g + part) * C_QUADS) * 256, 256)], passed)

                quad(0, 0)
                with sp.Fori(1, C_QUADS) as i:
                    quad(i, i * 9)
                for c in range(4):
                    load(u + 9 * C_QUADS + c, w_out[c])

            for st in STAGES:
                if st.kind == "ffn":
                    ffn(st)
                if st.kind == "a":
                    mlstm(st)
                if st.kind == "b":
                    nsa(st)
                if st.kind == "c":
                    dilated(st)
            for t in range(TT):
                sp.wait_ge(out_ready, t + 1)
                sp.dma_start(out[0, t * P:(t + 1) * P, :], hs[:, t, :]).then_inc(out_stored, 16)
            sp.wait_ge(out_stored, 16 * TT)

        @block.gpsimd
        def _(pool):
            pool.memset(ident[:, :], 0.0).then_inc(ident_ready, 1)
            pool.wait_ge(ident_ready, 1)
            pool.affine_select(out=ident[:, :], in_=ident[:, :], compare_op=ALU.not_equal, fill=1.0, base=0,
                               pattern=[[-1, P]], channel_multiplier=1).then_inc(ident_ready, 1)
            pool.memset(half[:, :], -0.5).then_inc(ident_ready, 1)
            pool.memset(key_first[:, :], 1.0).then_inc(ident_ready, 1)
            pool.wait_ge(ident_ready, 4)
            pool.affine_select(out=key_first[:, :], in_=key_first[:, :], compare_op=ALU.is_ge, fill=0.0, base=0,
                               pattern=[[1, P]], channel_multiplier=-1).then_inc(ident_ready, 1)
            pool.memset(residue4[:, :], 0.0).then_inc(ident_ready, 1)
            pool.memset(residue16[:, :], 0.0).then_inc(ident_ready, 1)
            pool.wait_ge(ident_ready, 7)
            for tile, m in ((residue4, 4), (residue16, 16)):
                at = tile[:, :].rearrange("r (a b) -> r a b", b=m)
                pool.affine_select(out=at, in_=at, compare_op=ALU.not_equal, fill=1.0, base=0,
                                   pattern=[[0, P // m], [-1, m]], channel_multiplier=1).then_inc(residues_ready, 1)
            pool.wait_ge(masks_filled, 2)

            def keep(at, pattern, base, mult):
                pool.affine_select(out=at, in_=at, compare_op=ALU.is_ge, fill=NEG, base=base, pattern=pattern,
                                   channel_multiplier=mult).then_inc(masks_ready, 1)

            keep(mask_c[:, 0:C_T0].rearrange("p (g n) -> p g n", g=C_GROUPS), [[0, C_GROUPS], [-1, P]], 0, 1)
            t1 = mask_c[:, C_T0:C_SCORES].rearrange("p (g n) -> p g n", g=C_GROUPS)
            keep(t1[:, :, P:T], [[0, C_GROUPS], [-1, P]], 0, 1)
            keep(t1[:, 0, 0:P], [[1, P]], 0, -1)
            keep(mask_b[:, 0:T].rearrange("p (g n) -> p g n", g=2), [[0, 2], [-1, P]], 0, 1)
            keep(mask_b[:, T:T + 16], [[-16, 16]], -31, 1)
            keep(mask_b[:, 528:544], [[-16, 16]], P - 31, 1)
            keep(mask_b[:, 544:800].rearrange("p (g n) -> p g n", g=2), [[0, 2], [-1, P]], 0, 1)
            pool.affine_select(out=has_cmp[:, :], in_=has_cmp[:, :], compare_op=ALU.is_ge, fill=0.0, base=-31,
                               pattern=[[0, 1]], channel_multiplier=1).then_inc(masks_ready, 1)

            def norm(st):
                for t in range(TT):
                    pool.wait_ge(S["ssq_ready"], st["ssq_ready"] + t + 1)
                    pool.tensor_scalar(mean_sq[:, t:t + 1], ssq[:, t:t + 1], 1.0 / D, EPS,
                                       ALU.mult, ALU.add).then_inc(S["rstd_ready"], 1)
                    pool.wait_ge(S["rstd_ready"], st["rstd_ready"] + 2 * t + 1)
                    pool.tensor_tensor(rstd[:, t:t + 1], mean_sq[:, t:t + 1], half[:, t:t + 1],
                                       ALU.pow).then_inc(S["rstd_ready"], 1)

            def mlstm(st):
                with pool.Fori(0, A_HEADS) as h:
                    pool.wait_ge(S["decay_exp"], h + (st["decay_exp"] + 1))
                    for t in range(TT):
                        at = weights[:, t, t * P:(t + 1) * P]
                        ins = pool.tensor_tensor(at, at, key_first[:, :], ALU.mult)
                    ins.then_inc(S["decay_masked"], 1)
                    pool.wait_ge(S["head_stats"], h * 11 + (st["head_stats"] + 11))
                    pool.tensor_tensor(var_rs[:, :], var_eps[:, :], half[:, :], ALU.pow).then_inc(S["var_pow"], 1)

            for st in STAGES:
                if st.kind in ("norm", "last"):
                    norm(st)
                if st.kind == "a":
                    mlstm(st)

        @block.scalar
        def _(act):
            for t in range(TT):
                act.dma_start(h[:, t, :], a["x"][0, t * P:(t + 1) * P, :]).then_inc(x_loaded, 16)
            act.dma_start(final_gain[:, :], a["norm_final"].rearrange("(o n) -> o n", o=1).to_broadcast([P, D])).then_inc(gain_loaded, 16)
            act.wait_ge(rows_cleared, 1)
            for group, at, src in ROW_LOADS:
                act.dma_start(rows[at:at + src.shape[0], group, :], src).then_inc(rows_loaded, 16)

            for j in range(2):
                act.dma_start(gate_raw[:, j, :, :],
                              a["a_w_in"][j, :, 2 * A_INNER:].rearrange("(kt p) n -> p kt n", p=P)).then_inc(gate_loaded, 16)
                for g in range(2):
                    act.dma_start(gate_bias[:, j, g:g + 1],
                                  a["a_b_gate"][j, g * A_HEADS:(g + 1) * A_HEADS].rearrange("(h o) -> h o", o=1)).then_inc(gate_loaded, 16)

            def split_high(u, passed=0):
                if u >= N_UNITS:
                    return
                k = slot(u)
                act.wait_ge(unit_loaded[k], passed * 16 // RING + 16 * (u // RING + 1))
                if u >= RING or not isinstance(passed, int):
                    act.wait_ge(unit_used, passed + (u - RING + 1))
                act.activation(w_hi[k][:, :], raw[k][:, :], ACT.Copy).then_inc(hi_ready, 1)

            def square_sums(st):
                for t in range(TT):
                    if st.first:
                        act.wait_ge(x_loaded, 16 * TT)
                    else:
                        act.wait_ge(S["h_added"], st["h_added"] + t + 1)
                    act.activation(hs[:, t, :], h[:, t, :], ACT.Square,
                                   accum_out=ssq[:, t:t + 1]).then_inc(S["ssq_ready"], 1)

            def norm(st):
                square_sums(st)
                if st.first:
                    act.wait_ge(cols_ready, 3)
                for kt in range(KT):
                    act.wait_ge(S["turned"], st["turned"] + kt // 2 + 1)
                    act.activation(hn_hi[:, kt, :], ps[:, 4 + kt // 2, (kt % 2) * T:(kt % 2 + 1) * T], ACT.Copy,
                                   scale=col(0, st.gain + kt)).then_inc(S["hn_hi_ready"], 1)

            def ffn(st):
                L, u = st.layer, st.unit
                act.preload_act_table(ACT.Silu)

                def last_tap(i, which, bank, tile):
                    acc = acc_gate if which == "gate" else acc_val
                    for n in range(2):
                        ins = act.activation(acc[:, n, :], ps[:, bank, n * T:(n + 1) * T], ACT.Identity,
                                             scale=col(5 + 2 * L, i * 2 + (tile + n)),
                                             bias=col(5 + 2 * L, i * 2 + (tile + n + 2 * F_TILES)))
                    ins.then_inc(S[which + "_acc"], 1)

                def product_high(i, u, passed):
                    act.wait_ge(unit_used, passed + (u + 2))
                    last_tap(i, "val", VAL, F_TILES)
                    act.wait_ge(S["gate_taps"], i * 4 + (st["gate_taps"] + 4))
                    act.activation(acc_gate[:, :, :], acc_gate[:, :, :], ACT.Silu).then_inc(S["silu_ready"], 1)
                    act.wait_ge(S["prod_ready"], i + (st["prod_ready"] + 1))
                    act.activation(g_hi[:, :, :], prod[:, :, :], ACT.Copy).then_inc(S["g_hi_ready"], 1)
                    split_high(u + 4, passed)

                def body(i, u, passed):
                    product_high(i, u, passed)
                    split_high(u + 5, passed)
                    act.wait_ge(unit_used, passed + (u + 3))
                    last_tap(i + 1, "gate", GATE, 0)
                    split_high(u + 6, passed)

                split_high(u + 2)
                act.wait_ge(unit_used, u + 1)
                last_tap(0, "gate", GATE, 0)
                split_high(u + 3)
                with act.Fori(0, FC - 2) as i:
                    body(i, u, i * 3)
                body(FC - 2, u + 3 * (FC - 2), 0)
                product_high(FC - 1, u + 3 * (FC - 1), 0)

            def mlstm(st):
                j, u = st.layer // 3, st.unit
                act.wait_ge(gates_padded, j + 1)
                act.activation(gate_hi[:, :, :], gate_pad[:, :, :], ACT.Copy).then_inc(S["gates_split"], 1)

                def conv_start(h, c, bank):
                    for n in range(2):
                        act.activation(xc[:, 2 * c + n, :], ps[:, bank, n * T:(n + 1) * T], ACT.Identity,
                                       scale=col(1, h * A_HT + (j * A_TAPS * A_TILES + 3 * A_TILES + 2 * c + n)),
                                       bias=col(2, h * A_HT + (j * A_TILES + 2 * c + n)))
                    act.activation(xm_hi[:, 2 * c:2 * c + 2, :], ps[:, bank, :], ACT.Copy).then_inc(S["xm_acc"], 1)

                def conv_end(h, c):
                    act.wait_ge(S["xm_taps"], h * 12 + (st["xm_taps"] + 6 * c + 6))
                    at = slice(2 * c, 2 * c + 2)
                    act.activation(xc[:, at, :], xc[:, at, :], ACT.Silu).then_inc(S["xc_ready"], 1)
                    act.wait_ge(S["xc_ready"], h * 2 + (st["xc_ready"] + c + 1))
                    act.activation(xc_hi[:, at, :], xc[:, at, :], ACT.Copy).then_inc(S["xc_hi_ready"], 1)

                def head(h, b, passed, more):
                    for n in range(A_HT):
                        ins = act.activation(skipped[:, n, :], xc[:, n, :], ACT.Copy,
                                             scale=col(2, h * A_HT + (4 * A_TILES + j * A_TILES + n)))
                    ins.then_inc(S["skip_ready"], 1)
                    act.wait_ge(S["decay_diff"], h + (st["decay_diff"] + 1))
                    act.activation(weights[:, 0, :], weights[:, 0, :], ACT.Exp, scale=-1.0)
                    act.activation(weights[:, 1, P:T], weights[:, 1, P:T], ACT.Exp, scale=-1.0).then_inc(S["decay_exp"], 1)
                    split_high(b + 2, passed)
                    act.wait_ge(unit_used, passed + (b + 1))
                    act.activation(v_s[:, :, :], ps[:, 4:6, :], ACT.Copy).then_inc(S["v_ready"], 1)
                    split_high(b + 3, passed)
                    act.wait_ge(unit_used, passed + (b + 2))
                    act.activation(q_t[:, :, :], ps[:, 6:8, :], ACT.Copy, scale=float(A_DH) ** -0.5).then_inc(S["q_ready"], 1)
                    split_high(b + 4, passed)
                    split_high(b + 5, passed)
                    act.wait_ge(unit_used, passed + (b + 4))
                    act.activation(o_gate[:, 0:2, :], ps[:, 5, :], ACT.Sigmoid).then_inc(S["o_ready"], 1)
                    split_high(b + 6, passed)
                    act.wait_ge(unit_used, passed + (b + 5))
                    act.activation(o_gate[:, 2:4, :], ps[:, 4, :], ACT.Sigmoid).then_inc(S["o_ready"], 1)
                    if more:
                        split_high(b + 7, passed)
                        act.wait_ge(S["skip_ready"], h + (st["skip_ready"] + 1))
                        act.wait_ge(unit_used, passed + (b + 6))
                        conv_start(h + 1, 0, 4)
                    act.wait_ge(S["y_steps"], h * 5 + (st["y_steps"] + 5))
                    act.activation(y_hi[:, :, :], y_all[:, :, :], ACT.Copy).then_inc(S["y_hi_ready"], 1)
                    if more:
                        split_high(b + 8, passed)
                        act.wait_ge(unit_used, passed + (b + 7))
                        conv_start(h + 1, 1, 5)
                        conv_end(h + 1, 0)
                        split_high(b + 9, passed)
                        conv_end(h + 1, 1)
                        split_high(b + 10, passed)
                    else:
                        split_high(b + 7, passed)
                        split_high(b + 8, passed)

                act.wait_ge(S["gate_rows"], st["gate_rows"] + 4)
                act.activation(expf[:, :], absf[:, :], ACT.Exp, scale=-1.0).then_inc(S["gate_acts"], 1)
                act.wait_ge(S["gate_acts"], st["gate_acts"] + 1)
                act.activation(logf[:, :], expf[:, :], ACT.Ln, bias=1.0).then_inc(S["gate_acts"], 1)
                split_high(u + 2)
                act.wait_ge(unit_used, u + 1)
                conv_start(0, 0, 4)
                split_high(u + 3)
                act.wait_ge(unit_used, u + 2)
                conv_start(0, 1, 5)
                conv_end(0, 0)
                conv_end(0, 1)
                act.wait_ge(S["gates_spread"], st["gates_spread"] + 1)
                act.activation(floor_col[:, :, :], ps[:, 0, 8:16], ACT.Exp, scale=-1.0).then_inc(S["gate_cols"], 1)
                act.activation(top_all[:, :, :], ps[:, 6:8, :], ACT.Copy).then_inc(S["gate_cols"], 1)
                act.wait_ge(S["gate_cols"], st["gate_cols"] + 3)
                with act.Fori(0, A_HEADS - 1) as h:
                    head(h, u + 2, h * 9, True)
                head(A_HEADS - 1, u + 2 + 9 * (A_HEADS - 1), 0, False)

            def nsa(st):
                u = st.unit
                act.wait_ge(b_params_loaded, 64)
                act.activation(b_gate_hi[:, :, :], b_gate_raw[:, :, :], ACT.Copy).then_inc(S["b_gates_split"], 1)
                split_high(u + 2)
                act.wait_ge(unit_used, u + 1)
                for s in range(2):
                    for d in range(2):
                        ins = act.activation(x2[0][DH * d:DH * (d + 1), s::2, 0:T - d],
                                             ps[DH * s:DH * (s + 1), 0, :].rearrange("p (n t) -> p n t", n=2)[:, :, d:T], ACT.Copy)
                ins.then_inc(S["b_cmp_copied"], 1)
                act.wait_ge(S["b_gate_steps"], 1)
                for t in range(TT):
                    gate_in = b_gate_in[:, t, :].rearrange("p (h c) -> p h c", c=3)
                    act.activation(b_gates[:, :, 4 + t:5 + t], gate_in[:, :, 0:1], ACT.Sigmoid)
                    ins = act.activation(b_gates[:, :, 2 * t:2 * t + 2], gate_in[:, :, 1:3], ACT.Sigmoid)
                ins.then_inc(S["b_gate_steps"], 1)
                split_high(u + 3)

                def flat_high(n):
                    act.wait_ge(S["b_flat_ready"], n + 1)
                    act.activation(flat_hi[n], flat[n].rearrange("p m g n -> p (m g n)"), ACT.Copy).then_inc(S["b_flat_hi"], 1)

                def keys(s, unit):
                    act.wait_ge(unit_used, unit + 1)
                    for d in range(2):
                        src = ps[DH * d:DH * (d + 1), 2, :].rearrange("p (n t x) -> p n t x", n=2, t=TT)
                        for e in range(2):
                            dst = b_keys[DH * e:DH * (e + 1), d::2, :].rearrange("p n (t x) -> p n t x", t=TT)
                            ins = act.activation(dst[:, :, :, s * P:(s + 1) * P], src, ACT.Copy)
                    ins.then_inc(S["b_keys_ready"], 1)

                def hidden(n, unit, banks):
                    act.wait_ge(unit_used, unit + 1)
                    for c in range(2):
                        ins = act.activation(b_hidden[:, n, c, :], ps[:, banks[c], 0:B_GROUPS * B_CMP], ACT.Silu,
                                             bias=col(3, 32 + 2 * n + c))
                    ins.then_inc(S["b_hidden_ready"], 1)

                flat_high(0)
                split_high(u + 4)
                keys(0, u + 2)
                flat_high(1)
                split_high(u + 5)
                split_high(u + 6)
                hidden(0, u + 4, (4, 5))
                split_high(u + 7)
                split_high(u + 8)
                split_high(u + 9)
                hidden(1, u + 7, (0, 1))
                split_high(u + 10)
                keys(1, u + 8)
                split_high(u + 11)
                split_high(u + 12)
                for g in range(B_GROUPS):
                    act.wait_ge(unit_used, u + 11 + g)
                    act.activation(b_q[:, 2 * g:2 * g + 2, :], ps[:, (4, 5, 0, 1)[g], :], ACT.Copy,
                                   scale=float(DH) ** -0.5).then_inc(S["b_q_ready"], 1)
                    if g < 3:
                        split_high(u + 13 + g)
                act.wait_ge(S["b_q_ready"], B_GROUPS)
                act.wait_ge(S["b_gate_steps"], 3)
                act.wait_ge(S["b_cmp_ready"], 2)
                act.wait_ge(S["b_values_ready"], 2)
                act.preload_act_table(ACT.Exp)

                def exps(g, m):
                    act.wait_ge(S["b_neg"], g * B_PER + (m + 1))
                    sm = b_sm[:, m % 2, :]
                    late = sm[:, 272:816].rearrange("p (c x) -> p c x", x=272)
                    for n, at in enumerate((sm[:, 0:P], sm[:, P:2 * P], late[:, :, 0:P], late[:, :, P:2 * P],
                                            sm[:, 256:272], sm[:, 528:544])):
                        ins = act.activation(at, at, ACT.Exp, bias=b_nm[:, m % 2, n:n + 1], accum_out=b_den[:, m % 2, n:n + 1])
                    ins.then_inc(S["b_exp"], 1)

                def turned(g, m):
                    act.wait_ge(S["b_turned"], g * B_PER + (m + 1))
                    act.activation(b_pt[:, m % 2, 0:512], ps[:, 3, :], ACT.Copy).then_inc(S["b_pt_act"], 1)

                with act.Fori(0, B_GROUPS) as g:
                    act.wait_ge(S["b_out"], g * B_PER)
                    act.activation(b_sq, b_q[:, bass.ds(g * 2, 2), :], ACT.Copy)
                    act.activation(b_sk, b_keys[:, bass.ds(g, 1), 0:528].rearrange("p o n -> p (o n)"), ACT.Copy)
                    act.activation(b_sv, b_values[:, :, bass.ds(g, 1), :].rearrange("p t o n -> p t (o n)"), ACT.Copy)
                    act.activation(b_svc[0:B_CMP, :], b_vcmp[0:B_CMP, bass.ds(g, 1), :].rearrange("p o n -> p (o n)"), ACT.Copy)
                    act.activation(b_sgate[:, :], b_gates[:, bass.ds(g * B_PER, B_PER), :].rearrange("p h n -> p (h n)"),
                                   ACT.Copy).then_inc(S["b_staged"], 1)
                    exps(g, 0)
                    for m in range(B_PER):
                        turned(g, m)
                        if m < B_PER - 1:
                            exps(g, m + 1)
                        if m % 2:
                            act.wait_ge(S["b_out"], g * B_PER + (m + 1))
                            act.activation(b_o_hi[:, bass.ds(g * 2 + m // 2, 1), :].rearrange("p o t -> p (o t)"),
                                           ps[:, 6 + m // 2, 0:T], ACT.Copy).then_inc(S["b_o_hi"], 1)
                for c in range(4):
                    split_high(u + 16 + c)

            def dilated(st):
                u = st.unit
                act.preload_act_table(ACT.Exp)

                def evacuate(i, x, passed):
                    g, part = x // 3, x % 3
                    if part < 2:
                        act.wait_ge(unit_used, passed + (u + x + 1))
                    if part == 0:
                        act.activation(c_v[:, g, :, :], ps[:, 2, :], ACT.Copy).then_inc(S["c_v_ready"], 1)
                    if part == 1:
                        act.activation(c_q[:, g, :, :], ps[:, 0, :], ACT.Copy, scale=float(DH) ** -0.5).then_inc(S["c_q_ready"], 1)

                def exps(i, m):
                    act.wait_ge(S["c_neg"], i * 4 + (m + 1))
                    for t, at in enumerate((c_sm[:, m % 2, 0:C_T0], c_sm[:, m % 2, C_T0:C_SCORES])):
                        ins = act.activation(at, at, ACT.Exp, bias=c_nm[:, m % 2, t:t + 1], accum_out=c_den[:, m % 2, t:t + 1])
                    ins.then_inc(S["c_exp"], 1)

                def turned(i, m):
                    act.wait_ge(S["c_turned"], i * 4 + (m + 1))
                    act.activation(c_pt[:, m % 2, 0:512], ps[:, 3, :], ACT.Copy)
                    act.activation(c_pt[:, m % 2, 1024:C_PT], ps[:, 5, 0:P], ACT.Copy).then_inc(S["c_pt_act"], 1)

                with act.Fori(0, C_QUADS) as i:
                    for x in range(9):
                        if x:
                            evacuate(i, x - 1, i * 9)
                        split_high(u + x + 2, i * 9)
                    exps(i, 0)
                    for m in range(4):
                        turned(i, m)
                        if m < 3:
                            exps(i, m + 1)
                        if m % 2:
                            act.wait_ge(S["c_out"], i * 4 + (m + 1))
                            act.activation(c_o_hi[:, bass.ds(i * 2 + m // 2, 1), :].rearrange("p o t -> p (o t)"),
                                           ps[:, 6 + m // 2, 0:T], ACT.Copy).then_inc(S["c_o_hi"], 1)
                for c in range(4):
                    split_high(u + 9 * C_QUADS + 2 + c)

            for u in range(AHEAD):
                split_high(u)
            for st in STAGES:
                if st.kind == "norm":
                    norm(st)
                if st.kind == "b":
                    nsa(st)
                if st.kind == "c":
                    dilated(st)
                if st.kind == "a":
                    mlstm(st)
                if st.kind == "ffn":
                    ffn(st)
                if st.kind == "last":
                    square_sums(st)

        @block.vector
        def _(dve):
            dve.memset(rows[:, :, :], 0.0).then_inc(rows_cleared, 1)
            dve.memset(mask_c[:, :], 0.0)
            dve.memset(mask_b[:, :], 0.0)
            dve.memset(has_cmp[:, :], 1.0).then_inc(masks_zeroed, 1)
            dve.memset(zeros[:, :], 0.0).then_inc(zeros_ready, 1)
            dve.wait_ge(zeros_ready, 1)
            dve.tensor_copy(zero_r[:, :], zeros[:, :]).then_inc(zeros_ready, 1)
            for b in range(3):
                dve.wait_ge(rows_turned, b + 1)
                dve.tensor_copy(cols[:, b * 512:(b + 1) * 512], ps[:, b, :]).then_inc(cols_ready, 1)

            dve.wait_ge(residues_turned, 1)
            dve.wait_ge(masks_zeroed, 1)
            for n in range(2):
                dve.tensor_scalar(mask_c[:, (n + 1) * P:(n + 2) * P], ps[:, 3, n * P:(n + 1) * P], -1.0, -NEG, ALU.add, ALU.mult)
                for half_at in range(2):
                    at = C_T0 + (n + 1) * T + half_at * P
                    ins = dve.tensor_scalar(mask_c[:, at:at + P], ps[:, 3, n * P:(n + 1) * P], -1.0, -NEG, ALU.add, ALU.mult)
                ins.then_inc(masks_filled, 1)

            def split_low(u, passed=0):
                if u >= N_UNITS:
                    return
                k = slot(u)
                dve.wait_ge(hi_ready, passed + (u + 1))
                dve.tensor_tensor(w_lo[k][:, :], raw[k][:, :], w_hi[k][:, :].bitcast(fp32),
                                  ALU.subtract).then_inc(lo_ready, 1)

            def add_residual(st):
                dve.wait_ge(unit_used, st.unit)
                for t in range(TT):
                    dve.tensor_tensor(h[:, t, :], ps[:, 2 * t:2 * t + 2, :].rearrange("p b n -> p (b n)"),
                                      h[:, t, :], ALU.add).then_inc(S["h_added"], 1)

            def norm(st):
                if not st.first:
                    add_residual(st)
                for t in range(TT):
                    dve.wait_ge(S["rstd_ready"], st["rstd_ready"] + 2 * t + 2)
                    dve.tensor_scalar(hs[:, t, :], h[:, t, :], rstd[:, t:t + 1], None,
                                      ALU.mult).then_inc(S["hs_ready"], 1)
                for kt in range(KT):
                    dve.wait_ge(S["hn_hi_ready"], st["hn_hi_ready"] + 2 * (kt // 2) + 2)
                    dve.scalar_tensor_tensor(out=hn_lo[:, kt, :], in0=ps[:, 4 + kt // 2, (kt % 2) * T:(kt % 2 + 1) * T],
                                             scalar=col(0, st.gain + kt), in1=hn_hi[:, kt, :].bitcast(fp32),
                                             op0=ALU.mult, op1=ALU.subtract).then_inc(S["hn_lo_ready"], 1)

            def last(st):
                add_residual(st)
                dve.wait_ge(gain_loaded, 16)
                for t in range(TT):
                    dve.wait_ge(S["rstd_ready"], st["rstd_ready"] + 2 * t + 2)
                    dve.scalar_tensor_tensor(out=hs[:, t, :], in0=h[:, t, :], scalar=rstd[:, t:t + 1],
                                             in1=final_gain[:, :], op0=ALU.mult, op1=ALU.mult).then_inc(out_ready, 1)

            def ffn(st):
                L, u = st.layer, st.unit

                def earlier_taps(i, which, bank, tile):
                    dve.wait_ge(S[which + "_acc"], i + (st[which + "_acc"] + 1))
                    acc = acc_gate if which == "gate" else acc_val
                    for tap, back in ((1, 1), (0, 2)):
                        for n in range(2):
                            at = (4 if tap < 2 else 5) + 2 * L
                            dve.scalar_tensor_tensor(
                                out=acc[:, n, back:T], in0=ps[:, bank, n * T:(n + 1) * T - back],
                                scalar=col(at, i * 2 + (tap * 2 * F_TILES + tile + n)), in1=acc[:, n, back:T],
                                op0=ALU.mult, op1=ALU.add).then_inc(S[which + "_taps"], 1)
                        if tap == 1:
                            dve.wait_ge(S[which + "_taps"], i * 4 + (st[which + "_taps"] + 2))

                def multiply(i, u, passed):
                    earlier_taps(i, "val", VAL, F_TILES)
                    dve.wait_ge(S["silu_ready"], i + (st["silu_ready"] + 1))
                    dve.wait_ge(S["val_taps"], i * 4 + (st["val_taps"] + 4))
                    dve.tensor_tensor(prod[:, :, :], acc_gate[:, :, :], acc_val[:, :, :],
                                      ALU.mult).then_inc(S["prod_ready"], 1)
                    dve.wait_ge(S["g_hi_ready"], i + (st["g_hi_ready"] + 1))
                    dve.tensor_tensor(g_lo[:, :, :], prod[:, :, :], g_hi[:, :, :].bitcast(fp32),
                                      ALU.subtract).then_inc(S["g_lo_ready"], 1)
                    split_low(u + 4, passed)

                def body(i, u, passed):
                    multiply(i, u, passed)
                    split_low(u + 5, passed)
                    earlier_taps(i + 1, "gate", GATE, 0)
                    split_low(u + 6, passed)

                split_low(u + 2)
                earlier_taps(0, "gate", GATE, 0)
                split_low(u + 3)
                with dve.Fori(0, FC - 2) as i:
                    body(i, u, i * 3)
                body(FC - 2, u + 3 * (FC - 2), 0)
                multiply(FC - 1, u + 3 * (FC - 1), 0)

            def mlstm(st):
                j, u = st.layer // 3, st.unit
                rows_at = st["gate_rows"]
                dve.memset(ones[:, :], 1.0)
                dve.memset(gate_pad[:, :, :], 0.0).then_inc(gates_zeroed, 1)
                dve.wait_ge(gates_zeroed, j + 1)
                dve.wait_ge(gate_loaded, 16 * N_GATE_LOADS)
                for half_at in range(2):
                    ins = dve.tensor_copy(gate_pad[:, :, 32 * half_at:32 * half_at + A_HEADS],
                                          gate_raw[:, j, :, half_at * A_HEADS:(half_at + 1) * A_HEADS])
                ins.then_inc(gates_padded, 1)
                dve.wait_ge(S["gates_split"], st["gates_split"] + 1)
                dve.tensor_tensor(gate_lo[:, :, :], gate_pad[:, :, :], gate_hi[:, :, :].bitcast(fp32),
                                  ALU.subtract).then_inc(S["gates_split"], 1)

                dve.wait_ge(S["gates_made"], st["gates_made"] + 1)
                dve.tensor_scalar(log_i[:, :], ps[0:A_HEADS, 6, 0:T], gate_bias[:, j, 0:1], None, ALU.add).then_inc(S["gate_rows"], 1)
                dve.tensor_copy(cum_f[:, :], ps[32:32 + A_HEADS, 6, 0:T]).then_inc(S["gate_rows"], 1)
                dve.wait_ge(S["gate_rows"], rows_at + 2)
                dve.tensor_scalar(forget[:, :], cum_f[:, :], gate_bias[:, j, 1:2], None, ALU.add).then_inc(S["gate_rows"], 1)
                dve.wait_ge(S["gate_rows"], rows_at + 3)
                dve.scalar_tensor_tensor(out=absf[:, :], in0=forget[:, :], scalar=-1.0, in1=forget[:, :],
                                         op0=ALU.mult, op1=ALU.max).then_inc(S["gate_rows"], 1)
                dve.wait_ge(S["gate_acts"], st["gate_acts"] + 2)
                dve.scalar_tensor_tensor(out=forget[:, :], in0=forget[:, :], scalar=0.0, in1=logf[:, :],
                                         op0=ALU.min, op1=ALU.subtract).then_inc(S["gate_rows"], 1)
                dve.wait_ge(S["gate_rows"], rows_at + 5)
                dve.tensor_tensor_scan(cum_f[:, :], forget[:, :], zeros[0:A_HEADS, 0:T], 0.0, ALU.add, ALU.add).then_inc(S["gate_rows"], 1)
                dve.wait_ge(S["gate_rows"], rows_at + 6)
                dve.tensor_tensor(source[:, :], log_i[:, :], cum_f[:, :], ALU.subtract).then_inc(S["gate_rows"], 1)
                dve.wait_ge(S["gate_rows"], rows_at + 7)
                dve.tensor_tensor_scan(top[:, :], source[:, :], zeros[0:A_HEADS, 0:T], 0.0, ALU.max, ALU.max).then_inc(S["gate_rows"], 1)
                dve.wait_ge(S["gate_rows"], rows_at + 8)
                dve.tensor_tensor(stab[:, :], cum_f[:, :], top[:, :], ALU.add).then_inc(S["gate_rows"], 1)

                def conv(h, c, bank):
                    dve.wait_ge(S["xm_acc"], h * 2 + (st["xm_acc"] + c + 1))
                    dve.tensor_tensor(xm_lo[:, 2 * c:2 * c + 2, :], ps[:, bank, :].rearrange("p (n t) -> p n t", n=2),
                                      xm_hi[:, 2 * c:2 * c + 2, :].bitcast(fp32), ALU.subtract).then_inc(S["xm_lo_ready"], 1)
                    for back in range(1, A_TAPS):
                        tap = A_TAPS - 1 - back
                        if back > 1:
                            dve.wait_ge(S["xm_taps"], h * 12 + (st["xm_taps"] + 6 * c + 2 * back - 2))
                        for n in range(2):
                            acc = xc[:, 2 * c + n, back:T]
                            dve.scalar_tensor_tensor(
                                out=acc, in0=ps[:, bank, n * T:(n + 1) * T - back],
                                scalar=col(1, h * A_HT + (j * A_TAPS * A_TILES + tap * A_TILES + 2 * c + n)), in1=acc,
                                op0=ALU.mult, op1=ALU.add).then_inc(S["xm_taps"], 1)

                def conv_low(h, c):
                    dve.wait_ge(S["xc_hi_ready"], h * 2 + (st["xc_hi_ready"] + c + 1))
                    at = slice(2 * c, 2 * c + 2)
                    dve.tensor_tensor(xc_lo[:, at, :], xc[:, at, :], xc_hi[:, at, :].bitcast(fp32),
                                      ALU.subtract).then_inc(S["xc_lo_ready"], 1)

                def normalise(h):
                    at = st["head_stats"]

                    def step(ins):
                        ins.then_inc(S["head_stats"], 1)

                    def steps_done(n):
                        dve.wait_ge(S["head_stats"], h * 11 + (at + n))

                    dve.wait_ge(S["num_made"], h + (st["num_made"] + 1))
                    step(dve.tensor_copy(den[:, :], ps[:, 5, 0:TT]))
                    for t in range(TT):
                        step(dve.bn_stats(stats[:, t, :], ps[:, 6 + t, :]))
                    steps_done(3)
                    step(dve.scalar_tensor_tensor(out=den_abs[:, :], in0=den[:, :], scalar=-1.0, in1=den[:, :],
                                                  op0=ALU.mult, op1=ALU.max))
                    for t in range(TT):
                        step(dve.bn_aggr(mv[:, t, :], stats[:, t, :]))
                    steps_done(6)
                    step(dve.tensor_tensor(den_max[:, :], den_abs[:, :], floor_col[:, :, bass.ds(h, 1)].rearrange("p t o -> p (t o)"), ALU.max))
                    steps_done(7)
                    step(dve.reciprocal(den_rec[:, :], den_max[:, :]))
                    steps_done(8)
                    step(dve.tensor_tensor(rec_sq[:, :], den_rec[:, :], den_rec[:, :], ALU.mult))
                    steps_done(9)
                    step(dve.tensor_tensor(var_in[:, :], rec_sq[:, :], mv[:, :, 1], ALU.mult))
                    steps_done(10)
                    step(dve.tensor_scalar(var_eps[:, :], var_in[:, :], EPS, None, ALU.add))
                    dve.wait_ge(S["var_pow"], h + (st["var_pow"] + 1))
                    dve.tensor_tensor(h_scale[:, :], den_rec[:, :], var_rs[:, :], ALU.mult).then_inc(scale_ready, 1)
                    dve.wait_ge(scale_ready, h + (j * A_HEADS + 1))
                    for t in range(TT):
                        ins = dve.tensor_scalar(head_n[:, t, :], ps[:, 6 + t, :], mv[:, t, 0:1], h_scale[:, t:t + 1],
                                                ALU.subtract, ALU.mult)
                    ins.then_inc(S["head_normed"], 1)

                def gate_output(h):
                    dve.wait_ge(S["head_turned"], h + (st["head_turned"] + 1))
                    dve.wait_ge(S["skip_ready"], h + (st["skip_ready"] + 1))
                    dve.wait_ge(S["o_ready"], h * 2 + (st["o_ready"] + 2))
                    for n in range(A_HT):
                        dve.scalar_tensor_tensor(out=y_all[:, n, :], in0=ps[:, 6 + n // 2, (n % 2) * T:(n % 2 + 1) * T],
                                                 scalar=col(2, h * A_HT + (2 * A_TILES + j * A_TILES + n)),
                                                 in1=o_gate[:, n, :], op0=ALU.mult, op1=ALU.mult).then_inc(S["y_steps"], 1)
                    dve.wait_ge(S["y_steps"], h * 5 + (st["y_steps"] + 4))
                    dve.tensor_tensor(y_all[:, :, :], y_all[:, :, :], skipped[:, :, :], ALU.add).then_inc(S["y_steps"], 1)
                    dve.wait_ge(S["y_hi_ready"], h + (st["y_hi_ready"] + 1))
                    dve.tensor_tensor(y_lo[:, :, :], y_all[:, :, :], y_hi[:, :, :].bitcast(fp32),
                                      ALU.subtract).then_inc(S["y_lo_ready"], 1)

                def head(h, b, passed, more):
                    dve.wait_ge(S["num_made"], h + st["num_made"])
                    for t in range(TT):
                        ins = dve.tensor_scalar(weights[:, t, t * P:T], top_all[:, bass.ds(h, 1), t * P:T].rearrange("p o t -> p (o t)"),
                                                source_col[:, t, bass.ds(h, 1)], 0.0, ALU.subtract, ALU.max)
                    ins.then_inc(S["decay_diff"], 1)
                    for n in range(2, 5):
                        split_low(b + n, passed)
                    dve.wait_ge(unit_used, passed + (b + 3))
                    dve.tensor_copy(k_t[:, :, :], ps[:, 4:6, :].rearrange("p b n -> p (b n)").rearrange("p (n t) -> p n t", n=A_HT)).then_inc(S["k_ready"], 1)
                    split_low(b + 5, passed)
                    dve.wait_ge(S["scores_made"], h + (st["scores_made"] + 1))
                    dve.wait_ge(S["decay_masked"], h + (st["decay_masked"] + 1))
                    for t in range(TT):
                        at = weights[:, t, t * P:T]
                        ins = dve.tensor_tensor(at, ps[:, 6, t * T + t * P:(t + 1) * T], at, ALU.mult)
                    ins.then_inc(S["weights_ready"], 1)
                    split_low(b + 6, passed)
                    normalise(h)
                    if more:
                        split_low(b + 7, passed)
                    gate_output(h)
                    if more:
                        conv(h + 1, 0, 4)
                        split_low(b + 8, passed)
                        conv(h + 1, 1, 5)
                        conv_low(h + 1, 0)
                        split_low(b + 9, passed)
                        conv_low(h + 1, 1)
                        split_low(b + 10, passed)
                    else:
                        split_low(b + 7, passed)
                        split_low(b + 8, passed)

                split_low(u + 2)
                conv(0, 0, 4)
                split_low(u + 3)
                conv(0, 1, 5)
                conv_low(0, 0)
                conv_low(0, 1)
                dve.wait_ge(S["gate_cols"], st["gate_cols"] + 1)
                dve.tensor_copy(source_col[:, :, :], ps[:, 0, 0:8].rearrange("p (t h) -> p t h", t=TT)).then_inc(S["gate_cols"], 1)
                dve.wait_ge(S["gate_cols"], st["gate_cols"] + 3)
                with dve.Fori(0, A_HEADS - 1) as h:
                    head(h, u + 2, h * 9, True)
                head(A_HEADS - 1, u + 2 + 9 * (A_HEADS - 1), 0, False)

            def nsa(st):
                u = st.unit
                dve.memset(b_keys[:, :, 271:272], 0.0).then_inc(b_pad_ready, 1)
                dve.wait_ge(S["b_gates_split"], 1)
                dve.tensor_tensor(b_gate_lo[:, :, :], b_gate_raw[:, :, :], b_gate_hi[:, :, :].bitcast(fp32),
                                  ALU.subtract).then_inc(S["b_gates_split"], 1)
                dve.wait_ge(S["b_gates_made"], 1)
                for t in range(TT):
                    ins = dve.tensor_tensor(b_gate_in[:, t, :], ps[:, 7, 48 * t:48 * t + 48], b_gate_bias[:, :], ALU.add)
                ins.then_inc(S["b_gate_steps"], 1)
                split_low(u + 2)

                def flatten(n):
                    pe_col = cols[:, 3 * P + 16 * n:3 * P + 16 * n + 16].rearrange("p (m g k) -> p m g k", g=1, k=1)
                    for part in range(2):
                        src = x2[n][:, :, 16 * part:16 * part + 240].rearrange("p g (n m w) -> p w m g n", w=2, m=8)[:, 0]
                        ins = dve.tensor_tensor(flat[n][:, 8 * part:8 * part + 8], src,
                                                pe_col[:, 8 * part:8 * part + 8].to_broadcast([P, 8, B_GROUPS, B_CMP]), ALU.add)
                    ins.then_inc(S["b_flat_ready"], 1)

                def flat_low(n):
                    dve.wait_ge(S["b_flat_hi"], n + 1)
                    dve.tensor_tensor(flat_lo[n], flat[n].rearrange("p m g n -> p (m g n)"), flat_hi[n].bitcast(fp32),
                                      ALU.subtract).then_inc(S["b_flat_lo"], 1)

                def values(s, unit):
                    dve.wait_ge(unit_used, unit + 1)
                    for t in range(TT):
                        ins = dve.tensor_copy(b_values[:, t, :, s * DH:(s + 1) * DH],
                                              ps[:, 6, t * B_KV:(t + 1) * B_KV].rearrange("p (g n) -> p g n", g=B_GROUPS))
                    ins.then_inc(S["b_values_ready"], 1)

                dve.wait_ge(S["b_cmp_copied"], 1)
                flatten(0)
                split_low(u + 3)
                dve.wait_ge(unit_used, u + 2)
                for s in range(2):
                    for d in range(2):
                        ins = dve.tensor_copy(x2[1][DH * d:DH * (d + 1), s::2, 0:T - d],
                                              ps[DH * s:DH * (s + 1), 1, :].rearrange("p (n t) -> p n t", n=2)[:, :, d:T])
                ins.then_inc(S["b_cmp_copied"], 1)
                flat_low(0)
                dve.wait_ge(S["b_cmp_copied"], 2)
                flatten(1)
                split_low(u + 4)
                flat_low(1)
                split_low(u + 5)
                dve.wait_ge(S["b_gate_steps"], 2)
                dve.wait_ge(masks_ready, 8)
                dve.tensor_scalar(b_gates[:, :, 4:5], b_gates[:, :, 4:5], has_cmp[:, 0:1], None, ALU.mult).then_inc(S["b_gate_steps"], 1)
                split_low(u + 6)
                split_low(u + 7)
                values(0, u + 5)
                dve.wait_ge(S["b_cmp_made"], 1)
                dve.tensor_copy(b_keys[:, :, 256:256 + B_CMP], ps[:, 4, 0:B_GROUPS * B_CMP].rearrange("p (g n) -> p g n", g=B_GROUPS)).then_inc(S["b_cmp_ready"], 1)
                split_low(u + 8)
                split_low(u + 9)
                split_low(u + 10)
                dve.wait_ge(S["b_cmp_made"], 2)
                dve.tensor_copy(b_vcmp[0:B_CMP, :, :], ps[0:B_CMP, 5, 0:B_KV].rearrange("p (g n) -> p g n", g=B_GROUPS)).then_inc(S["b_cmp_ready"], 1)
                split_low(u + 11)
                values(1, u + 9)
                for n in range(12, 16):
                    split_low(u + n)

                def mask(g, m):
                    dve.wait_ge(S["b_scores"], g * B_PER + (m + 1))
                    sm = b_sm[:, m % 2, :]
                    dve.tensor_tensor(sm[:, 0:544].rearrange("p (c x) -> p c x", c=2), ps[:, 0:2, 0:272],
                                      mask_b[:, 0:544].rearrange("p (c x) -> p c x", c=2), ALU.add)
                    dve.tensor_tensor(sm[:, 544:800], ps[:, 2, 0:T], mask_b[:, 544:800], ALU.add).then_inc(S["b_added"], 1)
                    dve.wait_ge(S["b_added"], g * B_PER + (m + 1))
                    late = sm[:, 272:816].rearrange("p (c x) -> p c x", x=272)[:, :, 0:256]
                    dve.tensor_reduce(b_mx[:, m % 2, 0:2], sm[:, 0:256].rearrange("p (s n) -> p s n", s=2), AX.X, ALU.max)
                    dve.tensor_reduce(b_mx[:, m % 2, 2:4], late.rearrange("p c (s n) -> p s c n", s=2), AX.XY, ALU.max)
                    dve.tensor_reduce(b_mx[:, m % 2, 4:6], sm[:, 0:544].rearrange("p (c x) -> p c x", c=2)[:, :, 256:272],
                                      AX.X, ALU.max).then_inc(S["b_max"], 1)
                    dve.wait_ge(S["b_max"], g * B_PER + (m + 1))
                    dve.tensor_scalar(b_nm[:, m % 2, :], b_mx[:, m % 2, :], -1.0, None, ALU.mult).then_inc(S["b_neg"], 1)

                def scale(g, m):
                    dve.wait_ge(S["b_exp"], g * B_PER + (m + 1))
                    dve.reciprocal(b_rden[:, m % 2, :], b_den[:, m % 2, :]).then_inc(S["b_rec"], 1)
                    dve.wait_ge(S["b_rec"], g * 2 * B_PER + (2 * m + 1))
                    dve.tensor_tensor(b_fac[:, m % 2, :], b_rden[:, m % 2, :], b_sgate[:, 6 * m:6 * m + 6], ALU.mult).then_inc(S["b_rec"], 1)
                    dve.wait_ge(S["b_rec"], g * 2 * B_PER + (2 * m + 2))
                    sm = b_sm[:, m % 2, :]
                    late = sm[:, 272:816].rearrange("p (c x) -> p c x", x=272)
                    for n, at in enumerate((sm[:, 0:P], sm[:, P:2 * P], late[:, :, 0:P], late[:, :, P:2 * P],
                                            sm[:, 256:272], sm[:, 528:544])):
                        ins = dve.tensor_scalar(at, at, b_fac[:, m % 2, n:n + 1], None, ALU.mult)
                    ins.then_inc(S["b_normed"], 1)

                def turned(g, m):
                    dve.wait_ge(S["b_turned"], g * B_PER + (m + 1))
                    dve.tensor_copy(b_pt[:, m % 2, 512:768], ps[:, 4, 0:256])
                    dve.tensor_copy(b_pt[0:16, m % 2, 768:1024], ps[0:16, 4, 256:512]).then_inc(S["b_pt_dve"], 1)

                with dve.Fori(0, B_GROUPS) as g:
                    dve.wait_ge(S["b_staged"], g + 1)
                    mask(g, 0)
                    scale(g, 0)
                    for m in range(B_PER):
                        if m < B_PER - 1:
                            mask(g, m + 1)
                        turned(g, m)
                        if m < B_PER - 1:
                            scale(g, m + 1)
                        if m % 2:
                            dve.wait_ge(S["b_o_hi"], g * 2 + (m // 2 + 1))
                            pair = bass.ds(g * 2 + m // 2, 1)
                            dve.tensor_tensor(b_o_lo[:, pair, :].rearrange("p o t -> p (o t)"), ps[:, 6 + m // 2, 0:T],
                                              b_o_hi[:, pair, :].rearrange("p o t -> p (o t)").bitcast(fp32),
                                              ALU.subtract).then_inc(S["b_o_lo"], 1)
                for c in range(4):
                    split_low(u + 16 + c)

            def dilated(st):
                u = st.unit
                dve.wait_ge(masks_ready, 8)

                def mask(i, m):
                    dve.wait_ge(S["c_scores"], i * 4 + (m + 1))
                    dve.memset(c_den[:, m % 2, :], 0.0)
                    for t, (at, to) in enumerate(((0, C_T0), (C_T0, C_SCORES))):
                        src = ps[:, 0, 0:C_T0] if t == 0 else ps[:, 1:3, :].rearrange("p b n -> p (b n)")[:, 0:C_SCORES - C_T0]
                        ins = dve.tensor_tensor_reduce(c_sm[:, m % 2, at:to], src, mask_c[:, at:to], 1.0, -3e38, ALU.add, ALU.max,
                                                       c_mx[:, m % 2, t:t + 1])
                    ins.then_inc(S["c_max"], 1)
                    dve.wait_ge(S["c_max"], i * 4 + (m + 1))
                    dve.tensor_scalar(c_nm[:, m % 2, :], c_mx[:, m % 2, :], -1.0, None, ALU.mult).then_inc(S["c_neg"], 1)

                def scale(i, m):
                    dve.wait_ge(S["c_exp"], i * 4 + (m + 1))
                    dve.reciprocal(c_rden[:, m % 2, :], c_den[:, m % 2, :]).then_inc(S["c_rec"], 1)
                    dve.wait_ge(S["c_rec"], i * 4 + (m + 1))
                    for t, at in enumerate((c_sm[:, m % 2, 0:C_T0], c_sm[:, m % 2, C_T0:C_SCORES])):
                        ins = dve.tensor_scalar(at, at, c_rden[:, m % 2, t:t + 1], None, ALU.mult)
                    ins.then_inc(S["c_normed"], 1)

                def turned(i, m):
                    dve.wait_ge(S["c_turned"], i * 4 + (m + 1))
                    dve.tensor_copy(c_pt[:, m % 2, 512:1024], ps[:, 4, :]).then_inc(S["c_pt_dve"], 1)

                with dve.Fori(0, C_QUADS) as i:
                    for x in range(9):
                        if x and x % 3 == 0:
                            dve.wait_ge(unit_used, i * 9 + (u + x))
                            dve.tensor_copy(c_k[:, x // 3 - 1, :, :], ps[:, 1, :].rearrange("p (n t) -> p n t", n=2)).then_inc(S["c_k_ready"], 1)
                        split_low(u + x + 2, i * 9)
                    dve.wait_ge(unit_used, i * 9 + (u + 9))
                    dve.tensor_copy(c_k[:, 2, :, :], ps[:, 1, :].rearrange("p (n t) -> p n t", n=2)).then_inc(S["c_k_ready"], 1)
                    mask(i, 0)
                    scale(i, 0)
                    for m in range(4):
                        if m < 3:
                            mask(i, m + 1)
                        turned(i, m)
                        if m < 3:
                            scale(i, m + 1)
                        if m % 2:
                            dve.wait_ge(S["c_o_hi"], i * 2 + (m // 2 + 1))
                            pair = bass.ds(i * 2 + m // 2, 1)
                            dve.tensor_tensor(c_o_lo[:, pair, :].rearrange("p o t -> p (o t)"), ps[:, 6 + m // 2, 0:T],
                                              c_o_hi[:, pair, :].rearrange("p o t -> p (o t)").bitcast(fp32),
                                              ALU.subtract).then_inc(S["c_o_lo"], 1)
                for c in range(4):
                    split_low(u + 9 * C_QUADS + 2 + c)

            for u in range(AHEAD):
                split_low(u)
            for st in STAGES:
                if st.kind == "norm":
                    norm(st)
                if st.kind == "b":
                    nsa(st)
                if st.kind == "c":
                    dilated(st)
                if st.kind == "a":
                    mlstm(st)
                if st.kind == "ffn":
                    ffn(st)
                if st.kind == "last":
                    last(st)

        @block.tensor
        def _(pe):
            pe.wait_ge(ident_ready, 2)
            pe.wait_ge(rows_loaded, 16 * len(ROW_LOADS))
            for g in range(N_GROUPS):
                ins = pe.transpose(ps[:, g // 4, (g % 4) * P:(g % 4 + 1) * P], rows[:, g, :], ident[:, :])
                if g % 4 == 3:
                    ins.then_inc(rows_turned, 1)
            pe.wait_ge(residues_ready, 2)
            pe.matmul(ps[:, 3, 0:P], residue4[:, :], residue4[:, :], start=True, stop=True)
            pe.matmul(ps[:, 3, P:2 * P], residue16[:, :], residue16[:, :], start=True, stop=True).then_inc(residues_turned, 1)
            pe.wait_ge(zeros_ready, 2)

            def products(pairs, dst, start, stop):
                for n, (stationary, moving) in enumerate(pairs):
                    ins = pe.matmul(dst, stationary, moving, start=start and n == 0, stop=stop and n == len(pairs) - 1,
                                    skip_group_check=True)
                return ins

            def up(k, bank, x_hi=hn_hi, x_lo=hn_lo):
                wh = w_hi[k][:, :].rearrange("p (t n) -> p t n", t=KT)
                wl = w_lo[k][:, :].rearrange("p (t n) -> p t n", t=KT)
                for n in range(2):
                    at = slice(n * P, (n + 1) * P)
                    for kt in range(KT):
                        ins = products([(wh[:, kt, at], x_hi[:, kt, :]), (wh[:, kt, at], x_lo[:, kt, :]),
                                        (wl[:, kt, at], x_hi[:, kt, :])],
                                       ps[:, bank, n * T:(n + 1) * T], kt == 0, kt == KT - 1)
                return ins

            def by_token(k, bank):
                wh = w_hi[k][:, :].rearrange("p (t n) -> p t n", t=KT)
                wl = w_lo[k][:, :].rearrange("p (t n) -> p t n", t=KT)
                for t in range(TT):
                    tok = slice(t * P, (t + 1) * P)
                    for kt in range(KT):
                        ins = products([(hn_hi[:, kt, tok], wh[:, kt, :]), (hn_hi[:, kt, tok], wl[:, kt, :]),
                                        (hn_lo[:, kt, tok], wh[:, kt, :])], ps[:, bank, t * 256:(t + 1) * 256], kt == 0, kt == KT - 1)
                return ins

            def clear_y():
                for b in range(4):
                    pe.matmul(ps[:, b, :], zero_r[:, 0:P], zero_r[:, :], start=True, stop=False, skip_group_check=True)

            def down(k, x_hi, x_lo, stop):
                wh = w_hi[k][:, :].rearrange("p (c n) -> p c n", c=2)
                wl = w_lo[k][:, :].rearrange("p (c n) -> p c n", c=2)
                for c in range(2):
                    for t in range(TT):
                        tok = slice(t * P, (t + 1) * P)
                        for b in range(2):
                            at = slice(b * 512, (b + 1) * 512)
                            ins = products([(x_hi[:, c, tok], wh[:, c, at]), (x_hi[:, c, tok], wl[:, c, at]),
                                            (x_lo[:, c, tok], wh[:, c, at])],
                                           ps[:, 2 * t + b, :], False, stop and c == 1)
                return ins

            def norm(st):
                for t in range(TT):
                    pe.wait_ge(S["hs_ready"], st["hs_ready"] + t + 1)
                    for kt in range(KT):
                        ins = pe.transpose(ps[:, 4 + kt // 2, (kt % 2) * T + t * P:(kt % 2) * T + (t + 1) * P],
                                           hs[:, t, kt * P:(kt + 1) * P], ident[:, :])
                        if t == TT - 1 and kt % 2 == 1:
                            ins.then_inc(S["turned"], 1)

            def ffn(st):
                L, u = st.layer, st.unit

                def gate_up(i, u, passed):
                    pe.wait_ge(lo_ready, passed + (u + 1))
                    pe.wait_ge(S["gate_taps"], i * 4 + st["gate_taps"])
                    up(slot(u), GATE).then_inc(unit_used, 1)

                def val_up(i, u, passed):
                    pe.wait_ge(lo_ready, passed + (u + 1))
                    pe.wait_ge(S["val_taps"], i * 4 + st["val_taps"])
                    up(slot(u), VAL).then_inc(unit_used, 1)

                def project(i, u, passed, stop):
                    pe.wait_ge(lo_ready, passed + (u + 1))
                    pe.wait_ge(S["g_lo_ready"], i + (st["g_lo_ready"] + 1))
                    down(slot(u), g_hi, g_lo, stop).then_inc(unit_used, 1)

                pe.wait_ge(S["h_added"], st["h_added"])
                clear_y()
                pe.wait_ge(S["hn_lo_ready"], st["hn_lo_ready"])
                gate_up(0, u, 0)
                with pe.Fori(0, FC - 1) as i:
                    val_up(i, u + 1, i * 3)
                    gate_up(i + 1, u + 2, i * 3)
                    project(i, u + 3, i * 3, False)
                val_up(FC - 1, u + 3 * FC - 2, 0)
                project(FC - 1, u + 3 * FC - 1, 0, True)

            def mlstm(st):
                u = st.unit
                if st["h_added"]:
                    pe.wait_ge(S["h_added"], st["h_added"])
                pe.wait_ge(S["hn_lo_ready"], st["hn_lo_ready"])
                pe.wait_ge(S["gates_split"], st["gates_split"] + 2)
                for kt in range(KT):
                    ins = products([(gate_hi[:, kt, :], hn_hi[:, kt, :]), (gate_hi[:, kt, :], hn_lo[:, kt, :]),
                                    (gate_lo[:, kt, :], hn_hi[:, kt, :])], ps[:, 6, 0:T], kt == 0, kt == KT - 1)
                ins.then_inc(S["gates_made"], 1)

                def x_m(b, passed, bank):
                    pe.wait_ge(lo_ready, passed + (b + 1))
                    up(slot(b), bank).then_inc(unit_used, 1)

                def head_up(k, bank, x_hi, x_lo):
                    wh = w_hi[k][:, :].rearrange("p (t n) -> p t n", t=A_HT)
                    wl = w_lo[k][:, :].rearrange("p (t n) -> p t n", t=A_HT)
                    for n in range(A_HT):
                        at = slice(n * P, (n + 1) * P)
                        for kt in range(A_HT):
                            ins = products([(wh[:, kt, at], x_hi[:, kt, :]), (wh[:, kt, at], x_lo[:, kt, :]),
                                            (wl[:, kt, at], x_hi[:, kt, :])],
                                           ps[:, bank + n // 2, (n % 2) * T:(n % 2 + 1) * T], kt == 0, kt == A_HT - 1)
                    return ins

                def head(h, b, passed, more):
                    pe.wait_ge(lo_ready, passed + (b + 1))
                    pe.wait_ge(S["xm_lo_ready"], h * 2 + (st["xm_lo_ready"] + 2))
                    pe.wait_ge(S["xm_taps"], h * 12 + (st["xm_taps"] + 12))
                    wh = w_hi[slot(b)][:, :].rearrange("p (t n) -> p t n", t=A_HT)
                    wl = w_lo[slot(b)][:, :].rearrange("p (t n) -> p t n", t=A_HT)
                    for t in range(TT):
                        tok = slice(t * P, (t + 1) * P)
                        for kt in range(A_HT):
                            ins = products([(xm_hi[:, kt, tok], wh[:, kt, :]), (xm_hi[:, kt, tok], wl[:, kt, :]),
                                            (xm_lo[:, kt, tok], wh[:, kt, :])], ps[:, 4 + t, :], kt == 0, kt == A_HT - 1)
                    ins.then_inc(unit_used, 1)
                    pe.wait_ge(lo_ready, passed + (b + 2))
                    pe.wait_ge(S["xc_lo_ready"], h * 2 + (st["xc_lo_ready"] + 2))
                    pe.wait_ge(S["y_steps"], h * 5 + st["y_steps"])
                    head_up(slot(b + 1), 6, xc_hi, xc_lo).then_inc(unit_used, 1)
                    pe.wait_ge(lo_ready, passed + (b + 3))
                    pe.wait_ge(S["v_ready"], h + (st["v_ready"] + 1))
                    head_up(slot(b + 2), 4, xc_hi, xc_lo).then_inc(unit_used, 1)
                    pe.wait_ge(S["q_ready"], h + (st["q_ready"] + 1))
                    pe.wait_ge(S["k_ready"], h + (st["k_ready"] + 1))
                    for t in range(TT):
                        for e in range(A_HT):
                            ins = pe.matmul(ps[:, 6, t * T + t * P:(t + 1) * T], k_t[:, e, t * P:(t + 1) * P],
                                            q_t[:, e, t * P:T], start=(e == 0), stop=(e == A_HT - 1))
                    ins.then_inc(S["scores_made"], 1)
                    pe.wait_ge(lo_ready, passed + (b + 4))
                    up(slot(b + 3), 5).then_inc(unit_used, 1)
                    pe.wait_ge(lo_ready, passed + (b + 5))
                    up(slot(b + 4), 4).then_inc(unit_used, 1)
                    pe.wait_ge(S["weights_ready"], h + (st["weights_ready"] + 1))
                    pe.wait_ge(S["o_ready"], h * 2 + (st["o_ready"] + 1))
                    for t in range(TT):
                        for s in range(t + 1):
                            pe.matmul(ps[:, 6 + t, :], weights[:, s, t * P:(t + 1) * P], v_s[:, s, :],
                                      start=(s == 0), stop=(s == t))
                    for t in range(TT):
                        for s in range(t + 1):
                            ins = pe.matmul(ps[:, 5, t:t + 1], weights[:, s, t * P:(t + 1) * P], ones[:, 0:1],
                                            start=(s == 0), stop=(s == t))
                    ins.then_inc(S["num_made"], 1)
                    if more:
                        pe.wait_ge(S["o_ready"], h * 2 + (st["o_ready"] + 2))
                        x_m(b + 5, passed, 4)
                    pe.wait_ge(S["head_normed"], h + (st["head_normed"] + 1))
                    for e in range(A_HT):
                        for t in range(TT):
                            ins = pe.transpose(ps[:, 6 + e // 2, (e % 2) * T + t * P:(e % 2) * T + (t + 1) * P],
                                               head_n[:, t, e * P:(e + 1) * P], ident[:, :])
                    ins.then_inc(S["head_turned"], 1)
                    if more:
                        x_m(b + 6, passed, 5)
                        b += 2
                    pe.wait_ge(S["y_lo_ready"], h + (st["y_lo_ready"] + 1))
                    for c in range(2):
                        pe.wait_ge(lo_ready, passed + (b + 6 + c))
                        down(slot(b + 5 + c), y_hi[:, 2 * c:2 * c + 2, :], y_lo[:, 2 * c:2 * c + 2, :],
                             not more and c == 1).then_inc(unit_used, 1)

                x_m(u, 0, 4)
                x_m(u + 1, 0, 5)
                pe.wait_ge(S["gate_rows"], st["gate_rows"] + 9)
                for t in range(TT):
                    pe.transpose(ps[:, 0, 4 * t:4 * t + 4], source[:, t * P:(t + 1) * P], ident[0:A_HEADS, 0:A_HEADS])
                    pe.transpose(ps[:, 0, 8 + 4 * t:12 + 4 * t], stab[:, t * P:(t + 1) * P], ident[0:A_HEADS, 0:A_HEADS])
                for n in range(A_HEADS):
                    ins = pe.matmul(ps[:, 6 + n // 2, (n % 2) * T:(n % 2 + 1) * T],
                                    ident[0:A_HEADS, n:n + 1].to_broadcast([A_HEADS, P]), top[:, :], start=True, stop=True)
                ins.then_inc(S["gates_spread"], 1)
                pe.wait_ge(S["gate_cols"], st["gate_cols"] + 3)
                clear_y()
                with pe.Fori(0, A_HEADS - 1) as h:
                    head(h, u + 2, h * 9, True)
                head(A_HEADS - 1, u + 2 + 9 * (A_HEADS - 1), 0, False)

            def output_projection(u, o_hi, o_lo):
                clear_y()
                for c in range(4):
                    pe.wait_ge(lo_ready, u + c + 1)
                    down(slot(u + c), o_hi[:, 2 * c:2 * c + 2, :], o_lo[:, 2 * c:2 * c + 2, :], c == 3).then_inc(unit_used, 1)

            def nsa(st):
                u = st.unit
                if st["h_added"]:
                    pe.wait_ge(S["h_added"], st["h_added"])
                pe.wait_ge(S["hn_lo_ready"], st["hn_lo_ready"])
                pe.wait_ge(S["b_gates_split"], 2)
                for t in range(TT):
                    tok = slice(t * P, (t + 1) * P)
                    for kt in range(KT):
                        ins = products([(hn_hi[:, kt, tok], b_gate_hi[:, kt, :]), (hn_hi[:, kt, tok], b_gate_lo[:, kt, :]),
                                        (hn_lo[:, kt, tok], b_gate_hi[:, kt, :])], ps[:, 7, 48 * t:48 * t + 48], kt == 0, kt == KT - 1)
                ins.then_inc(S["b_gates_made"], 1)

                def ready(n):
                    pe.wait_ge(lo_ready, u + n + 1)

                def phi(n, which, half_at, banks):
                    ready(n)
                    wh = w_hi[slot(u + n)][:, :].rearrange("p (t n) -> p t n", t=KT)
                    wl = w_lo[slot(u + n)][:, :].rearrange("p (t n) -> p t n", t=KT)
                    NB = B_GROUPS * B_CMP
                    for c in range(2):
                        at = slice(c * P, (c + 1) * P)
                        for kt in range(KT):
                            m = KT * half_at + kt
                            fh, fl = flat_hi[which][:, m * NB:(m + 1) * NB], flat_lo[which][:, m * NB:(m + 1) * NB]
                            ins = products([(wh[:, kt, at], fh), (wh[:, kt, at], fl), (wl[:, kt, at], fh)],
                                           ps[:, banks[c], 0:NB], m == 0, m == 2 * KT - 1)
                    ins.then_inc(unit_used, 1)

                ready(0)
                up(slot(u), 0).then_inc(unit_used, 1)
                ready(1)
                up(slot(u + 1), 1).then_inc(unit_used, 1)
                ready(2)
                up(slot(u + 2), 2).then_inc(unit_used, 1)
                pe.wait_ge(S["b_flat_lo"], 1)
                phi(3, 0, 0, (4, 5))
                phi(4, 0, 1, (4, 5))
                ready(5)
                by_token(slot(u + 5), 6).then_inc(unit_used, 1)
                pe.wait_ge(b_params_loaded, 64)
                pe.wait_ge(S["b_hidden_ready"], 1)
                NB = B_GROUPS * B_CMP
                for d in range(2):
                    for c in range(2):
                        ins = pe.matmul(ps[DH * d:DH * (d + 1), 4, 0:NB], b_w2[:, 0, c, :], b_hidden[:, 0, c, :],
                                        start=(c == 0), stop=(c == 1))
                ins.then_inc(S["b_cmp_made"], 1)
                pe.wait_ge(S["b_flat_lo"], 2)
                phi(6, 1, 0, (0, 1))
                phi(7, 1, 1, (0, 1))
                pe.wait_ge(S["b_keys_ready"], 1)
                ready(8)
                up(slot(u + 8), 2).then_inc(unit_used, 1)
                pe.wait_ge(S["b_hidden_ready"], 2)
                for g in range(B_GROUPS):
                    for c in range(2):
                        ins = pe.matmul(ps[0:B_CMP, 5, g * DH:(g + 1) * DH], b_hidden[:, 1, c, g * B_CMP:(g + 1) * B_CMP],
                                        b_w2[:, 1, c, :], start=(c == 0), stop=(c == 1))
                ins.then_inc(S["b_cmp_made"], 1)
                pe.wait_ge(S["b_values_ready"], 1)
                ready(9)
                by_token(slot(u + 9), 6).then_inc(unit_used, 1)
                pe.wait_ge(S["b_cmp_ready"], 2)
                for g in range(B_GROUPS):
                    ready(10 + g)
                    up(slot(u + 10 + g), (4, 5, 0, 1)[g]).then_inc(unit_used, 1)
                pe.wait_ge(S["b_q_ready"], B_GROUPS)
                pe.wait_ge(S["b_keys_ready"], 2)
                pe.wait_ge(S["b_values_ready"], 2)
                pe.wait_ge(b_pad_ready, 1)

                def scores(g, m):
                    if m:
                        pe.wait_ge(S["b_added"], g * B_PER + m)
                    at = slice(DH * (m % 2), DH * (m % 2) + DH)
                    q = b_sq[at, m // 2, :]
                    pe.matmul(ps[:, 0, 0:272], q[:, 0:P], b_sk[at, 0:272], start=True, stop=True)
                    pe.matmul(ps[:, 1, 0:272], q[:, P:T], b_sk[at, 0:272], start=True, stop=True)
                    pe.matmul(ps[:, 2, 0:T], q[:, P:T], b_sk[at, 272:528], start=True, stop=True).then_inc(S["b_scores"], 1)

                def turn(g, m):
                    pe.wait_ge(S["b_normed"], g * B_PER + (m + 1))
                    pe.wait_ge(S["b_pt_act"], g * B_PER + m)
                    pe.wait_ge(S["b_pt_dve"], g * B_PER + m)
                    sm = b_sm[:, m % 2, :]
                    for n, at in enumerate((0, 272, P, 272 + P)):
                        pe.transpose(ps[:, 3, n * P:(n + 1) * P], sm[:, at:at + P], ident[:, :])
                    for n in range(2):
                        pe.transpose(ps[:, 4, n * P:(n + 1) * P], sm[:, 544 + n * P:544 + (n + 1) * P], ident[:, :])
                    for t in range(TT):
                        ins = pe.transpose(ps[0:16, 4, (2 + t) * P:(3 + t) * P], sm[:, 256 + 272 * t:272 + 272 * t], ident[:, :])
                    ins.then_inc(S["b_turned"], 1)

                def mix(g, m):
                    pe.wait_ge(S["b_pt_act"], g * B_PER + (m + 1))
                    pe.wait_ge(S["b_pt_dve"], g * B_PER + (m + 1))
                    half_at = slice(DH * (m % 2), DH * (m % 2) + DH)
                    dst = ps[half_at, 6 + m // 2, :]
                    pt = b_pt[:, m % 2, :]
                    for s in range(2):
                        pe.matmul(dst[:, 0:T], b_sv[:, 0, s * DH:(s + 1) * DH], pt[:, s * T:(s + 1) * T], start=(s == 0), stop=False)
                        pe.matmul(dst[:, P:T], b_sv[:, 1, s * DH:(s + 1) * DH], pt[:, 512 + s * P:512 + (s + 1) * P], start=False, stop=False)
                    pe.matmul(dst[:, 0:T], b_svc[0:B_CMP, :], pt[0:B_CMP, 768:1024], start=False, stop=True).then_inc(S["b_out"], 1)

                with pe.Fori(0, B_GROUPS) as g:
                    pe.wait_ge(S["b_staged"], g + 1)
                    pe.wait_ge(S["b_added"], g * B_PER)
                    pe.wait_ge(S["b_o_lo"], g * 2)
                    scores(g, 0)
                    for m in range(B_PER):
                        if m < B_PER - 1:
                            scores(g, m + 1)
                        turn(g, m)
                        mix(g, m)
                pe.wait_ge(S["b_o_lo"], 2 * B_GROUPS)
                output_projection(u + 14, b_o_hi, b_o_lo)

            def dilated(st):
                u = st.unit
                pe.wait_ge(S["h_added"], st["h_added"]) if st["h_added"] else None
                pe.wait_ge(S["hn_lo_ready"], st["hn_lo_ready"])

                def scores(i, m):
                    if m:
                        pe.wait_ge(S["c_max"], i * 4 + m)
                    at = slice(DH * (m % 2), DH * (m % 2) + DH)
                    for g in range(C_GROUPS):
                        q, k = c_q[at, g, m // 2, :], c_k[at, g, m // 2, :]
                        pe.matmul(ps[:, 0, g * P:(g + 1) * P], q[:, 0:P], k[:, 0:P], start=True, stop=True)
                        ins = pe.matmul(ps[:, 1 + g // 2, (g % 2) * T:(g % 2 + 1) * T], q[:, P:T], k, start=True, stop=True)
                    ins.then_inc(S["c_scores"], 1)

                def turn(i, m):
                    pe.wait_ge(S["c_normed"], i * 4 + (m + 1))
                    pe.wait_ge(S["c_pt_act"], i * 4 + m)
                    pe.wait_ge(S["c_pt_dve"], i * 4 + m)
                    blocks = [x for g in range(C_GROUPS) for x in (g * P, C_T0 + g * T)] + [C_T0 + g * T + P for g in range(C_GROUPS)]
                    for n, at in enumerate(blocks):
                        ins = pe.transpose(ps[:, 3 + n // 4, (n % 4) * P:(n % 4 + 1) * P], c_sm[:, m % 2, at:at + P], ident[:, :])
                    ins.then_inc(S["c_turned"], 1)

                def mix(i, m):
                    pe.wait_ge(S["c_pt_act"], i * 4 + (m + 1))
                    pe.wait_ge(S["c_pt_dve"], i * 4 + (m + 1))
                    dst = ps[DH * (m % 2):DH * (m % 2) + DH, 6 + m // 2, :]
                    pt = c_pt[:, m % 2, :]
                    for g in range(C_GROUPS):
                        pe.matmul(dst[:, 0:T], c_v[:, g, 0, m * DH:(m + 1) * DH], pt[:, g * T:(g + 1) * T], start=(g == 0), stop=False)
                        ins = pe.matmul(dst[:, P:T], c_v[:, g, 1, m * DH:(m + 1) * DH], pt[:, (6 + g) * P:(7 + g) * P],
                                        start=False, stop=(g == C_GROUPS - 1))
                    ins.then_inc(S["c_out"], 1)

                with pe.Fori(0, C_QUADS) as i:
                    pe.wait_ge(S["c_max"], i * 4)
                    pe.wait_ge(S["c_o_lo"], i * 2)
                    for g in range(C_GROUPS):
                        pe.wait_ge(lo_ready, i * 9 + (u + 3 * g + 1))
                        pe.wait_ge(S["c_v_ready"], i * 3 + g)
                        by_token(slot(u + 3 * g), 2).then_inc(unit_used, 1)
                        pe.wait_ge(lo_ready, i * 9 + (u + 3 * g + 2))
                        pe.wait_ge(S["c_q_ready"], i * 3 + g)
                        up(slot(u + 3 * g + 1), 0).then_inc(unit_used, 1)
                        pe.wait_ge(lo_ready, i * 9 + (u + 3 * g + 3))
                        pe.wait_ge(S["c_k_ready"], i * 3 + g)
                        up(slot(u + 3 * g + 2), 1).then_inc(unit_used, 1)
                    pe.wait_ge(S["c_v_ready"], i * 3 + 3)
                    pe.wait_ge(S["c_q_ready"], i * 3 + 3)
                    pe.wait_ge(S["c_k_ready"], i * 3 + 3)
                    scores(i, 0)
                    for m in range(4):
                        if m < 3:
                            scores(i, m + 1)
                        turn(i, m)
                        mix(i, m)
                pe.wait_ge(S["c_o_lo"], 2 * C_QUADS)
                output_projection(u + 9 * C_QUADS, c_o_hi, c_o_lo)

            for st in STAGES:
                if st.kind == "norm":
                    norm(st)
                if st.kind == "a":
                    mlstm(st)
                if st.kind == "b":
                    nsa(st)
                if st.kind == "c":
                    dilated(st)
                if st.kind == "ffn":
                    ffn(st)


_OUTS = [((1, T, D), "float32")]
PLAN = [("norm", 0), ("a", 0), ("norm", 4), ("ffn", 0), ("norm", 1), ("b", 1), ("norm", 5), ("ffn", 1),
        ("norm", 2), ("c", 2), ("norm", 6), ("ffn", 2), ("norm", 3), ("a", 3), ("norm", 7), ("ffn", 3), ("last", 0)]


def kernel(**inputs):
    import numpy as _np
    import concourse.bacc as _bacc
    from concourse import mybir as _mybir
    from concourse.bass_utils import run_bass_kernel_spmd as _run

    nc = _bacc.Bacc("TRN2", target_bir_lowering=False, num_devices=1)
    arrays, a = {}, {}
    for name in inputs:
        x = _np.ascontiguousarray(inputs[name])
        arrays[f"in_{name}_dram"] = x
        a[name] = nc.dram_tensor(f"in_{name}_dram", x.shape, _mybir.dt.from_np(x.dtype), kind="ExternalInput").ap()
    shape, dtype = _OUTS[0]
    out = nc.dram_tensor("out_0_dram", shape, _mybir.dt.from_np(_np.dtype(dtype)), kind="ExternalOutput").ap()
    build(nc, a, out, PLAN)
    r = _run(nc, [arrays], core_ids=[0])
    return r.results[0]["out_0_dram"]
```

```python
import concourse.bass as bass
from concourse import mybir
from contextlib import ExitStack

P = 128
T = 256
TT = T // P
D = 1024
KT = D // P
DEPTH = 4
EPS = 1e-6
NEG = -1e30

F_HIDDEN = 2816
FC = F_HIDDEN // 256
F_TILES = F_HIDDEN // P

A_INNER = 2 * D
A_HEADS = 4
A_DH = A_INNER // A_HEADS
A_TAPS = 4
A_TILES = A_INNER // P
A_HT = A_DH // P

B_HEADS = 16
B_GROUPS = 4
B_PER = B_HEADS // B_GROUPS
DH = D // B_HEADS
B_KV = B_GROUPS * DH
B_CMP = (T - 32) // 16 + 1
B_SCORES = 3 * 272
B_PT = 1024

C_GROUPS = 3
C_QUADS = 4
C_T0 = C_GROUPS * P
C_SCORES = C_T0 + C_GROUPS * T
C_PT = 9 * P

UNIT = 2048
RING = 3

fp32 = mybir.dt.float32
f32r = mybir.dt.float32r
ALU = mybir.AluOpType
ACT = mybir.ActivationFunctionType
AX = mybir.AxisListType

GAINS = {
    "norm": dict(h_added=2 * TT, ssq_ready=2 * TT, rstd_ready=2 * TT, hs_ready=TT, hs_act_ready=TT, turned=4,
                 hn_hi_ready=KT, hn_lo_ready=KT),
    "a": dict(y_banks=3, gates_split=2, gates_made=1, gate_rows=9, gate_acts=2, gates_spread=1, gate_cols=3,
              xm_acc=2 * A_HEADS, xm_lo_ready=2 * A_HEADS, xm_taps=12 * A_HEADS,
              xc_ready=2 * A_HEADS, xc_hi_ready=2 * A_HEADS, xc_lo_ready=2 * A_HEADS, skip_ready=A_HEADS,
              v_ready=A_HEADS, q_ready=A_HEADS, k_ready=2 * A_HEADS,
              decay_diff=A_HEADS, decay_exp=A_HEADS, decay_masked=A_HEADS, scores_made=A_HEADS,
              weights_ready=A_HEADS, o_ready=2 * A_HEADS, num_made=A_HEADS, head_stats=11 * A_HEADS,
              var_pow=A_HEADS, head_normed=A_HEADS, head_turned=A_HEADS, y_steps=6 * A_HEADS,
              y_hi_ready=2 * A_HEADS, y_lo_ready=2 * A_HEADS),
    "b": dict(y_banks=3, b_gates_made=1, b_gates_copied=1, b_gates_turned=1, b_pre_ready=2, b_pre_turned=2,
              b_gates_split=2, b_cmp_copied=2, b_flat_ready=2, b_flat_hi=2, b_flat_lo=2,
              b_hidden_ready=2, b_cmp_made=2, b_cmp_ready=2, b_keys_ready=2, b_values_ready=2,
              b_q_ready=B_GROUPS, b_gate_steps=3, b_staged=2 * B_GROUPS,
              b_scores=B_HEADS, b_max=B_HEADS, b_neg=B_HEADS, b_exp=B_HEADS, b_rec=2 * B_HEADS,
              b_normed=B_HEADS, b_turned=B_HEADS, b_pt_act=B_HEADS, b_pt_dve=B_HEADS, b_out=B_HEADS,
              b_o_hi=B_HEADS // 2, b_o_lo=B_HEADS // 2),
    "c": dict(y_banks=3, c_v_ready=3 * C_QUADS, c_q_ready=3 * C_QUADS, c_k_ready=3 * C_QUADS,
              c_scores=4 * C_QUADS, c_max=4 * C_QUADS, c_neg=4 * C_QUADS, c_exp=4 * C_QUADS, c_rec=4 * C_QUADS,
              c_normed=4 * C_QUADS, c_turned=4 * C_QUADS, c_pt_act=4 * C_QUADS, c_pt_dve=4 * C_QUADS,
              c_out=4 * C_QUADS, c_o_hi=2 * C_QUADS, c_o_lo=2 * C_QUADS),
    "last": dict(h_added=2 * TT, ssq_ready=2 * TT, rstd_ready=2 * TT),
    "ffn": dict(y_banks=3, gate_acc=FC, val_acc=FC, gate_taps=4 * FC, val_taps=4 * FC,
                silu_ready=FC, prod_ready=FC, g_hi_ready=FC, g_lo_ready=FC),
}
UNITS = {"norm": 0, "last": 0, "a": 9 * A_HEADS, "b": 18, "c": 9 * C_QUADS + 4, "ffn": 3 * FC}


class Stage:

    def __init__(self, kind, layer, unit, base):
        self.kind, self.layer, self.unit, self.base = kind, layer, unit, base

    @property
    def first(self):
        return self.unit == 0

    @property
    def gain(self):
        return (self.layer % DEPTH) * KT + (self.layer // DEPTH) * DEPTH * KT

    def __getitem__(self, name):
        return self.base.get(name, 0)


def stages_of(plan):
    unit, base, out = 0, {}, []
    for kind, layer in plan:
        out.append(Stage(kind, layer, unit, dict(base)))
        for name, n in GAINS[kind].items():
            base[name] = base.get(name, 0) + (0 if name == "h_added" and unit == 0 else n)
        unit += UNITS[kind]
    return out, unit


def build(nc, a, out, plan):
    STAGES, N_UNITS = stages_of(plan)
    ctx = ExitStack()
    with ctx:
        def sb(name, shape, dt=fp32):
            return ctx.enter_context(nc.sbuf_tensor(name, shape, dt))

        def sem(name):
            return ctx.enter_context(nc.semaphore(name))

        raw = [sb(f"raw{i}", [P, UNIT]) for i in range(RING)]
        w_hi = [sb(f"w_hi{i}", [P, UNIT], f32r) for i in range(RING)]
        w_lo = [sb(f"w_lo{i}", [P, UNIT], f32r) for i in range(RING)]
        h = sb("h", [P, TT, D])
        hs = sb("hs", [P, TT, D])
        hn_hi = sb("hn_hi", [P, KT, T], f32r)
        hn_lo = sb("hn_lo", [P, KT, T], f32r)
        ssq = sb("ssq", [P, TT, 2])
        mean_sq = sb("mean_sq", [P, TT])
        rstd = sb("rstd", [P, TT])
        half = sb("half", [P, TT])
        ident = sb("ident", [P, P])
        key_first = sb("key_first", [P, P])
        zeros = sb("zeros", [P, 512])
        residue4 = sb("residue4", [4, P])
        residue16 = sb("residue16", [16, P])
        mask_c = sb("mask_c", [P, C_SCORES])
        mask_b = sb("mask_b", [P, B_SCORES])
        has_cmp = sb("has_cmp", [P, 1])
        zero_r = sb("zero_r", [P, 512], f32r)
        N_GROUPS = 4 + 2 * DEPTH
        cols = sb("cols", [P, N_GROUPS * P])
        final_gain = sb("final_gain", [P, D])
        gate_raw = sb("gate_raw", [P, 2, KT, 2 * A_HEADS])
        gate_bias = sb("gate_bias", [A_HEADS, 2, 2])
        acc_gate = sb("acc_gate", [P, 2, T])
        acc_val = sb("acc_val", [P, 2, T])
        prod = sb("prod", [P, 2, T])
        g_hi = sb("g_hi", [P, 2, T], f32r)
        g_lo = sb("g_lo", [P, 2, T], f32r)

        GATE, VAL = 4, 5

        a_ctx = ExitStack()

        def sa(name, shape, dt=fp32):
            return a_ctx.enter_context(nc.sbuf_tensor(name, shape, dt))

        top_all = sa("top_all", [P, A_HEADS, T])
        source_col = sa("source_col", [P, TT, A_HEADS])
        floor_col = sa("floor_col", [P, TT, A_HEADS])
        xc = sa("xc", [P, A_HT, T])
        skipped = sa("skipped", [P, A_HT, T])
        o_gate = sa("o_gate", [P, A_HT, T])
        q_t = sa("q_t", [P, A_HT, T])
        k_t = sa("k_t", [P, A_HT, T])
        v_s = sa("v_s", [P, TT, A_DH])
        weights = sa("weights", [P, TT, T])
        head_n = sa("head_n", [P, TT, A_DH])
        y_all = sa("y_all", [P, A_HT, T])
        ones = sa("ones", [P, 2])
        den = sa("den", [P, TT])
        den_abs = sa("den_abs", [P, TT])
        den_max = sa("den_max", [P, TT])
        den_rec = sa("den_rec", [P, TT])
        rec_sq = sa("rec_sq", [P, TT])
        var_in = sa("var_in", [P, TT])
        var_eps = sa("var_eps", [P, TT])
        var_rs = sa("var_rs", [P, TT])
        h_scale = sa("h_scale", [P, TT])
        stats = sa("stats", [P, TT, 6])
        mv = sa("mv", [P, TT, 2])
        xm_hi = sa("xm_hi", [P, A_HT, T], f32r)
        xm_lo = sa("xm_lo", [P, A_HT, T], f32r)
        xc_hi = sa("xc_hi", [P, A_HT, T], f32r)
        xc_lo = sa("xc_lo", [P, A_HT, T], f32r)
        y_hi = sa("y_hi", [P, A_HT, T], f32r)
        y_lo = sa("y_lo", [P, A_HT, T], f32r)
        gate_pad = y_all[:, :, :].rearrange("p n (b c) -> p (n b) c", c=P)
        gate_hi = y_hi[:, :, :].rearrange("p n (b c) -> p (n b) c", c=P)
        gate_lo = y_lo[:, :, :].rearrange("p n (b c) -> p (n b) c", c=P)
        log_i, forget, absf, expf = [skipped[0:A_HEADS, n, :] for n in range(4)]
        logf, cum_f, source, top = [o_gate[0:A_HEADS, n, :] for n in range(4)]
        stab = weights[0:A_HEADS, 0, :]
        a_ctx.close()

        b_ctx = ExitStack()

        def sbb(name, shape, dt=fp32):
            return b_ctx.enter_context(nc.sbuf_tensor(name, shape, dt))

        b_q = sbb("b_q", [P, KT, T])
        b_keys = sbb("b_keys", [P, B_GROUPS, 544])
        b_values = sbb("b_values", [P, TT, B_GROUPS, P])
        b_vcmp = sbb("b_vcmp", [16, B_GROUPS, DH])
        b_hidden = sbb("b_hidden", [P, 2, TT, B_GROUPS * B_CMP])
        b_gate_raw = sbb("b_gate_raw", [P, KT, 3 * B_HEADS])
        b_gate_hi = sbb("b_gate_hi", [P, KT, 3 * B_HEADS], f32r)
        b_gate_lo = sbb("b_gate_lo", [P, KT, 3 * B_HEADS], f32r)
        b_gate_bias = sbb("b_gate_bias", [P, 3 * B_HEADS])
        b_gate_t = sbb("b_gate_t", [3 * B_HEADS, T])
        b_pre = sbb("b_pre", [B_GROUPS * B_CMP, 2, T])
        b_gate_in = sbb("b_gate_in", [P, TT, 3 * B_HEADS])
        b_gates = sbb("b_gates", [P, B_HEADS, 6])
        b_w2 = sbb("b_w2", [P, 2, 2, DH])
        b_sm = sbb("b_sm", [P, 2, B_SCORES])
        b_pt = sbb("b_pt", [P, 2, B_PT])
        b_stage = sbb("b_stage", [P, 2 * T + 528 + 2 * P])
        b_svc = sbb("b_svc", [16, DH])
        b_sgate = sbb("b_sgate", [P, 6 * B_PER])
        b_mx = sbb("b_mx", [P, 2, 6])
        b_nm = sbb("b_nm", [P, 2, 6])
        b_den = sbb("b_den", [P, 2, 6])
        b_rden = sbb("b_rden", [P, 2, 6])
        b_fac = sbb("b_fac", [P, 2, 6])
        b_o_hi = sbb("b_o_hi", [P, KT, T], f32r)
        b_o_lo = sbb("b_o_lo", [P, KT, T], f32r)
        b_ctx.close()
        b_sq = b_stage[:, 0:2 * T].rearrange("p (n t) -> p n t", n=2)
        b_sk = b_stage[:, 2 * T:2 * T + 528]
        b_sv = b_stage[:, 2 * T + 528:2 * T + 528 + 2 * P].rearrange("p (t n) -> p t n", t=TT)
        FLAT = 16 * B_GROUPS * B_CMP

        def branches(x):
            late = x[:, 272:816].rearrange("p (c x) -> p c x", x=272)
            return x[:, 0:P], x[:, P:2 * P], late[:, :, 0:P], late[:, :, P:2 * P], x[:, 256:272], x[:, 528:544]
        x2 = [b_sm[:, :, :].rearrange("p a b -> p (a b)")[:, 0:4 * T].rearrange("p (g t) -> p g t", g=B_GROUPS),
              b_pt[:, 0, :].rearrange("p (g t) -> p g t", g=B_GROUPS)]
        flat = [x[:, 0:FLAT].rearrange("p (m g n) -> p m g n", m=16, g=B_GROUPS) for x in (b_pt[:, 1, :], b_stage[:, :])]

        def flat_part(x, n):
            return x[:, :, :].rearrange("p k t -> p (k t)")[:, n * FLAT:(n + 1) * FLAT]

        flat_hi = [flat_part(b_o_hi, n) for n in range(2)]
        flat_lo = [flat_part(b_o_lo, n) for n in range(2)]

        c_ctx = ExitStack()

        def sbc(name, shape, dt=fp32):
            return c_ctx.enter_context(nc.sbuf_tensor(name, shape, dt))

        c_q = sbc("c_q", [P, C_GROUPS, 2, T])
        c_k = sbc("c_k", [P, C_GROUPS, 2, T])
        c_v = sbc("c_v", [P, C_GROUPS, TT, 256])
        c_sm = sbc("c_sm", [P, 2, C_SCORES])
        c_pt = sbc("c_pt", [P, 2, C_PT])
        c_mx = sbc("c_mx", [P, 2, TT])
        c_nm = sbc("c_nm", [P, 2, TT])
        c_den = sbc("c_den", [P, 2, TT])
        c_rden = sbc("c_rden", [P, 2, TT])
        c_o_hi = sbc("c_o_hi", [P, KT, T], f32r)
        c_o_lo = sbc("c_o_lo", [P, KT, T], f32r)
        c_ctx.close()

        rows_ctx = ExitStack()
        rows = rows_ctx.enter_context(nc.sbuf_tensor("rows", [P, N_GROUPS, P], fp32))
        rows_ctx.close()
        ps = ctx.enter_context(nc.psum_tensor("ps", [P, 8, 512], fp32))

        unit_loaded = [sem(f"unit_loaded{i}") for i in range(RING)]
        hi_ready = sem("hi_ready")
        lo_ready = sem("lo_ready")
        unit_used = sem("unit_used")
        x_loaded = [sem(f"x_loaded{t}") for t in range(TT)]
        masks_zeroed = sem("masks_zeroed")
        residues_turned = sem("residues_turned")
        residues_ready = sem("residues_ready")
        masks_filled = sem("masks_filled")
        masks_ready = sem("masks_ready")
        b_params_loaded = sem("b_params_loaded")
        b_pad_ready = sem("b_pad_ready")
        gate_loaded = sem("gate_loaded")
        gates_zeroed = sem("gates_zeroed")
        gates_padded = sem("gates_padded")
        scale_ready = sem("scale_ready")
        gain_loaded = sem("gain_loaded")
        rows_cleared = sem("rows_cleared")
        gains_loaded = sem("gains_loaded")
        gains_turned = sem("gains_turned")
        gains_ready = sem("gains_ready")
        rows_loaded = sem("rows_loaded")
        rows_turned = sem("rows_turned")
        cols_ready = sem("cols_ready")
        zeros_ready = sem("zeros_ready")
        N_GATE_LOADS = 6

        ROW_LOADS = [(0, 0, a["norm_mix"].rearrange("l (k p) -> (l k) p", p=P)),
                     (0, 32, a["norm_ffn"].rearrange("l (k p) -> (l k) p", p=P))]
        conv_rows = a["a_conv_w"].rearrange("j i (k p) -> (j i k) p", p=P)
        ROW_LOADS += [(1, 0, conv_rows)]
        for n, name in enumerate(("a_conv_b", "a_gn", "a_skip")):
            ROW_LOADS += [(2, 2 * A_TILES * n, a[name].rearrange("j (k p) -> (j k) p", p=P))]
        for n, name in enumerate(("b_pe_k", "b_pe_v")):
            ROW_LOADS += [(3, 16 * n, a[name][0].rearrange("(m w) d -> m (w d)", w=2))]
        for n, name in enumerate(("b_phik_b1", "b_phiv_b1")):
            ROW_LOADS += [(3, 32 + 2 * n, a[name][0].rearrange("(k p) -> k p", p=P))]
        conv = a["f_conv_w"].rearrange("l i (k p) -> (i k) l p", p=P)
        ROW_LOADS += [(slice(4, 4 + 2 * DEPTH, 2), 0, conv[0:88]), (slice(5, 4 + 2 * DEPTH, 2), 0, conv[88:132]),
                      (slice(5, 4 + 2 * DEPTH, 2), 44, a["f_conv_b"].rearrange("l (k p) -> k l p", p=P))]
        ident_ready = sem("ident_ready")
        out_ready = sem("out_ready")
        out_stored = sem("out_stored")
        names = sorted({n for g in GAINS.values() for n in g})
        S = {n: sem(n) for n in names}

        def col(group, index):
            return cols[:, bass.ds(index + group * P, 1)]

        up_w = a["f_w_up"].rearrange("l (kt p) n -> l p kt n", p=P)
        down_w = a["f_w_down"].rearrange("l (c b p) n -> l c p b n", b=2, p=P)

        def slot(u):
            return u % RING

        def mixer_after(st):
            n = STAGES.index(st) + 2
            return STAGES[n] if n < len(STAGES) and STAGES[n].kind in ("a", "b") else None

        block = ctx.enter_context(nc.Block())

        @block.sync
        def _(sp):
            def load(u, src, passed=0):
                k = slot(u)
                if u >= RING or not isinstance(passed, int):
                    sp.wait_ge(lo_ready, passed + (u - RING + 1))
                dst = raw[k][:, :].rearrange("p (b n) -> p b n", n=src.shape[-1])
                sp.dma_start(dst, src).then_inc(unit_loaded[k], 16)
                if u == 0 and isinstance(passed, int):
                    sp.wait_ge(rows_cleared, 1)
                    for group, at, src in ROW_LOADS[2:]:
                        sp.dma_start(rows[at:at + src.shape[0], group, :], src).then_inc(rows_loaded, 16)
                    for j in range(2):
                        for g in range(2):
                            bias = a["a_b_gate"][j, g * A_HEADS:(g + 1) * A_HEADS].rearrange("(h o) -> h o", o=1)
                            sp.dma_start(gate_bias[:, j, g:g + 1], bias).then_inc(gate_loaded, 16)

            def b_parameters(after):
                w_in = a["b_w_in"][0].rearrange("(kt p) n -> p kt n", p=P)
                if after:
                    sp.wait_ge(S["h_added"], after)
                sp.dma_start(b_gate_raw[:, :, :], w_in[:, :, D + 6 * B_KV:]).then_inc(b_params_loaded, 16)
                bias = a["b_b_gate"][0].rearrange("(o n) -> o n", o=1)
                sp.dma_start(b_gate_bias[:, :], bias.to_broadcast([P, 3 * B_HEADS])).then_inc(b_params_loaded, 16)
                for n, name in enumerate(("b_phik_w2", "b_phiv_w2")):
                    sp.dma_start(b_w2[:, n, :, :], a[name][0].rearrange("(c p) n -> p c n", p=P)).then_inc(b_params_loaded, 16)

            def ffn(st):
                L, u = st.layer, st.unit

                def gate(i):
                    return up_w[L][:, :, bass.ds(i * 256, 256)]

                def val(i):
                    return up_w[L][:, :, bass.ds(i * 256 + F_HIDDEN, 256)]

                def down(i):
                    return down_w[L][bass.ds(i, 1)].rearrange("o p b n -> (o p) b n")

                load(u, gate(0))
                load(u + 1, val(0))
                if mixer_after(st) and mixer_after(st).kind == "b":
                    b_parameters(st["h_added"])
                with sp.Fori(0, FC - 1) as i:
                    load(u + 2, gate(i + 1), i * 3)
                    load(u + 3, val(i + 1), i * 3)
                    load(u + 4, down(i), i * 3)
                load(u + 3 * FC - 1, down(FC - 1))

            def mlstm(st):
                j, u = st.layer // 3, st.unit
                w_in = a["a_w_in"][j].rearrange("(kt p) n -> p kt n", p=P)
                w_out = a["a_w_out"][j].rearrange("(h c b p) n -> h c p b n", c=2, b=2, p=P)

                def inner(h, c, at):
                    return w_in[:, :, bass.ds(h * A_DH + (at + c * 256), 256)]

                def head_w(name, h):
                    return a[name][j][bass.ds(h, 1)].rearrange("o (kt p) n -> (o p) kt n", p=P)

                def head(h, b, passed, more):
                    load(b, head_w("a_wv", h), passed)
                    load(b + 1, head_w("a_wq", h), passed)
                    load(b + 2, head_w("a_wk", h), passed)
                    load(b + 3, inner(h, 0, A_INNER), passed)
                    load(b + 4, inner(h, 1, A_INNER), passed)
                    if more:
                        load(b + 5, inner(h + 1, 0, 0), passed)
                        load(b + 6, inner(h + 1, 1, 0), passed)
                        b += 2
                    for c in range(2):
                        load(b + 5 + c, w_out[bass.ds(h, 1)].rearrange("o c p b n -> (o c) p b n")[c], passed)

                load(u, inner(0, 0, 0))
                load(u + 1, inner(0, 1, 0))
                head(0, u + 2, 0, True)
                with sp.Fori(1, A_HEADS - 1) as h:
                    head(h, u + 2, h * 9, True)
                head(A_HEADS - 1, u + 2 + 9 * (A_HEADS - 1), 0, False)

            def nsa(st):
                u = st.unit
                w_in = a["b_w_in"][0].rearrange("(kt p) n -> p kt n", p=P)
                w_out = a["b_w_out"][0].rearrange("(c b p) n -> c p b n", b=2, p=P)

                def kv(n):
                    return w_in[:, :, D + n * B_KV:D + (n + 1) * B_KV]

                def phi(name, n):
                    return a[name][0][n * 1024:(n + 1) * 1024, :].rearrange("(kt p) n -> p kt n", p=P)

                order = [kv(0), kv(1), kv(2), phi("b_phik_w1", 0), phi("b_phik_w1", 1), kv(3),
                         phi("b_phiv_w1", 0), phi("b_phiv_w1", 1), kv(4), kv(5)]
                order += [w_in[:, :, 256 * g:256 * (g + 1)] for g in range(B_GROUPS)]
                order += [w_out[c] for c in range(4)]
                for n, src in enumerate(order):
                    load(u + n, src)

            def dilated(st):
                u = st.unit
                w_in = a["c_w_in"][0].rearrange("(kt p) n -> p kt n", p=P)
                w_out = a["c_w_out"][0].rearrange("(c b p) n -> c p b n", b=2, p=P)

                def quad(i, passed):
                    for g in range(C_GROUPS):
                        for part in range(3):
                            load(u + 3 * g + part, w_in[:, :, bass.ds((i + (3 * g + part) * C_QUADS) * 256, 256)], passed)

                quad(0, 0)
                with sp.Fori(1, C_QUADS) as i:
                    quad(i, i * 9)
                for c in range(4):
                    load(u + 9 * C_QUADS + c, w_out[c])

            if STAGES[1].kind == "b":
                b_parameters(0)
            for st in STAGES:
                if st.kind == "ffn":
                    ffn(st)
                if st.kind == "a":
                    mlstm(st)
                if st.kind == "b":
                    nsa(st)
                if st.kind == "c":
                    dilated(st)
            for t in range(TT):
                sp.wait_ge(out_ready, t + 1)
                sp.dma_start(out[0, t * P:(t + 1) * P, :], hs[:, t, :]).then_inc(out_stored, 16)
            sp.wait_ge(out_stored, 16 * TT)
            if not any(st.kind == "a" for st in STAGES):
                sp.wait_ge(gate_loaded, 16 * N_GATE_LOADS)
            if not any(st.kind == "b" for st in STAGES):
                sp.wait_ge(masks_ready, 8)

        @block.gpsimd
        def _(pool):
            pool.memset(ident[:, :], 0.0).then_inc(ident_ready, 1)
            pool.wait_ge(ident_ready, 1)
            pool.affine_select(out=ident[:, :], in_=ident[:, :], compare_op=ALU.not_equal, fill=1.0, base=0,
                               pattern=[[-1, P]], channel_multiplier=1).then_inc(ident_ready, 1)
            pool.memset(half[:, :], -0.5).then_inc(ident_ready, 1)
            pool.memset(key_first[:, :], 1.0).then_inc(ident_ready, 1)
            pool.wait_ge(ident_ready, 4)
            pool.affine_select(out=key_first[:, :], in_=key_first[:, :], compare_op=ALU.is_ge, fill=0.0, base=0,
                               pattern=[[1, P]], channel_multiplier=-1).then_inc(ident_ready, 1)
            pool.memset(residue4[:, :], 0.0).then_inc(ident_ready, 1)
            pool.memset(residue16[:, :], 0.0).then_inc(ident_ready, 1)
            pool.wait_ge(ident_ready, 7)
            for tile, m in ((residue4, 4), (residue16, 16)):
                at = tile[:, :].rearrange("r (a b) -> r a b", b=m)
                pool.affine_select(out=at, in_=at, compare_op=ALU.not_equal, fill=1.0, base=0,
                                   pattern=[[0, P // m], [-1, m]], channel_multiplier=1).then_inc(residues_ready, 1)
            def norm(st):
                at = st["rstd_ready"]
                for t in range(TT):
                    pool.wait_ge(S["ssq_ready"], st["ssq_ready"] + 2 * t + 2)
                    pool.tensor_scalar(mean_sq[:, t:t + 1], ssq[:, t, 0:1], ssq[:, t, 1:2], EPS,
                                       ALU.add, ALU.add).then_inc(S["rstd_ready"], 1)
                    pool.wait_ge(S["rstd_ready"], at + 2 * t + 1)
                    pool.tensor_tensor(rstd[:, t:t + 1], mean_sq[:, t:t + 1], half[:, t:t + 1],
                                       ALU.pow).then_inc(S["rstd_ready"], 1)

            norm(STAGES[0])
            pool.wait_ge(masks_filled, 2)

            def keep(at, pattern, base, mult):
                pool.affine_select(out=at, in_=at, compare_op=ALU.is_ge, fill=NEG, base=base, pattern=pattern,
                                   channel_multiplier=mult).then_inc(masks_ready, 1)

            keep(mask_c[:, 0:C_T0].rearrange("p (g n) -> p g n", g=C_GROUPS), [[0, C_GROUPS], [-1, P]], 0, 1)
            t1 = mask_c[:, C_T0:C_SCORES].rearrange("p (g n) -> p g n", g=C_GROUPS)
            keep(t1[:, :, P:T], [[0, C_GROUPS], [-1, P]], 0, 1)
            keep(t1[:, 0, 0:P], [[1, P]], 0, -1)
            keep(mask_b[:, 0:T].rearrange("p (g n) -> p g n", g=2), [[0, 2], [-1, P]], 0, 1)
            keep(mask_b[:, T:T + 16], [[-16, 16]], -31, 1)
            keep(mask_b[:, 528:544], [[-16, 16]], P - 31, 1)
            keep(mask_b[:, 544:800].rearrange("p (g n) -> p g n", g=2), [[0, 2], [-1, P]], 0, 1)
            pool.affine_select(out=has_cmp[:, :], in_=has_cmp[:, :], compare_op=ALU.is_ge, fill=0.0, base=-31,
                               pattern=[[0, 1]], channel_multiplier=1).then_inc(masks_ready, 1)

            def mlstm(st):
                with pool.Fori(0, A_HEADS) as h:
                    pool.wait_ge(S["decay_exp"], h + (st["decay_exp"] + 1))
                    for t in range(TT):
                        at = weights[:, t, t * P:(t + 1) * P]
                        ins = pool.tensor_tensor(at, at, key_first[:, :], ALU.mult)
                    ins.then_inc(S["decay_masked"], 1)
                    pool.wait_ge(S["head_stats"], h * 11 + (st["head_stats"] + 11))
                    pool.tensor_tensor(var_rs[:, :], var_eps[:, :], half[:, :], ALU.pow).then_inc(S["var_pow"], 1)

            for st in STAGES[1:]:
                if st.kind in ("norm", "last"):
                    norm(st)
                if st.kind == "a":
                    mlstm(st)

        @block.scalar
        def _(act):
            for t in range(TT):
                act.dma_start(h[:, t, :], a["x"][0, t * P:(t + 1) * P, :]).then_inc(x_loaded[t], 16)
            act.wait_ge(rows_cleared, 1)
            for group, at, src in ROW_LOADS[:2]:
                act.dma_start(rows[at:at + src.shape[0], group, :], src).then_inc(gains_loaded, 16)
            for j in range(2):
                act.dma_start(gate_raw[:, j, :, :],
                              a["a_w_in"][j, :, 2 * A_INNER:].rearrange("(kt p) n -> p kt n", p=P)).then_inc(gate_loaded, 16)
            act.dma_start(final_gain[:, :], a["norm_final"].rearrange("(o n) -> o n", o=1).to_broadcast([P, D])).then_inc(gain_loaded, 16)

            def split_high(u, passed=0):
                if u >= N_UNITS:
                    return
                k = slot(u)
                act.wait_ge(unit_loaded[k], passed * 16 // RING + 16 * (u // RING + 1))
                if u >= RING or not isinstance(passed, int):
                    act.wait_ge(unit_used, passed + (u - RING + 1))
                act.activation(w_hi[k][:, :], raw[k][:, :], ACT.Copy).then_inc(hi_ready, 1)

            def gates_high(mixer):
                if mixer.kind == "a":
                    act.wait_ge(gates_padded, mixer.layer // 3 + 1)
                    act.activation(gate_hi[:, :, :], gate_pad[:, :, :], ACT.Copy).then_inc(S["gates_split"], 1)
                else:
                    act.wait_ge(b_params_loaded, 64)
                    act.activation(b_gate_hi[:, :, :], b_gate_raw[:, :, :], ACT.Copy).then_inc(S["b_gates_split"], 1)

            def square_sums(st, scaled):
                for t in range(TT):
                    for b in range(2):
                        if st.first:
                            act.wait_ge(x_loaded[t], 16)
                        else:
                            act.wait_ge(S["h_added"], st["h_added"] + 2 * t + b + 1)
                        at = slice(b * 512, (b + 1) * 512)
                        act.activation(hs[:, t, at], h[:, t, at], ACT.Square, scale=D ** -0.5,
                                       accum_out=ssq[:, t, b:b + 1]).then_inc(S["ssq_ready"], 1)
                if scaled:
                    for t in range(TT):
                        act.wait_ge(S["rstd_ready"], st["rstd_ready"] + 2 * t + 2)
                        act.activation(hs[:, t, 512:], h[:, t, 512:], ACT.Copy, scale=rstd[:, t:t + 1]).then_inc(S["hs_act_ready"], 1)

            def norm(st):
                if not st.first:
                    square_sums(st, True)
                else:
                    act.wait_ge(gains_ready, 1)
                for kt in range(KT):
                    if kt < 4:
                        act.wait_ge(S["turned"], st["turned"] + kt + 1)
                    else:
                        act.wait_ge(S["hn_lo_ready"], st["hn_lo_ready"] + kt - 3)
                    act.activation(hn_hi[:, kt, :], ps[:, kt % 4, (kt // 4) * T:(kt // 4 + 1) * T], ACT.Copy,
                                   scale=col(0, st.gain + kt)).then_inc(S["hn_hi_ready"], 1)
                split_high(st.unit + 1)

            def ffn(st):
                L, u = st.layer, st.unit
                act.preload_act_table(ACT.Silu)

                def last_tap(i, which, bank, tile):
                    acc = acc_gate if which == "gate" else acc_val
                    for n in range(2):
                        ins = act.activation(acc[:, n, :], ps[:, bank, n * T:(n + 1) * T], ACT.Identity,
                                             scale=col(5 + 2 * L, i * 2 + (tile + n)),
                                             bias=col(5 + 2 * L, i * 2 + (tile + n + 2 * F_TILES)))
                    ins.then_inc(S[which + "_acc"], 1)

                def activate(i, used):
                    act.wait_ge(unit_used, used)
                    last_tap(i, "val", VAL, F_TILES)
                    act.wait_ge(S["gate_taps"], i * 4 + (st["gate_taps"] + 4))
                    act.activation(acc_gate[:, :, :], acc_gate[:, :, :], ACT.Silu).then_inc(S["silu_ready"], 1)

                def product_high(i, to):
                    act.wait_ge(S["prod_ready"], i + (st["prod_ready"] + 1))
                    act.activation(to, prod[:, :, :], ACT.Copy).then_inc(S["g_hi_ready"], 1)

                split_high(u + 2)
                act.wait_ge(unit_used, u + 1)
                last_tap(0, "gate", GATE, 0)
                split_high(u + 3)
                activate(0, u + 2)
                split_high(u + 4)
                product_high(0, g_hi[:, :, :])
                act.wait_ge(unit_used, u + 3)
                last_tap(1, "gate", GATE, 0)
                split_high(u + 5)
                if mixer_after(st):
                    gates_high(mixer_after(st))
                with act.Fori(1, FC - 1) as i:
                    activate(i, i * 3 + (u + 1))
                    split_high(u + 3, i * 3)
                    act.wait_ge(unit_used, i * 3 + (u + 2))
                    product_high(i, g_hi[:, :, :])
                    split_high(u + 4, i * 3)
                    act.wait_ge(unit_used, i * 3 + (u + 3))
                    last_tap(i + 1, "gate", GATE, 0)
                    split_high(u + 5, i * 3)
                activate(FC - 1, u + 3 * FC - 2)
                product_high(FC - 1, hn_hi[:, 0:2, :])
                split_high(u + 3 * FC)

            def mlstm(st):
                j, u = st.layer // 3, st.unit

                def conv_start(h, c, bank):
                    for n in range(2):
                        act.activation(xc[:, 2 * c + n, :], ps[:, bank, n * T:(n + 1) * T], ACT.Identity,
                                       scale=col(1, h * A_HT + (j * A_TAPS * A_TILES + 3 * A_TILES + 2 * c + n)),
                                       bias=col(2, h * A_HT + (j * A_TILES + 2 * c + n)))
                    act.activation(xm_hi[:, 2 * c:2 * c + 2, :], ps[:, bank, :], ACT.Copy).then_inc(S["xm_acc"], 1)

                def conv_end(h, c):
                    act.wait_ge(S["xm_taps"], h * 12 + (st["xm_taps"] + 6 * c + 6))
                    at = slice(2 * c, 2 * c + 2)
                    act.activation(xc[:, at, :], xc[:, at, :], ACT.Silu).then_inc(S["xc_ready"], 1)
                    act.wait_ge(S["xc_ready"], h * 2 + (st["xc_ready"] + c + 1))
                    act.activation(xc_hi[:, at, :], xc[:, at, :], ACT.Copy).then_inc(S["xc_hi_ready"], 1)

                def head(h, b, passed, more):
                    for n in range(A_HT):
                        ins = act.activation(skipped[:, n, :], xc[:, n, :], ACT.Copy,
                                             scale=col(2, h * A_HT + (4 * A_TILES + j * A_TILES + n)))
                    ins.then_inc(S["skip_ready"], 1)
                    act.wait_ge(S["decay_diff"], h + (st["decay_diff"] + 1))
                    act.activation(weights[:, 0, :], weights[:, 0, :], ACT.Exp, scale=-1.0)
                    act.activation(weights[:, 1, P:T], weights[:, 1, P:T], ACT.Exp, scale=-1.0).then_inc(S["decay_exp"], 1)
                    split_high(b + 2, passed)
                    act.wait_ge(unit_used, passed + (b + 1))
                    act.activation(v_s[:, :, :], ps[:, 4:6, :], ACT.Copy).then_inc(S["v_ready"], 1)
                    split_high(b + 3, passed)
                    act.wait_ge(unit_used, passed + (b + 2))
                    act.activation(q_t[:, :, :], ps[:, 6:8, :], ACT.Copy, scale=float(A_DH) ** -0.5).then_inc(S["q_ready"], 1)
                    split_high(b + 4, passed)
                    split_high(b + 5, passed)
                    act.wait_ge(unit_used, passed + (b + 4))
                    act.activation(o_gate[:, 0:2, :], ps[:, 5, :], ACT.Sigmoid).then_inc(S["o_ready"], 1)
                    split_high(b + 6, passed)
                    act.wait_ge(unit_used, passed + (b + 5))
                    act.activation(o_gate[:, 2:4, :], ps[:, 4, :], ACT.Sigmoid).then_inc(S["o_ready"], 1)
                    if more:
                        split_high(b + 7, passed)
                        act.wait_ge(S["skip_ready"], h + (st["skip_ready"] + 1))
                        act.wait_ge(unit_used, passed + (b + 6))
                        conv_start(h + 1, 0, 4)
                    for c in range(2):
                        act.wait_ge(S["y_steps"], h * 6 + (st["y_steps"] + 3 * c + 3))
                        at = slice(2 * c, 2 * c + 2)
                        act.activation(y_hi[:, at, :], y_all[:, at, :], ACT.Copy).then_inc(S["y_hi_ready"], 1)
                    if more:
                        split_high(b + 8, passed)
                        act.wait_ge(unit_used, passed + (b + 7))
                        conv_start(h + 1, 1, 5)
                        conv_end(h + 1, 0)
                        split_high(b + 9, passed)
                        conv_end(h + 1, 1)
                        split_high(b + 10, passed)
                    else:
                        split_high(b + 7, passed)

                split_high(u + 2)
                act.wait_ge(S["gate_rows"], st["gate_rows"] + 4)
                act.activation(expf[:, :], absf[:, :], ACT.Exp, scale=-1.0).then_inc(S["gate_acts"], 1)
                act.wait_ge(S["gate_acts"], st["gate_acts"] + 1)
                act.activation(logf[:, :], expf[:, :], ACT.Ln, bias=1.0).then_inc(S["gate_acts"], 1)
                act.wait_ge(unit_used, u + 1)
                conv_start(0, 0, 4)
                split_high(u + 3)
                act.wait_ge(unit_used, u + 2)
                conv_start(0, 1, 5)
                act.wait_ge(S["gates_spread"], st["gates_spread"] + 1)
                act.activation(floor_col[:, :, :], ps[:, 0, 8:16], ACT.Exp, scale=-1.0).then_inc(S["gate_cols"], 1)
                act.activation(top_all[:, :, :], ps[:, 6:8, :], ACT.Copy).then_inc(S["gate_cols"], 1)
                conv_end(0, 0)
                conv_end(0, 1)
                act.wait_ge(S["gate_cols"], st["gate_cols"] + 3)
                with act.Fori(0, A_HEADS - 1) as h:
                    head(h, u + 2, h * 9, True)
                head(A_HEADS - 1, u + 2 + 9 * (A_HEADS - 1), 0, False)

            def nsa(st):
                u = st.unit
                split_high(u + 2)
                act.wait_ge(unit_used, u + 1)
                for s in range(2):
                    for d in range(2):
                        ins = act.activation(x2[0][DH * d:DH * (d + 1), s::2, 0:T - d],
                                             ps[DH * s:DH * (s + 1), 0, :].rearrange("p (n t) -> p n t", n=2)[:, :, d:T], ACT.Copy)
                ins.then_inc(S["b_cmp_copied"], 1)
                split_high(u + 3)

                def flat_high(n):
                    act.wait_ge(S["b_flat_ready"], n + 1)
                    act.activation(flat_hi[n], flat[n].rearrange("p m g n -> p (m g n)"), ACT.Copy).then_inc(S["b_flat_hi"], 1)

                def keys(s, unit):
                    act.wait_ge(unit_used, unit + 1)
                    for d in range(2):
                        src = ps[DH * d:DH * (d + 1), 2, :].rearrange("p (n t x) -> p n t x", n=2, t=TT)
                        for e in range(2):
                            dst = b_keys[DH * e:DH * (e + 1), d::2, :].rearrange("p n (t x) -> p n t x", t=TT)
                            ins = act.activation(dst[:, :, :, s * P:(s + 1) * P], src, ACT.Copy)
                    ins.then_inc(S["b_keys_ready"], 1)

                def hidden(n):
                    act.wait_ge(S["b_pre_turned"], n + 1)
                    for c in range(2):
                        ins = act.activation(b_hidden[:, n, c, :], ps[:, 5 - 4 * n, P * c:P * c + B_GROUPS * B_CMP], ACT.Silu,
                                             bias=col(3, 32 + 2 * n + c))
                    ins.then_inc(S["b_hidden_ready"], 1)

                flat_high(0)
                split_high(u + 4)
                keys(0, u + 2)
                flat_high(1)
                split_high(u + 5)
                act.wait_ge(S["b_gate_steps"], 1)
                for t in range(TT):
                    gate_in = b_gate_in[:, t, :].rearrange("p (h c) -> p h c", c=3)
                    act.activation(b_gates[:, :, 4 + t:5 + t], gate_in[:, :, 0:1], ACT.Sigmoid)
                    ins = act.activation(b_gates[:, :, 2 * t:2 * t + 2], gate_in[:, :, 1:3], ACT.Sigmoid)
                ins.then_inc(S["b_gate_steps"], 1)
                split_high(u + 6)
                split_high(u + 7)
                split_high(u + 8)
                hidden(0)
                split_high(u + 9)
                split_high(u + 10)
                split_high(u + 11)
                hidden(1)
                keys(1, u + 8)
                split_high(u + 12)
                for g in range(B_GROUPS):
                    act.wait_ge(unit_used, u + 11 + g)
                    act.activation(b_q[:, 2 * g:2 * g + 2, :], ps[:, (4, 5, 0, 1)[g], :], ACT.Copy,
                                   scale=float(DH) ** -0.5).then_inc(S["b_q_ready"], 1)
                    split_high(u + 13 + g)
                act.wait_ge(S["b_q_ready"], B_GROUPS)
                act.wait_ge(S["b_gate_steps"], 3)
                act.wait_ge(S["b_cmp_ready"], 2)
                act.wait_ge(S["b_values_ready"], 2)
                act.preload_act_table(ACT.Exp)

                def exps(g, m):
                    act.wait_ge(S["b_neg"], g * B_PER + (m + 1))
                    for n, at in enumerate(branches(b_sm[:, m % 2, :])):
                        ins = act.activation(at, at, ACT.Exp, bias=b_nm[:, m % 2, n:n + 1], accum_out=b_den[:, m % 2, n:n + 1])
                    ins.then_inc(S["b_exp"], 1)

                def turned(g, m):
                    act.wait_ge(S["b_turned"], g * B_PER + (m + 1))
                    act.activation(b_pt[:, m % 2, 0:512], ps[:, 3, :], ACT.Copy).then_inc(S["b_pt_act"], 1)

                def stage_scores(g):
                    if not isinstance(g, int):
                        act.wait_ge(S["b_scores"], g * B_PER)
                        act.wait_ge(S["b_normed"], g * B_PER)
                    act.activation(b_sq, b_q[:, bass.ds(g * 2, 2), :], ACT.Copy)
                    act.activation(b_sk, b_keys[:, bass.ds(g, 1), 0:528].rearrange("p o n -> p (o n)"), ACT.Copy)
                    act.activation(b_sgate[:, :], b_gates[:, bass.ds(g * B_PER, B_PER), :].rearrange("p h n -> p (h n)"),
                                   ACT.Copy).then_inc(S["b_staged"], 1)

                def stage_values(g):
                    if not isinstance(g, int):
                        act.wait_ge(S["b_out"], g * B_PER)
                    act.activation(b_sv, b_values[:, :, bass.ds(g, 1), :].rearrange("p t o n -> p t (o n)"), ACT.Copy)
                    act.activation(b_svc[0:B_CMP, :], b_vcmp[0:B_CMP, bass.ds(g, 1), :].rearrange("p o n -> p (o n)"),
                                   ACT.Copy).then_inc(S["b_staged"], 1)

                def output_high(g, pair):
                    act.wait_ge(S["b_out"], g * B_PER + (2 * pair + 2))
                    act.activation(b_o_hi[:, bass.ds(g * 2 + pair, 1), :].rearrange("p o t -> p (o t)"),
                                   ps[:, 6 + pair, 0:T], ACT.Copy).then_inc(S["b_o_hi"], 1)

                def group(g, first):
                    stage_scores(g)
                    if not first:
                        turned(g - 1, 3)
                    exps(g, 0)
                    if not first:
                        output_high(g - 1, 1)
                    stage_values(g)
                    turned(g, 0)
                    exps(g, 1)
                    exps(g, 2)
                    turned(g, 1)
                    turned(g, 2)
                    output_high(g, 0)
                    exps(g, 3)

                group(0, True)
                with act.Fori(1, B_GROUPS) as g:
                    group(g, False)
                turned(B_GROUPS - 1, 3)
                output_high(B_GROUPS - 1, 1)
                for c in range(1, 3):
                    split_high(u + 16 + c)

            def dilated(st):
                u = st.unit
                act.preload_act_table(ACT.Exp)

                def evacuate(i, x):
                    g, part = x // 3, x % 3
                    if part != 1:
                        act.wait_ge(unit_used, i * 9 + (u + x + 1))
                    if part == 0:
                        act.activation(c_q[:, g, :, :], ps[:, 0, :], ACT.Copy, scale=float(DH) ** -0.5).then_inc(S["c_q_ready"], 1)
                    if part == 2:
                        act.activation(c_v[:, g, :, :], ps[:, 3, :], ACT.Copy).then_inc(S["c_v_ready"], 1)

                def exps(i, m):
                    act.wait_ge(S["c_neg"], i * 4 + (m + 1))
                    for t, at in enumerate((c_sm[:, m % 2, 0:C_T0], c_sm[:, m % 2, C_T0:C_SCORES])):
                        ins = act.activation(at, at, ACT.Exp, bias=c_nm[:, m % 2, t:t + 1], accum_out=c_den[:, m % 2, t:t + 1])
                    ins.then_inc(S["c_exp"], 1)

                def turned(i, m):
                    act.wait_ge(S["c_turned"], i * 4 + (m + 1))
                    act.activation(c_pt[:, m % 2, 0:512], ps[:, 3, :], ACT.Copy)
                    act.activation(c_pt[:, m % 2, 1024:C_PT], ps[:, 5, 0:P], ACT.Copy).then_inc(S["c_pt_act"], 1)

                def output_high(i, pair):
                    act.wait_ge(S["c_out"], i * 4 + (2 * pair + 2))
                    act.activation(c_o_hi[:, bass.ds(i * 2 + pair, 1), :].rearrange("p o t -> p (o t)"),
                                   ps[:, 6 + pair, 0:T], ACT.Copy).then_inc(S["c_o_hi"], 1)

                def quad(i, first):
                    split_high(u + 2, i * 9)
                    if not first:
                        turned(i - 1, 3)
                    evacuate(i, 0)
                    split_high(u + 3, i * 9)
                    split_high(u + 4, i * 9)
                    if not first:
                        output_high(i - 1, 1)
                    for x in range(3, 8):
                        evacuate(i, x - 1)
                        split_high(u + x + 2, i * 9)
                    exps(i, 0)
                    split_high(u + 10, i * 9)
                    evacuate(i, 8)
                    turned(i, 0)
                    exps(i, 1)
                    exps(i, 2)
                    turned(i, 1)
                    exps(i, 3)
                    turned(i, 2)
                    output_high(i, 0)

                quad(0, True)
                with act.Fori(1, C_QUADS) as i:
                    quad(i, False)
                split_high(u + 9 * C_QUADS + 2)
                turned(C_QUADS - 1, 3)
                output_high(C_QUADS - 1, 1)
                for c in range(1, 3):
                    split_high(u + 9 * C_QUADS + 2 + c)

            square_sums(STAGES[0], True)
            split_high(0)
            if STAGES[1].kind in ("a", "b"):
                gates_high(STAGES[1])
            norm(STAGES[0])
            act.wait_ge(cols_ready, 3)
            for st in STAGES[1:]:
                if st.kind == "norm":
                    norm(st)
                if st.kind == "b":
                    nsa(st)
                if st.kind == "c":
                    dilated(st)
                if st.kind == "a":
                    mlstm(st)
                if st.kind == "ffn":
                    ffn(st)
                if st.kind == "last":
                    square_sums(st, False)

        @block.vector
        def _(dve):
            dve.memset(rows[:, :, :], 0.0).then_inc(rows_cleared, 1)
            dve.memset(mask_c[:, :], 0.0)
            dve.memset(mask_b[:, :], 0.0)
            dve.memset(has_cmp[:, :], 1.0).then_inc(masks_zeroed, 1)
            dve.memset(zeros[:, :], 0.0).then_inc(zeros_ready, 1)
            dve.wait_ge(zeros_ready, 1)
            dve.tensor_copy(zero_r[:, :], zeros[:, :]).then_inc(zeros_ready, 1)
            def split_low(u, passed=0):
                if u >= N_UNITS:
                    return
                k = slot(u)
                dve.wait_ge(hi_ready, passed + (u + 1))
                dve.tensor_tensor(w_lo[k][:, :], raw[k][:, :], w_hi[k][:, :].bitcast(fp32),
                                  ALU.subtract).then_inc(lo_ready, 1)

            def gates_low(mixer):
                if mixer.kind == "b":
                    dve.wait_ge(S["b_gates_split"], 1)
                    dve.tensor_tensor(b_gate_lo[:, :, :], b_gate_raw[:, :, :], b_gate_hi[:, :, :].bitcast(fp32),
                                      ALU.subtract).then_inc(S["b_gates_split"], 1)
                    return
                j = mixer.layer // 3
                dve.memset(gate_pad[:, :, :], 0.0).then_inc(gates_zeroed, 1)
                dve.wait_ge(gates_zeroed, j + 1)
                dve.wait_ge(gate_loaded, 16 * N_GATE_LOADS)
                for n in range(2):
                    ins = dve.tensor_copy(gate_pad[:, :, 32 * n:32 * n + A_HEADS],
                                          gate_raw[:, j, :, n * A_HEADS:(n + 1) * A_HEADS])
                ins.then_inc(gates_padded, 1)
                dve.wait_ge(S["gates_split"], mixer["gates_split"] + 1)
                dve.tensor_tensor(gate_lo[:, :, :], gate_pad[:, :, :], gate_hi[:, :, :].bitcast(fp32),
                                  ALU.subtract).then_inc(S["gates_split"], 1)

            def add_residual(st, t):
                for b in range(2):
                    if 2 * t + b < 3:
                        dve.wait_ge(S["y_banks"], st["y_banks"] - 3 + (2 * t + b + 1))
                    else:
                        dve.wait_ge(unit_used, st.unit)
                    at = slice(b * 512, (b + 1) * 512)
                    dve.tensor_tensor(h[:, t, at], ps[:, 2 * t + b, :], h[:, t, at], ALU.add).then_inc(S["h_added"], 1)

            def scale_rows(st):
                for t in range(TT):
                    dve.wait_ge(S["rstd_ready"], st["rstd_ready"] + 2 * t + 2)
                    dve.tensor_scalar(hs[:, t, 0:512], h[:, t, 0:512], rstd[:, t:t + 1], None,
                                      ALU.mult).then_inc(S["hs_ready"], 1)

            def norm(st):
                if not st.first:
                    for t in range(TT):
                        add_residual(st, t)
                    scale_rows(st)
                for kt in range(KT):
                    dve.wait_ge(S["hn_hi_ready"], st["hn_hi_ready"] + kt + 1)
                    dve.scalar_tensor_tensor(out=hn_lo[:, kt, :], in0=ps[:, kt % 4, (kt // 4) * T:(kt // 4 + 1) * T],
                                             scalar=col(0, st.gain + kt), in1=hn_hi[:, kt, :].bitcast(fp32),
                                             op0=ALU.mult, op1=ALU.subtract).then_inc(S["hn_lo_ready"], 1)
                split_low(st.unit + 1)

            def last(st):
                dve.wait_ge(gain_loaded, 16)
                for t in range(TT):
                    add_residual(st, t)
                for t in range(TT):
                    dve.wait_ge(S["rstd_ready"], st["rstd_ready"] + 2 * t + 2)
                    dve.scalar_tensor_tensor(out=hs[:, t, :], in0=h[:, t, :], scalar=rstd[:, t:t + 1],
                                             in1=final_gain[:, :], op0=ALU.mult, op1=ALU.mult).then_inc(out_ready, 1)

            def ffn(st):
                L, u = st.layer, st.unit

                def earlier_taps(i, which, bank, tile):
                    dve.wait_ge(S[which + "_acc"], i + (st[which + "_acc"] + 1))
                    acc = acc_gate if which == "gate" else acc_val
                    for tap, back in ((1, 1), (0, 2)):
                        for n in range(2):
                            at = (4 if tap < 2 else 5) + 2 * L
                            dve.scalar_tensor_tensor(
                                out=acc[:, n, back:T], in0=ps[:, bank, n * T:(n + 1) * T - back],
                                scalar=col(at, i * 2 + (tap * 2 * F_TILES + tile + n)), in1=acc[:, n, back:T],
                                op0=ALU.mult, op1=ALU.add).then_inc(S[which + "_taps"], 1)
                        if tap == 1:
                            dve.wait_ge(S[which + "_taps"], i * 4 + (st[which + "_taps"] + 2))

                def multiply(i):
                    earlier_taps(i, "val", VAL, F_TILES)
                    dve.wait_ge(S["silu_ready"], i + (st["silu_ready"] + 1))
                    dve.wait_ge(S["val_taps"], i * 4 + (st["val_taps"] + 4))
                    dve.tensor_tensor(prod[:, :, :], acc_gate[:, :, :], acc_val[:, :, :],
                                      ALU.mult).then_inc(S["prod_ready"], 1)

                def product_low(i, high, to):
                    dve.wait_ge(S["g_hi_ready"], i + (st["g_hi_ready"] + 1))
                    dve.tensor_tensor(to, prod[:, :, :], high.bitcast(fp32), ALU.subtract).then_inc(S["g_lo_ready"], 1)

                split_low(u + 2)
                earlier_taps(0, "gate", GATE, 0)
                split_low(u + 3)
                multiply(0)
                split_low(u + 4)
                product_low(0, g_hi[:, :, :], g_lo[:, :, :])
                earlier_taps(1, "gate", GATE, 0)
                split_low(u + 5)
                if mixer_after(st):
                    gates_low(mixer_after(st))
                with dve.Fori(1, FC - 1) as i:
                    multiply(i)
                    split_low(u + 3, i * 3)
                    product_low(i, g_hi[:, :, :], g_lo[:, :, :])
                    split_low(u + 4, i * 3)
                    earlier_taps(i + 1, "gate", GATE, 0)
                    split_low(u + 5, i * 3)
                multiply(FC - 1)
                product_low(FC - 1, hn_hi[:, 0:2, :], hn_lo[:, 0:2, :])
                split_low(u + 3 * FC)

            def mlstm(st):
                j, u = st.layer // 3, st.unit
                rows_at = st["gate_rows"]
                split_low(u + 2)
                dve.memset(ones[:, :], 1.0)
                dve.wait_ge(S["gates_made"], st["gates_made"] + 1)
                dve.tensor_scalar(log_i[:, :], ps[0:A_HEADS, 6, 0:T], gate_bias[:, j, 0:1], None, ALU.add).then_inc(S["gate_rows"], 1)
                dve.tensor_copy(cum_f[:, :], ps[32:32 + A_HEADS, 6, 0:T]).then_inc(S["gate_rows"], 1)
                dve.wait_ge(S["gate_rows"], rows_at + 2)
                dve.tensor_scalar(forget[:, :], cum_f[:, :], gate_bias[:, j, 1:2], None, ALU.add).then_inc(S["gate_rows"], 1)
                dve.wait_ge(S["gate_rows"], rows_at + 3)
                dve.scalar_tensor_tensor(out=absf[:, :], in0=forget[:, :], scalar=-1.0, in1=forget[:, :],
                                         op0=ALU.mult, op1=ALU.max).then_inc(S["gate_rows"], 1)
                dve.wait_ge(S["gate_acts"], st["gate_acts"] + 2)
                dve.scalar_tensor_tensor(out=forget[:, :], in0=forget[:, :], scalar=0.0, in1=logf[:, :],
                                         op0=ALU.min, op1=ALU.subtract).then_inc(S["gate_rows"], 1)
                dve.wait_ge(S["gate_rows"], rows_at + 5)
                dve.tensor_tensor_scan(cum_f[:, :], forget[:, :], zeros[0:A_HEADS, 0:T], 0.0, ALU.add, ALU.add).then_inc(S["gate_rows"], 1)
                dve.wait_ge(S["gate_rows"], rows_at + 6)
                dve.tensor_tensor(source[:, :], log_i[:, :], cum_f[:, :], ALU.subtract).then_inc(S["gate_rows"], 1)
                dve.wait_ge(S["gate_rows"], rows_at + 7)
                dve.tensor_tensor_scan(top[:, :], source[:, :], zeros[0:A_HEADS, 0:T], 0.0, ALU.max, ALU.max).then_inc(S["gate_rows"], 1)
                dve.wait_ge(S["gate_rows"], rows_at + 8)
                dve.tensor_tensor(stab[:, :], cum_f[:, :], top[:, :], ALU.add).then_inc(S["gate_rows"], 1)

                def conv(h, c, bank):
                    dve.wait_ge(S["xm_acc"], h * 2 + (st["xm_acc"] + c + 1))
                    dve.tensor_tensor(xm_lo[:, 2 * c:2 * c + 2, :], ps[:, bank, :].rearrange("p (n t) -> p n t", n=2),
                                      xm_hi[:, 2 * c:2 * c + 2, :].bitcast(fp32), ALU.subtract).then_inc(S["xm_lo_ready"], 1)
                    for back in range(1, A_TAPS):
                        tap = A_TAPS - 1 - back
                        if back > 1:
                            dve.wait_ge(S["xm_taps"], h * 12 + (st["xm_taps"] + 6 * c + 2 * back - 2))
                        for n in range(2):
                            acc = xc[:, 2 * c + n, back:T]
                            dve.scalar_tensor_tensor(
                                out=acc, in0=ps[:, bank, n * T:(n + 1) * T - back],
                                scalar=col(1, h * A_HT + (j * A_TAPS * A_TILES + tap * A_TILES + 2 * c + n)), in1=acc,
                                op0=ALU.mult, op1=ALU.add).then_inc(S["xm_taps"], 1)

                def conv_low(h, c):
                    dve.wait_ge(S["xc_hi_ready"], h * 2 + (st["xc_hi_ready"] + c + 1))
                    at = slice(2 * c, 2 * c + 2)
                    dve.tensor_tensor(xc_lo[:, at, :], xc[:, at, :], xc_hi[:, at, :].bitcast(fp32),
                                      ALU.subtract).then_inc(S["xc_lo_ready"], 1)

                def normalise(h):
                    at = st["head_stats"]

                    def step(ins):
                        ins.then_inc(S["head_stats"], 1)

                    def steps_done(n):
                        dve.wait_ge(S["head_stats"], h * 11 + (at + n))

                    dve.wait_ge(S["num_made"], h + (st["num_made"] + 1))
                    step(dve.tensor_copy(den[:, :], ps[:, 5, 0:TT]))
                    for t in range(TT):
                        step(dve.bn_stats(stats[:, t, :], ps[:, 6 + t, :]))
                    steps_done(3)
                    step(dve.scalar_tensor_tensor(out=den_abs[:, :], in0=den[:, :], scalar=-1.0, in1=den[:, :],
                                                  op0=ALU.mult, op1=ALU.max))
                    for t in range(TT):
                        step(dve.bn_aggr(mv[:, t, :], stats[:, t, :]))
                    steps_done(6)
                    step(dve.tensor_tensor(den_max[:, :], den_abs[:, :], floor_col[:, :, bass.ds(h, 1)].rearrange("p t o -> p (t o)"), ALU.max))
                    steps_done(7)
                    step(dve.reciprocal(den_rec[:, :], den_max[:, :]))
                    steps_done(8)
                    step(dve.tensor_tensor(rec_sq[:, :], den_rec[:, :], den_rec[:, :], ALU.mult))
                    steps_done(9)
                    step(dve.tensor_tensor(var_in[:, :], rec_sq[:, :], mv[:, :, 1], ALU.mult))
                    steps_done(10)
                    step(dve.tensor_scalar(var_eps[:, :], var_in[:, :], EPS, None, ALU.add))
                    dve.wait_ge(S["var_pow"], h + (st["var_pow"] + 1))
                    dve.tensor_tensor(h_scale[:, :], den_rec[:, :], var_rs[:, :], ALU.mult).then_inc(scale_ready, 1)
                    dve.wait_ge(scale_ready, h + (j * A_HEADS + 1))
                    for t in range(TT):
                        ins = dve.tensor_scalar(head_n[:, t, :], ps[:, 6 + t, :], mv[:, t, 0:1], h_scale[:, t:t + 1],
                                                ALU.subtract, ALU.mult)
                    ins.then_inc(S["head_normed"], 1)

                def gate_output(h):
                    dve.wait_ge(S["head_turned"], h + (st["head_turned"] + 1))
                    dve.wait_ge(S["skip_ready"], h + (st["skip_ready"] + 1))
                    dve.wait_ge(S["o_ready"], h * 2 + (st["o_ready"] + 2))
                    for c in range(2):
                        for n in (2 * c, 2 * c + 1):
                            dve.scalar_tensor_tensor(out=y_all[:, n, :], in0=ps[:, 6 + n // 2, (n % 2) * T:(n % 2 + 1) * T],
                                                     scalar=col(2, h * A_HT + (2 * A_TILES + j * A_TILES + n)),
                                                     in1=o_gate[:, n, :], op0=ALU.mult, op1=ALU.mult).then_inc(S["y_steps"], 1)
                        dve.wait_ge(S["y_steps"], h * 6 + (st["y_steps"] + 3 * c + 2))
                        at = slice(2 * c, 2 * c + 2)
                        dve.tensor_tensor(y_all[:, at, :], y_all[:, at, :], skipped[:, at, :], ALU.add).then_inc(S["y_steps"], 1)
                    for c in range(2):
                        at = slice(2 * c, 2 * c + 2)
                        dve.wait_ge(S["y_hi_ready"], h * 2 + (st["y_hi_ready"] + c + 1))
                        dve.tensor_tensor(y_lo[:, at, :], y_all[:, at, :], y_hi[:, at, :].bitcast(fp32),
                                          ALU.subtract).then_inc(S["y_lo_ready"], 1)

                def head(h, b, passed, more):
                    for t in range(TT):
                        ins = dve.tensor_scalar(weights[:, t, t * P:T], top_all[:, bass.ds(h, 1), t * P:T].rearrange("p o t -> p (o t)"),
                                                source_col[:, t, bass.ds(h, 1)], 0.0, ALU.subtract, ALU.max)
                    ins.then_inc(S["decay_diff"], 1)
                    for n in range(2, 5):
                        split_low(b + n, passed)
                    dve.wait_ge(unit_used, passed + (b + 3))
                    for n in range(2):
                        dve.tensor_copy(k_t[:, 2 * n:2 * n + 2, :],
                                        ps[:, 4 + n, :].rearrange("p (n t) -> p n t", n=2)).then_inc(S["k_ready"], 1)
                    split_low(b + 5, passed)
                    dve.wait_ge(S["scores_made"], h + (st["scores_made"] + 1))
                    dve.wait_ge(S["decay_masked"], h + (st["decay_masked"] + 1))
                    for t in range(TT):
                        at = weights[:, t, t * P:T]
                        ins = dve.tensor_tensor(at, ps[:, 6, t * T + t * P:(t + 1) * T], at, ALU.mult)
                    ins.then_inc(S["weights_ready"], 1)
                    split_low(b + 6, passed)
                    normalise(h)
                    if more:
                        split_low(b + 7, passed)
                    gate_output(h)
                    if more:
                        conv(h + 1, 0, 4)
                        split_low(b + 8, passed)
                        conv(h + 1, 1, 5)
                        conv_low(h + 1, 0)
                        split_low(b + 9, passed)
                        conv_low(h + 1, 1)
                        split_low(b + 10, passed)
                    else:
                        split_low(b + 7, passed)

                conv(0, 0, 4)
                conv(0, 1, 5)
                dve.wait_ge(S["gate_cols"], st["gate_cols"] + 1)
                dve.tensor_copy(source_col[:, :, :], ps[:, 0, 0:8].rearrange("p (t h) -> p t h", t=TT)).then_inc(S["gate_cols"], 1)
                split_low(u + 3)
                conv_low(0, 0)
                conv_low(0, 1)
                dve.wait_ge(S["gate_cols"], st["gate_cols"] + 3)
                with dve.Fori(0, A_HEADS - 1) as h:
                    head(h, u + 2, h * 9, True)
                head(A_HEADS - 1, u + 2 + 9 * (A_HEADS - 1), 0, False)

            def nsa(st):
                u = st.unit
                dve.memset(b_keys[:, :, 271:272], 0.0).then_inc(b_pad_ready, 1)
                dve.wait_ge(S["b_gates_made"], 1)
                dve.tensor_copy(b_gate_t[:, :], ps[0:3 * B_HEADS, 7, 0:T]).then_inc(S["b_gates_copied"], 1)
                split_low(u + 2)

                def flatten(n):
                    pe_col = cols[:, 3 * P + 16 * n:3 * P + 16 * n + 16].rearrange("p (m g k) -> p m g k", g=1, k=1)
                    for part in range(2):
                        src = x2[n][:, :, 16 * part:16 * part + 240].rearrange("p g (n m w) -> p w m g n", w=2, m=8)[:, 0]
                        ins = dve.tensor_tensor(flat[n][:, 8 * part:8 * part + 8], src,
                                                pe_col[:, 8 * part:8 * part + 8].to_broadcast([P, 8, B_GROUPS, B_CMP]), ALU.add)
                    ins.then_inc(S["b_flat_ready"], 1)

                def flat_low(n):
                    dve.wait_ge(S["b_flat_hi"], n + 1)
                    dve.tensor_tensor(flat_lo[n], flat[n].rearrange("p m g n -> p (m g n)"), flat_hi[n].bitcast(fp32),
                                      ALU.subtract).then_inc(S["b_flat_lo"], 1)

                def values(s, unit):
                    dve.wait_ge(unit_used, unit + 1)
                    for t in range(TT):
                        ins = dve.tensor_copy(b_values[:, t, :, s * DH:(s + 1) * DH],
                                              ps[:, 6, t * B_KV:(t + 1) * B_KV].rearrange("p (g n) -> p g n", g=B_GROUPS))
                    ins.then_inc(S["b_values_ready"], 1)

                dve.wait_ge(S["b_cmp_copied"], 1)
                flatten(0)
                split_low(u + 3)
                dve.wait_ge(unit_used, u + 2)
                for s in range(2):
                    for d in range(2):
                        ins = dve.tensor_copy(x2[1][DH * d:DH * (d + 1), s::2, 0:T - d],
                                              ps[DH * s:DH * (s + 1), 1, :].rearrange("p (n t) -> p n t", n=2)[:, :, d:T])
                ins.then_inc(S["b_cmp_copied"], 1)
                flat_low(0)
                dve.wait_ge(S["b_cmp_copied"], 2)
                flatten(1)
                split_low(u + 4)
                flat_low(1)
                dve.wait_ge(S["b_gates_turned"], 1)
                for t in range(TT):
                    ins = dve.tensor_tensor(b_gate_in[:, t, :], ps[:, 7, T + 64 * t:T + 64 * t + 48], b_gate_bias[:, :], ALU.add)
                ins.then_inc(S["b_gate_steps"], 1)
                split_low(u + 5)
                dve.wait_ge(S["b_gate_steps"], 2)
                dve.wait_ge(masks_ready, 8)
                dve.tensor_scalar(b_gates[:, :, 4:5], b_gates[:, :, 4:5], has_cmp[:, 0:1], None, ALU.mult).then_inc(S["b_gate_steps"], 1)

                def pre(n, unit):
                    dve.wait_ge(unit_used, unit + 1)
                    dve.tensor_copy(b_pre[:, n, :], ps[0:B_GROUPS * B_CMP, 4 - 4 * n, 0:T]).then_inc(S["b_pre_ready"], 1)

                split_low(u + 6)
                pre(0, u + 4)
                split_low(u + 7)
                values(0, u + 5)
                split_low(u + 8)
                dve.wait_ge(S["b_cmp_made"], 1)
                dve.tensor_copy(b_keys[:, :, 256:256 + B_CMP], ps[:, 4, 0:B_GROUPS * B_CMP].rearrange("p (g n) -> p g n", g=B_GROUPS)).then_inc(S["b_cmp_ready"], 1)
                split_low(u + 9)
                pre(1, u + 7)
                split_low(u + 10)
                split_low(u + 11)
                dve.wait_ge(S["b_cmp_made"], 2)
                dve.tensor_copy(b_vcmp[0:B_CMP, :, :], ps[0:B_CMP, 5, 0:B_KV].rearrange("p (g n) -> p g n", g=B_GROUPS)).then_inc(S["b_cmp_ready"], 1)
                values(1, u + 9)
                for n in range(12, 17):
                    split_low(u + n)

                def mask(g, m):
                    dve.wait_ge(S["b_scores"], g * B_PER + (m + 1))
                    dve.memset(b_den[:, m % 2, :], 0.0)
                    for n, (to, add) in enumerate(zip(branches(b_sm[:, m % 2, :]), branches(mask_b[:, :]))):
                        src = (ps[:, 0, 0:P], ps[:, 0, P:2 * P], ps[:, 1:3, 0:P], ps[:, 1:3, P:2 * P],
                               ps[:, 0, 2 * P:272], ps[:, 1, 2 * P:272])[n]
                        ins = dve.tensor_tensor_reduce(to, src, add, 1.0, -3e38, ALU.add, ALU.max, b_mx[:, m % 2, n:n + 1])
                    ins.then_inc(S["b_max"], 1)
                    dve.wait_ge(S["b_max"], g * B_PER + (m + 1))
                    dve.tensor_scalar(b_nm[:, m % 2, :], b_mx[:, m % 2, :], -1.0, None, ALU.mult).then_inc(S["b_neg"], 1)

                def scale(g, m):
                    dve.wait_ge(S["b_exp"], g * B_PER + (m + 1))
                    dve.reciprocal(b_rden[:, m % 2, :], b_den[:, m % 2, :]).then_inc(S["b_rec"], 1)
                    dve.wait_ge(S["b_rec"], g * 2 * B_PER + (2 * m + 1))
                    dve.tensor_tensor(b_fac[:, m % 2, :], b_rden[:, m % 2, :], b_sgate[:, 6 * m:6 * m + 6], ALU.mult).then_inc(S["b_rec"], 1)
                    dve.wait_ge(S["b_rec"], g * 2 * B_PER + (2 * m + 2))
                    for n, at in enumerate(branches(b_sm[:, m % 2, :])):
                        ins = dve.tensor_scalar(at, at, b_fac[:, m % 2, n:n + 1], None, ALU.mult)
                    ins.then_inc(S["b_normed"], 1)

                def turned(g, m):
                    dve.wait_ge(S["b_turned"], g * B_PER + (m + 1))
                    dve.tensor_copy(b_pt[:, m % 2, 512:768], ps[:, 4, 0:256])
                    dve.tensor_copy(b_pt[0:16, m % 2, 768:1024], ps[0:16, 4, 256:512]).then_inc(S["b_pt_dve"], 1)

                def output_low(g, pair):
                    dve.wait_ge(S["b_o_hi"], g * 2 + (pair + 1))
                    at = bass.ds(g * 2 + pair, 1)
                    dve.tensor_tensor(b_o_lo[:, at, :].rearrange("p o t -> p (o t)"), ps[:, 6 + pair, 0:T],
                                      b_o_hi[:, at, :].rearrange("p o t -> p (o t)").bitcast(fp32),
                                      ALU.subtract).then_inc(S["b_o_lo"], 1)

                def group(g, first):
                    dve.wait_ge(S["b_staged"], g * 2 + 1)
                    mask(g, 0)
                    if not first:
                        turned(g - 1, 3)
                    scale(g, 0)
                    mask(g, 1)
                    if not first:
                        output_low(g - 1, 1)
                    turned(g, 0)
                    scale(g, 1)
                    mask(g, 2)
                    turned(g, 1)
                    scale(g, 2)
                    mask(g, 3)
                    turned(g, 2)
                    output_low(g, 0)
                    scale(g, 3)

                group(0, True)
                with dve.Fori(1, B_GROUPS) as g:
                    group(g, False)
                turned(B_GROUPS - 1, 3)
                output_low(B_GROUPS - 1, 1)
                for c in range(1, 3):
                    split_low(u + 16 + c)

            def dilated(st):
                u = st.unit
                dve.wait_ge(masks_ready, 8)

                def mask(i, m):
                    dve.wait_ge(S["c_scores"], i * 4 + (m + 1))
                    dve.memset(c_den[:, m % 2, :], 0.0)
                    for t, (at, to) in enumerate(((0, C_T0), (C_T0, C_SCORES))):
                        src = ps[:, 0, 0:C_T0] if t == 0 else ps[:, 1:3, :].rearrange("p b n -> p (b n)")[:, 0:C_SCORES - C_T0]
                        ins = dve.tensor_tensor_reduce(c_sm[:, m % 2, at:to], src, mask_c[:, at:to], 1.0, -3e38, ALU.add, ALU.max,
                                                       c_mx[:, m % 2, t:t + 1])
                    ins.then_inc(S["c_max"], 1)
                    dve.wait_ge(S["c_max"], i * 4 + (m + 1))
                    dve.tensor_scalar(c_nm[:, m % 2, :], c_mx[:, m % 2, :], -1.0, None, ALU.mult).then_inc(S["c_neg"], 1)

                def scale(i, m):
                    dve.wait_ge(S["c_exp"], i * 4 + (m + 1))
                    dve.reciprocal(c_rden[:, m % 2, :], c_den[:, m % 2, :]).then_inc(S["c_rec"], 1)
                    dve.wait_ge(S["c_rec"], i * 4 + (m + 1))
                    for t, at in enumerate((c_sm[:, m % 2, 0:C_T0], c_sm[:, m % 2, C_T0:C_SCORES])):
                        ins = dve.tensor_scalar(at, at, c_rden[:, m % 2, t:t + 1], None, ALU.mult)
                    ins.then_inc(S["c_normed"], 1)

                def turned(i, m):
                    dve.wait_ge(S["c_turned"], i * 4 + (m + 1))
                    dve.tensor_copy(c_pt[:, m % 2, 512:1024], ps[:, 4, :]).then_inc(S["c_pt_dve"], 1)

                def keys(i, g):
                    dve.wait_ge(unit_used, i * 9 + (u + 3 * g + 2))
                    dve.tensor_copy(c_k[:, g, :, :], ps[:, 1, :].rearrange("p (n t) -> p n t", n=2)).then_inc(S["c_k_ready"], 1)

                def output_low(i, pair):
                    dve.wait_ge(S["c_o_hi"], i * 2 + (pair + 1))
                    at = bass.ds(i * 2 + pair, 1)
                    dve.tensor_tensor(c_o_lo[:, at, :].rearrange("p o t -> p (o t)"), ps[:, 6 + pair, 0:T],
                                      c_o_hi[:, at, :].rearrange("p o t -> p (o t)").bitcast(fp32),
                                      ALU.subtract).then_inc(S["c_o_lo"], 1)

                def quad(i, first):
                    split_low(u + 2, i * 9)
                    if not first:
                        turned(i - 1, 3)
                    split_low(u + 3, i * 9)
                    keys(i, 0)
                    split_low(u + 4, i * 9)
                    if not first:
                        output_low(i - 1, 1)
                    split_low(u + 5, i * 9)
                    split_low(u + 6, i * 9)
                    keys(i, 1)
                    split_low(u + 7, i * 9)
                    split_low(u + 8, i * 9)
                    split_low(u + 9, i * 9)
                    keys(i, 2)
                    mask(i, 0)
                    scale(i, 0)
                    split_low(u + 10, i * 9)
                    for m in range(3):
                        mask(i, m + 1)
                        turned(i, m)
                        if m == 2:
                            output_low(i, 0)
                        scale(i, m + 1)

                quad(0, True)
                with dve.Fori(1, C_QUADS) as i:
                    quad(i, False)
                split_low(u + 9 * C_QUADS + 2)
                turned(C_QUADS - 1, 3)
                output_low(C_QUADS - 1, 1)
                for c in range(1, 3):
                    split_low(u + 9 * C_QUADS + 2 + c)

            scale_rows(STAGES[0])
            dve.wait_ge(gains_turned, 1)
            dve.tensor_copy(cols[:, 0:P], ps[:, 7, 2 * P:3 * P]).then_inc(gains_ready, 1)
            split_low(0)
            if STAGES[1].kind in ("a", "b"):
                gates_low(STAGES[1])
            for b in range(3):
                dve.wait_ge(rows_turned, b + 1)
                dve.tensor_copy(cols[:, b * 512 + (P if b == 0 else 0):(b + 1) * 512], ps[:, 4 + b, P if b == 0 else 0:]).then_inc(cols_ready, 1)

            dve.wait_ge(residues_turned, 1)
            dve.wait_ge(masks_zeroed, 1)
            for n in range(2):
                dve.tensor_scalar(mask_c[:, (n + 1) * P:(n + 2) * P], ps[:, 7, n * P:(n + 1) * P], -1.0, -NEG, ALU.add, ALU.mult)
                for half_at in range(2):
                    at = C_T0 + (n + 1) * T + half_at * P
                    ins = dve.tensor_scalar(mask_c[:, at:at + P], ps[:, 7, n * P:(n + 1) * P], -1.0, -NEG, ALU.add, ALU.mult)
                ins.then_inc(masks_filled, 1)

            norm(STAGES[0])
            for st in STAGES[1:]:
                if st.kind == "norm":
                    norm(st)
                if st.kind == "b":
                    nsa(st)
                if st.kind == "c":
                    dilated(st)
                if st.kind == "a":
                    mlstm(st)
                if st.kind == "ffn":
                    ffn(st)
                if st.kind == "last":
                    last(st)

        @block.tensor
        def _(pe):
            pe.wait_ge(ident_ready, 2)

            def products(pairs, dst, start, stop):
                for n, (stationary, moving) in enumerate(pairs):
                    ins = pe.matmul(dst, stationary, moving, start=start and n == 0, stop=stop and n == len(pairs) - 1,
                                    skip_group_check=True)
                return ins

            def up(k, bank, x_hi=hn_hi, x_lo=hn_lo, first=None):
                wh = w_hi[k][:, :].rearrange("p (t n) -> p t n", t=KT)
                wl = w_lo[k][:, :].rearrange("p (t n) -> p t n", t=KT)
                for n in range(2):
                    at = slice(n * P, (n + 1) * P)
                    for kt in range(KT):
                        if first is not None and n == 0:
                            pe.wait_ge(S["hn_lo_ready"], first["hn_lo_ready"] - KT + kt + 1)
                        ins = products([(wh[:, kt, at], x_hi[:, kt, :]), (wh[:, kt, at], x_lo[:, kt, :]),
                                        (wl[:, kt, at], x_hi[:, kt, :])],
                                       ps[:, bank, n * T:(n + 1) * T], kt == 0, kt == KT - 1)
                return ins

            def by_token(k, bank):
                wh = w_hi[k][:, :].rearrange("p (t n) -> p t n", t=KT)
                wl = w_lo[k][:, :].rearrange("p (t n) -> p t n", t=KT)
                for t in range(TT):
                    tok = slice(t * P, (t + 1) * P)
                    for kt in range(KT):
                        ins = products([(hn_hi[:, kt, tok], wh[:, kt, :]), (hn_hi[:, kt, tok], wl[:, kt, :]),
                                        (hn_lo[:, kt, tok], wh[:, kt, :])], ps[:, bank, t * 256:(t + 1) * 256], kt == 0, kt == KT - 1)
                return ins

            def clear_y():
                for b in range(4):
                    pe.matmul(ps[:, b, :], zero_r[:, 0:P], zero_r[:, :], start=True, stop=False, skip_group_check=True)

            def down(k, x_hi, x_lo, stop):
                wh = w_hi[k][:, :].rearrange("p (c n) -> p c n", c=2)
                wl = w_lo[k][:, :].rearrange("p (c n) -> p c n", c=2)
                for t in range(TT):
                    for b in range(2):
                        for c in range(2):
                            tok, at = slice(t * P, (t + 1) * P), slice(b * 512, (b + 1) * 512)
                            ins = products([(x_hi[:, c, tok], wh[:, c, at]), (x_hi[:, c, tok], wl[:, c, at]),
                                            (x_lo[:, c, tok], wh[:, c, at])],
                                           ps[:, 2 * t + b, :], False, stop and c == 1)
                        if stop and 2 * t + b < 3:
                            ins.then_inc(S["y_banks"], 1)
                return ins

            def norm(st):
                if not st.first:
                    pe.wait_ge(S["h_added"], st["h_added"] + 2 * TT)
                for t in range(TT):
                    pe.wait_ge(S["hs_ready"], st["hs_ready"] + t + 1)
                    pe.wait_ge(S["hs_act_ready"], st["hs_act_ready"] + t + 1)
                    for b in range(4):
                        for kt in (b, b + 4):
                            ins = pe.transpose(ps[:, b, (kt // 4) * T + t * P:(kt // 4) * T + (t + 1) * P],
                                               hs[:, t, kt * P:(kt + 1) * P], ident[:, :])
                        if t == TT - 1:
                            ins.then_inc(S["turned"], 1)

            def ffn(st):
                L, u = st.layer, st.unit

                def gate_up(i, u, passed):
                    pe.wait_ge(lo_ready, passed + (u + 1))
                    pe.wait_ge(S["gate_taps"], i * 4 + st["gate_taps"])
                    up(slot(u), GATE).then_inc(unit_used, 1)

                def val_up(i, u, passed):
                    pe.wait_ge(lo_ready, passed + (u + 1))
                    pe.wait_ge(S["val_taps"], i * 4 + st["val_taps"])
                    up(slot(u), VAL).then_inc(unit_used, 1)

                def project(i, u, passed, high, low, stop):
                    pe.wait_ge(lo_ready, passed + (u + 1))
                    pe.wait_ge(S["g_lo_ready"], i + (st["g_lo_ready"] + 1))
                    down(slot(u), high, low, stop).then_inc(unit_used, 1)

                pe.wait_ge(lo_ready, u + 1)
                up(slot(u), GATE, first=st).then_inc(unit_used, 1)
                pe.wait_ge(lo_ready, u + 2)
                up(slot(u + 1), VAL).then_inc(unit_used, 1)
                clear_y()
                with pe.Fori(0, FC - 1) as i:
                    gate_up(i + 1, u + 2, i * 3)
                    val_up(i + 1, u + 3, i * 3)
                    project(i, u + 4, i * 3, g_hi, g_lo, False)
                project(FC - 1, u + 3 * FC - 1, 0, hn_hi, hn_lo, True)

            def mlstm(st):
                u = st.unit
                if st["h_added"]:
                    pe.wait_ge(S["h_added"], st["h_added"])
                pe.wait_ge(S["gates_split"], st["gates_split"] + 2)
                for kt in range(KT):
                    pe.wait_ge(S["hn_lo_ready"], st["hn_lo_ready"] - KT + kt + 1)
                    ins = products([(gate_hi[:, kt, :], hn_hi[:, kt, :]), (gate_hi[:, kt, :], hn_lo[:, kt, :]),
                                    (gate_lo[:, kt, :], hn_hi[:, kt, :])], ps[:, 6, 0:T], kt == 0, kt == KT - 1)
                ins.then_inc(S["gates_made"], 1)

                def x_m(b, passed, bank):
                    pe.wait_ge(lo_ready, passed + (b + 1))
                    up(slot(b), bank).then_inc(unit_used, 1)

                def head_up(k, bank, x_hi, x_lo):
                    wh = w_hi[k][:, :].rearrange("p (t n) -> p t n", t=A_HT)
                    wl = w_lo[k][:, :].rearrange("p (t n) -> p t n", t=A_HT)
                    for n in range(A_HT):
                        at = slice(n * P, (n + 1) * P)
                        for kt in range(A_HT):
                            ins = products([(wh[:, kt, at], x_hi[:, kt, :]), (wh[:, kt, at], x_lo[:, kt, :]),
                                            (wl[:, kt, at], x_hi[:, kt, :])],
                                           ps[:, bank + n // 2, (n % 2) * T:(n % 2 + 1) * T], kt == 0, kt == A_HT - 1)
                    return ins

                def head(h, b, passed, more):
                    pe.wait_ge(lo_ready, passed + (b + 1))
                    pe.wait_ge(S["xm_lo_ready"], h * 2 + (st["xm_lo_ready"] + 2))
                    pe.wait_ge(S["xm_taps"], h * 12 + (st["xm_taps"] + 12))
                    wh = w_hi[slot(b)][:, :].rearrange("p (t n) -> p t n", t=A_HT)
                    wl = w_lo[slot(b)][:, :].rearrange("p (t n) -> p t n", t=A_HT)
                    for t in range(TT):
                        tok = slice(t * P, (t + 1) * P)
                        for kt in range(A_HT):
                            ins = products([(xm_hi[:, kt, tok], wh[:, kt, :]), (xm_hi[:, kt, tok], wl[:, kt, :]),
                                            (xm_lo[:, kt, tok], wh[:, kt, :])], ps[:, 4 + t, :], kt == 0, kt == A_HT - 1)
                    ins.then_inc(unit_used, 1)
                    pe.wait_ge(lo_ready, passed + (b + 2))
                    pe.wait_ge(S["xc_lo_ready"], h * 2 + (st["xc_lo_ready"] + 2))
                    head_up(slot(b + 1), 6, xc_hi, xc_lo).then_inc(unit_used, 1)
                    pe.wait_ge(lo_ready, passed + (b + 3))
                    pe.wait_ge(S["v_ready"], h + (st["v_ready"] + 1))
                    head_up(slot(b + 2), 4, xc_hi, xc_lo).then_inc(unit_used, 1)
                    pe.wait_ge(S["q_ready"], h + (st["q_ready"] + 1))
                    for t in range(TT):
                        for e in range(A_HT):
                            if t == 0 and e % 2 == 0:
                                pe.wait_ge(S["k_ready"], h * 2 + (st["k_ready"] + e // 2 + 1))
                            ins = pe.matmul(ps[:, 6, t * T + t * P:(t + 1) * T], k_t[:, e, t * P:(t + 1) * P],
                                            q_t[:, e, t * P:T], start=(e == 0), stop=(e == A_HT - 1))
                    ins.then_inc(S["scores_made"], 1)
                    pe.wait_ge(lo_ready, passed + (b + 4))
                    up(slot(b + 3), 5).then_inc(unit_used, 1)
                    if more:
                        pe.wait_ge(lo_ready, passed + (b + 5))
                        up(slot(b + 4), 4).then_inc(unit_used, 1)
                    pe.wait_ge(S["weights_ready"], h + (st["weights_ready"] + 1))
                    pe.wait_ge(S["o_ready"], h * 2 + (st["o_ready"] + 1))
                    for t in range(TT):
                        for s in range(t + 1):
                            pe.matmul(ps[:, 6 + t, :], weights[:, s, t * P:(t + 1) * P], v_s[:, s, :],
                                      start=(s == 0), stop=(s == t))
                    for t in range(TT):
                        for s in range(t + 1):
                            ins = pe.matmul(ps[:, 5, t:t + 1], weights[:, s, t * P:(t + 1) * P], ones[:, 0:1],
                                            start=(s == 0), stop=(s == t))
                    ins.then_inc(S["num_made"], 1)
                    if more:
                        pe.wait_ge(S["o_ready"], h * 2 + (st["o_ready"] + 2))
                        x_m(b + 5, passed, 4)
                    else:
                        pe.wait_ge(lo_ready, b + 5)
                        up(slot(b + 4), 4).then_inc(unit_used, 1)
                    pe.wait_ge(S["head_normed"], h + (st["head_normed"] + 1))
                    for e in range(A_HT):
                        for t in range(TT):
                            ins = pe.transpose(ps[:, 6 + e // 2, (e % 2) * T + t * P:(e % 2) * T + (t + 1) * P],
                                               head_n[:, t, e * P:(e + 1) * P], ident[:, :])
                    ins.then_inc(S["head_turned"], 1)
                    if more:
                        x_m(b + 6, passed, 5)
                        b += 2
                    for c in range(2):
                        pe.wait_ge(S["y_lo_ready"], h * 2 + (st["y_lo_ready"] + c + 1))
                        pe.wait_ge(lo_ready, passed + (b + 6 + c))
                        down(slot(b + 5 + c), y_hi[:, 2 * c:2 * c + 2, :], y_lo[:, 2 * c:2 * c + 2, :],
                             not more and c == 1).then_inc(unit_used, 1)

                x_m(u, 0, 4)
                x_m(u + 1, 0, 5)
                pe.wait_ge(S["gate_rows"], st["gate_rows"] + 9)
                for t in range(TT):
                    pe.transpose(ps[:, 0, 4 * t:4 * t + 4], source[:, t * P:(t + 1) * P], ident[0:A_HEADS, 0:A_HEADS])
                    pe.transpose(ps[:, 0, 8 + 4 * t:12 + 4 * t], stab[:, t * P:(t + 1) * P], ident[0:A_HEADS, 0:A_HEADS])
                for n in range(A_HEADS):
                    ins = pe.matmul(ps[:, 6 + n // 2, (n % 2) * T:(n % 2 + 1) * T],
                                    ident[0:A_HEADS, n:n + 1].to_broadcast([A_HEADS, P]), top[:, :], start=True, stop=True)
                ins.then_inc(S["gates_spread"], 1)
                pe.wait_ge(S["gate_cols"], st["gate_cols"] + 3)
                clear_y()
                with pe.Fori(0, A_HEADS - 1) as h:
                    head(h, u + 2, h * 9, True)
                head(A_HEADS - 1, u + 2 + 9 * (A_HEADS - 1), 0, False)

            def output_projection(u, o_hi, o_lo, done):
                clear_y()
                for c in range(4):
                    pe.wait_ge(done, 2 * c + 2)
                    pe.wait_ge(lo_ready, u + c + 1)
                    down(slot(u + c), o_hi[:, 2 * c:2 * c + 2, :], o_lo[:, 2 * c:2 * c + 2, :], c == 3).then_inc(unit_used, 1)

            def nsa(st):
                u = st.unit
                if st["h_added"]:
                    pe.wait_ge(S["h_added"], st["h_added"])
                pe.wait_ge(S["b_gates_split"], 2)
                for kt in range(KT):
                    pe.wait_ge(S["hn_lo_ready"], st["hn_lo_ready"] - KT + kt + 1)
                    ins = products([(b_gate_hi[:, kt, :], hn_hi[:, kt, :]), (b_gate_hi[:, kt, :], hn_lo[:, kt, :]),
                                    (b_gate_lo[:, kt, :], hn_hi[:, kt, :])], ps[0:3 * B_HEADS, 7, 0:T], kt == 0, kt == KT - 1)
                ins.then_inc(S["b_gates_made"], 1)

                def ready(n):
                    pe.wait_ge(lo_ready, u + n + 1)

                NB = B_GROUPS * B_CMP

                def phi(n, which, half_at):
                    ready(n)
                    wh = w_hi[slot(u + n)][:, :].rearrange("p (t n) -> p t n", t=KT)
                    wl = w_lo[slot(u + n)][:, :].rearrange("p (t n) -> p t n", t=KT)
                    for kt in range(KT):
                        m = KT * half_at + kt
                        fh, fl = flat_hi[which][:, m * NB:(m + 1) * NB], flat_lo[which][:, m * NB:(m + 1) * NB]
                        ins = products([(fh, wh[:, kt, :]), (fh, wl[:, kt, :]), (fl, wh[:, kt, :])],
                                       ps[0:NB, 4 - 4 * which, 0:T], m == 0, m == 2 * KT - 1)
                    ins.then_inc(unit_used, 1)

                def turn_hidden(which):
                    pe.wait_ge(S["b_pre_ready"], which + 1)
                    for c in range(2):
                        ins = pe.transpose(ps[:, 5 - 4 * which, c * P:c * P + NB], b_pre[:, which, c * P:(c + 1) * P], ident[0:NB, 0:NB])
                    ins.then_inc(S["b_pre_turned"], 1)

                ready(0)
                up(slot(u), 0).then_inc(unit_used, 1)
                pe.wait_ge(S["b_gates_copied"], 1)
                for t in range(TT):
                    ins = pe.transpose(ps[:, 7, T + 64 * t:T + 64 * t + 48], b_gate_t[:, t * P:(t + 1) * P], ident[0:48, 0:48])
                ins.then_inc(S["b_gates_turned"], 1)
                ready(1)
                up(slot(u + 1), 1).then_inc(unit_used, 1)
                ready(2)
                up(slot(u + 2), 2).then_inc(unit_used, 1)
                pe.wait_ge(S["b_flat_lo"], 1)
                phi(3, 0, 0)
                phi(4, 0, 1)
                ready(5)
                by_token(slot(u + 5), 6).then_inc(unit_used, 1)
                turn_hidden(0)
                pe.wait_ge(S["b_flat_lo"], 2)
                phi(6, 1, 0)
                pe.wait_ge(b_params_loaded, 64)
                pe.wait_ge(S["b_hidden_ready"], 1)
                for d in range(2):
                    for c in range(2):
                        ins = pe.matmul(ps[DH * d:DH * (d + 1), 4, 0:NB], b_w2[:, 0, c, :], b_hidden[:, 0, c, :],
                                        start=(c == 0), stop=(c == 1))
                ins.then_inc(S["b_cmp_made"], 1)
                phi(7, 1, 1)
                pe.wait_ge(S["b_keys_ready"], 1)
                ready(8)
                up(slot(u + 8), 2).then_inc(unit_used, 1)
                turn_hidden(1)
                pe.wait_ge(S["b_values_ready"], 1)
                ready(9)
                by_token(slot(u + 9), 6).then_inc(unit_used, 1)
                pe.wait_ge(S["b_hidden_ready"], 2)
                for g in range(B_GROUPS):
                    for c in range(2):
                        ins = pe.matmul(ps[0:B_CMP, 5, g * DH:(g + 1) * DH], b_hidden[:, 1, c, g * B_CMP:(g + 1) * B_CMP],
                                        b_w2[:, 1, c, :], start=(c == 0), stop=(c == 1))
                ins.then_inc(S["b_cmp_made"], 1)
                for g in range(B_GROUPS):
                    if g < 2:
                        pe.wait_ge(S["b_cmp_ready"], g + 1)
                    ready(10 + g)
                    up(slot(u + 10 + g), (4, 5, 0, 1)[g]).then_inc(unit_used, 1)
                pe.wait_ge(S["b_q_ready"], B_GROUPS)
                pe.wait_ge(S["b_keys_ready"], 2)
                pe.wait_ge(S["b_values_ready"], 2)
                pe.wait_ge(b_pad_ready, 1)

                def scores(g, m):
                    if m or not isinstance(g, int):
                        pe.wait_ge(S["b_max"], g * B_PER + m)
                    at = slice(DH * (m % 2), DH * (m % 2) + DH)
                    q = b_sq[at, m // 2, :]
                    pe.matmul(ps[:, 0, 0:272], q[:, 0:P], b_sk[at, 0:272], start=True, stop=True)
                    pe.matmul(ps[:, 1, 0:272], q[:, P:T], b_sk[at, 0:272], start=True, stop=True)
                    pe.matmul(ps[:, 2, 0:T], q[:, P:T], b_sk[at, 272:528], start=True, stop=True).then_inc(S["b_scores"], 1)

                def turn(g, m):
                    pe.wait_ge(S["b_normed"], g * B_PER + (m + 1))
                    if m or not isinstance(g, int):
                        pe.wait_ge(S["b_pt_act"], g * B_PER + m)
                        pe.wait_ge(S["b_pt_dve"], g * B_PER + m)
                    sm = b_sm[:, m % 2, :]
                    for n, at in enumerate((0, 272, P, 272 + P)):
                        pe.transpose(ps[:, 3, n * P:(n + 1) * P], sm[:, at:at + P], ident[:, :])
                    for n in range(2):
                        pe.transpose(ps[:, 4, n * P:(n + 1) * P], sm[:, 544 + n * P:544 + (n + 1) * P], ident[:, :])
                    for t in range(TT):
                        ins = pe.transpose(ps[0:16, 4, (2 + t) * P:(3 + t) * P], sm[:, 256 + 272 * t:272 + 272 * t], ident[:, :])
                    ins.then_inc(S["b_turned"], 1)

                def mix(g, m):
                    pe.wait_ge(S["b_pt_act"], g * B_PER + (m + 1))
                    pe.wait_ge(S["b_pt_dve"], g * B_PER + (m + 1))
                    if m == 0:
                        pe.wait_ge(S["b_staged"], g * 2 + 2)
                        if not isinstance(g, int):
                            pe.wait_ge(S["b_o_lo"], g * 2 - 1)
                    half_at = slice(DH * (m % 2), DH * (m % 2) + DH)
                    dst = ps[half_at, 6 + m // 2, :]
                    pt = b_pt[:, m % 2, :]
                    for s in range(2):
                        pe.matmul(dst[:, 0:T], b_sv[:, 0, s * DH:(s + 1) * DH], pt[:, s * T:(s + 1) * T], start=(s == 0), stop=False)
                        pe.matmul(dst[:, P:T], b_sv[:, 1, s * DH:(s + 1) * DH], pt[:, 512 + s * P:512 + (s + 1) * P], start=False, stop=False)
                    pe.matmul(dst[:, 0:T], b_svc[0:B_CMP, :], pt[0:B_CMP, 768:1024], start=False, stop=True).then_inc(S["b_out"], 1)

                def group(g, first):
                    if not first:
                        mix(g - 1, 2)
                    pe.wait_ge(S["b_staged"], g * 2 + 1)
                    scores(g, 0)
                    if not first:
                        turn(g - 1, 3)
                    scores(g, 1)
                    if not first:
                        mix(g - 1, 3)
                    turn(g, 0)
                    scores(g, 2)
                    mix(g, 0)
                    turn(g, 1)
                    scores(g, 3)
                    mix(g, 1)
                    turn(g, 2)

                group(0, True)
                with pe.Fori(1, B_GROUPS) as g:
                    group(g, False)
                mix(B_GROUPS - 1, 2)
                turn(B_GROUPS - 1, 3)
                mix(B_GROUPS - 1, 3)
                output_projection(u + 14, b_o_hi, b_o_lo, S["b_o_lo"])

            def dilated(st):
                u = st.unit
                pe.wait_ge(S["hn_lo_ready"], st["hn_lo_ready"])

                def scores(i, m):
                    if m:
                        pe.wait_ge(S["c_max"], i * 4 + m)
                    at = slice(DH * (m % 2), DH * (m % 2) + DH)
                    for g in range(C_GROUPS):
                        q, k = c_q[at, g, m // 2, :], c_k[at, g, m // 2, :]
                        pe.matmul(ps[:, 0, g * P:(g + 1) * P], q[:, 0:P], k[:, 0:P], start=True, stop=True)
                        ins = pe.matmul(ps[:, 1 + g // 2, (g % 2) * T:(g % 2 + 1) * T], q[:, P:T], k, start=True, stop=True)
                    ins.then_inc(S["c_scores"], 1)

                def turn(i, m):
                    pe.wait_ge(S["c_normed"], i * 4 + (m + 1))
                    if m == 0:
                        pe.wait_ge(S["c_v_ready"], i * 3 + 3)
                    blocks = [x for g in range(C_GROUPS) for x in (g * P, C_T0 + g * T)] + [C_T0 + g * T + P for g in range(C_GROUPS)]
                    for n, at in enumerate(blocks):
                        ins = pe.transpose(ps[:, 3 + n // 4, (n % 4) * P:(n % 4 + 1) * P], c_sm[:, m % 2, at:at + P], ident[:, :])
                    ins.then_inc(S["c_turned"], 1)

                def mix(i, m):
                    pe.wait_ge(S["c_pt_act"], i * 4 + (m + 1))
                    pe.wait_ge(S["c_pt_dve"], i * 4 + (m + 1))
                    if m == 0 and not isinstance(i, int):
                        pe.wait_ge(S["c_o_lo"], i * 2 - 1)
                    dst = ps[DH * (m % 2):DH * (m % 2) + DH, 6 + m // 2, :]
                    pt = c_pt[:, m % 2, :]
                    for g in range(C_GROUPS):
                        pe.matmul(dst[:, 0:T], c_v[:, g, 0, m * DH:(m + 1) * DH], pt[:, g * T:(g + 1) * T], start=(g == 0), stop=False)
                        ins = pe.matmul(dst[:, P:T], c_v[:, g, 1, m * DH:(m + 1) * DH], pt[:, (6 + g) * P:(7 + g) * P],
                                        start=False, stop=(g == C_GROUPS - 1))
                    ins.then_inc(S["c_out"], 1)

                def unit(i, x):
                    g, part = x // 3, x % 3
                    k = slot(u + x)
                    pe.wait_ge(lo_ready, i * 9 + (u + x + 1))
                    if g:
                        pe.wait_ge(S[("c_q_ready", "c_k_ready", "c_v_ready")[part]], i * 3 + g)
                    (by_token(k, 3) if part == 2 else up(k, part)).then_inc(unit_used, 1)

                def quad(i, first):
                    if not first:
                        pe.wait_ge(S["c_max"], i * 4)
                    unit(i, 0)
                    if not first:
                        mix(i - 1, 2)
                        turn(i - 1, 3)
                    unit(i, 1)
                    if not first:
                        mix(i - 1, 3)
                    for x in range(2, 8):
                        unit(i, x)
                    pe.wait_ge(S["c_q_ready"], i * 3 + 3)
                    pe.wait_ge(S["c_k_ready"], i * 3 + 3)
                    scores(i, 0)
                    unit(i, 8)
                    for m in range(3):
                        scores(i, m + 1)
                        if m:
                            mix(i, m - 1)
                        turn(i, m)

                quad(0, True)
                with pe.Fori(1, C_QUADS) as i:
                    quad(i, False)
                mix(C_QUADS - 1, 2)
                turn(C_QUADS - 1, 3)
                mix(C_QUADS - 1, 3)
                output_projection(u + 9 * C_QUADS, c_o_hi, c_o_lo, S["c_o_lo"])

            pe.wait_ge(gains_loaded, 16 * 2)
            pe.transpose(ps[:, 7, 2 * P:3 * P], rows[:, 0, :], ident[:, :]).then_inc(gains_turned, 1)
            norm(STAGES[0])
            pe.wait_ge(rows_loaded, 16 * len(ROW_LOADS[2:]))
            for g in range(1, N_GROUPS):
                ins = pe.transpose(ps[:, 4 + g // 4, (g % 4) * P:(g % 4 + 1) * P], rows[:, g, :], ident[:, :])
                if g % 4 == 3:
                    ins.then_inc(rows_turned, 1)
            pe.wait_ge(residues_ready, 2)
            pe.wait_ge(gains_ready, 1)
            pe.matmul(ps[:, 7, 0:P], residue4[:, :], residue4[:, :], start=True, stop=True)
            pe.matmul(ps[:, 7, P:2 * P], residue16[:, :], residue16[:, :], start=True, stop=True).then_inc(residues_turned, 1)
            pe.wait_ge(zeros_ready, 2)

            pe.wait_ge(cols_ready, 3)
            pe.wait_ge(masks_filled, 2)

            for st in STAGES[1:]:
                if st.kind == "norm":
                    norm(st)
                if st.kind == "a":
                    mlstm(st)
                if st.kind == "b":
                    nsa(st)
                if st.kind == "c":
                    dilated(st)
                if st.kind == "ffn":
                    ffn(st)


_OUTS = [((1, T, D), "float32")]
PLAN = [("norm", 0), ("a", 0), ("norm", 4), ("ffn", 0), ("norm", 1), ("b", 1), ("norm", 5), ("ffn", 1),
        ("norm", 2), ("c", 2), ("norm", 6), ("ffn", 2), ("norm", 3), ("a", 3), ("norm", 7), ("ffn", 3), ("last", 0)]


def kernel(**inputs):
    import numpy as _np
    import concourse.bacc as _bacc
    from concourse import mybir as _mybir
    from concourse.bass_utils import run_bass_kernel_spmd as _run

    nc = _bacc.Bacc("TRN2", target_bir_lowering=False, num_devices=1)
    arrays, a = {}, {}
    for name in inputs:
        x = _np.ascontiguousarray(inputs[name])
        arrays[f"in_{name}_dram"] = x
        a[name] = nc.dram_tensor(f"in_{name}_dram", x.shape, _mybir.dt.from_np(x.dtype), kind="ExternalInput").ap()
    shape, dtype = _OUTS[0]
    out = nc.dram_tensor("out_0_dram", shape, _mybir.dt.from_np(_np.dtype(dtype)), kind="ExternalOutput").ap()
    build(nc, a, out, PLAN)
    r = _run(nc, [arrays], core_ids=[0])
    return r.results[0]["out_0_dram"]
```
